# Optimizing a Trainium2 kernel written in Bass

```python
import math
import jax, jax.numpy as jnp
from jax import lax
import numpy as np

D_MODEL = 1024
BATCH = 1
SEQ = 1024
DEPTH = 2
DEC_BATCH = 8
DEC_SEQ = 4
PAST_LEN = 2048
PAGE_SIZE = 128

MIX_WIDTH = D_MODEL
MEM_HEADS = 4
MEM_HEAD_DIM = 64
MEM_WIDTH = MEM_HEADS * MEM_HEAD_DIM
TOK_WIDTH = MIX_WIDTH - MEM_WIDTH
N_MEM = 256
HG_HEAD_DIM = 128
HG_HEADS = TOK_WIDTH // HG_HEAD_DIM
HG_CHUNK = 64
HG_IN = 4 * TOK_WIDTH + MEM_WIDTH
LB_MAX = 0.999
SW_HEAD_DIM = 64
SW_Q_HEADS = TOK_WIDTH // SW_HEAD_DIM
SW_KV_HEADS = 4
SW_GROUP = SW_Q_HEADS // SW_KV_HEADS
WINDOW = 128
SW_IN = (SW_Q_HEADS + 2 * SW_KV_HEADS) * SW_HEAD_DIM + MEM_WIDTH
D_FF = -(-8 * D_MODEL // (3 * 256)) * 256
N_HGRN = (DEPTH + 1) // 2
N_SWA = DEPTH // 2
EPS = 1e-6
NEG = -1e30

kernel_name = 'hgrn2_swa_sink_memory_hybrid_step'

F32 = jnp.float32

def rmsnorm(x, g):
    xf = x.astype(F32)
    y = xf * lax.rsqrt(jnp.mean(xf * xf, axis=-1, keepdims=True) + EPS) * g.astype(F32)
    return y.astype(x.dtype)

def head_rms(x, g):
    xf = x.astype(F32)
    return xf * lax.rsqrt(jnp.mean(xf * xf, axis=-1, keepdims=True) + EPS) * g.astype(F32)

def _chunk_len(L):
    return L if L <= HG_CHUNK else math.gcd(L, HG_CHUNK)

def hgrn_recurrence(q, k, v, logf, s0):
    b_, L, H, DK = q.shape
    DV = v.shape[-1]
    C = _chunk_len(L)
    n = L // C

    def to_chunks(t):
        return t.reshape(b_, n, C, H, t.shape[-1]).transpose(1, 0, 3, 2, 4)

    causal = jnp.tril(jnp.ones((C, C), bool))[:, :, None]

    def step(s, inp):
        qc, kc, vc, gc = inp
        cum = jnp.cumsum(gc, axis=2)
        diff = cum[:, :, :, None, :] - cum[:, :, None, :, :]
        decay = jnp.exp(jnp.where(causal, diff, NEG))
        att = jnp.einsum('bhtc,bhsc,bhtsc->bhts', qc, kc, decay)
        o = (jnp.einsum('bhts,bhsv->bhtv', att, vc)
             + jnp.einsum('bhtc,bhcv->bhtv', qc * jnp.exp(cum), s))
        last = cum[:, :, -1:, :]
        s_new = (jnp.exp(last[:, :, 0, :, None]) * s
                 + jnp.einsum('bhsc,bhsv->bhcv', kc * jnp.exp(last - cum), vc))
        return s_new, o

    s_fin, o = lax.scan(step, s0, (to_chunks(q), to_chunks(k), to_chunks(v), to_chunks(logf)))
    o = o.transpose(1, 0, 3, 2, 4).reshape(b_, L, H, DV)
    return o, s_fin

def hgrn_branch(p, lb, g_norm, s0):
    q, fz, i_in, g = jnp.split(p, 4, axis=-1)
    B, L, _ = q.shape
    shp = (B, L, HG_HEADS, HG_HEAD_DIM)
    qf = (jax.nn.silu(q.astype(F32)) * HG_HEAD_DIM ** -0.5).reshape(shp)
    z = fz.astype(F32)
    f = lb + (1.0 - lb) * jax.nn.sigmoid(z)
    logf = jnp.log(f).reshape(shp)
    kf = ((1.0 - lb) * jax.nn.sigmoid(-z)).reshape(shp)
    vf = i_in.astype(F32).reshape(shp)
    o, s = hgrn_recurrence(qf, kf, vf, logf, s0.astype(F32))
    o = head_rms(o, jnp.ones((HG_HEAD_DIM,), F32)).reshape(B, L, TOK_WIDTH)
    o = o * g_norm.astype(F32) * jax.nn.silu(g.astype(F32))
    return o, s

def sink_softmax(s, sinks):
    sk = sinks.astype(F32).reshape(SW_KV_HEADS, SW_GROUP, 1, 1)
    m = jnp.maximum(jnp.max(s, axis=-1, keepdims=True), sk)
    p = jnp.exp(s - m)
    return p / (jnp.sum(p, axis=-1, keepdims=True) + jnp.exp(sk - m))

def swa_prompt(q, k, v, sinks):
    B, L = q.shape[:2]
    n = L // WINDOW
    qb = q.reshape(B, n, WINDOW, SW_KV_HEADS, SW_GROUP, SW_HEAD_DIM)
    kb = k.reshape(B, n, WINDOW, SW_KV_HEADS, SW_HEAD_DIM)
    vb = v.reshape(B, n, WINDOW, SW_KV_HEADS, SW_HEAD_DIM)

    def with_prev(t):
        prev = jnp.pad(t[:, :-1], ((0, 0), (1, 0), (0, 0), (0, 0), (0, 0)))
        return jnp.concatenate([prev, t], axis=2)

    kk, vv = with_prev(kb), with_prev(vb)
    s = jnp.einsum('bnqkgd,bnskd->bnkgqs', qb, kk) * SW_HEAD_DIM ** -0.5
    qi = jnp.arange(WINDOW)[:, None]
    r = jnp.arange(2 * WINDOW)[None, :]
    band = (r > qi) & (r <= qi + WINDOW)
    has_prev = (jnp.arange(n)[:, None, None] > 0) | (r >= WINDOW)[None]
    mask = (band[None] & has_prev)[None, :, None, None]
    p = sink_softmax(jnp.where(mask, s, NEG), sinks)
    o = jnp.einsum('bnkgqs,bnskd->bnqkgd', p, vv)
    return o.reshape(B, L, SW_Q_HEADS * SW_HEAD_DIM)

def swa_sample(q, k, v, buf_k, buf_v, sinks):
    B, L = q.shape[:2]
    kk = jnp.concatenate([buf_k.astype(F32), k], axis=1)
    vv = jnp.concatenate([buf_v.astype(F32), v], axis=1)
    qg = q.reshape(B, L, SW_KV_HEADS, SW_GROUP, SW_HEAD_DIM)
    s = jnp.einsum('bqkgd,bskd->bkgqs', qg, kk) * SW_HEAD_DIM ** -0.5
    j = jnp.arange(L)[:, None]
    r = jnp.arange(WINDOW + L)[None, :]
    mask = (r > j) & (r <= j + WINDOW)
    p = sink_softmax(jnp.where(mask, s, NEG), sinks)
    o = jnp.einsum('bkgqs,bskd->bqkgd', p, vv).reshape(B, L, SW_Q_HEADS * SW_HEAD_DIM)
    return o, kk[:, -WINDOW:], vv[:, -WINDOW:]

def mem_kv(mem, norm_g, w_kv, k_norm):
    B = mem.shape[0]
    kv = rmsnorm(mem, norm_g) @ w_kv
    k, v = jnp.split(kv, 2, axis=-1)
    k = head_rms(k.reshape(B, N_MEM, MEM_HEADS, MEM_HEAD_DIM), k_norm)
    v = v.reshape(B, N_MEM, MEM_HEADS, MEM_HEAD_DIM).astype(F32)
    return k, v

def mem_attend(cq, mk, mv, q_norm):
    B, L, _ = cq.shape
    q = head_rms(cq.reshape(B, L, MEM_HEADS, MEM_HEAD_DIM), q_norm)
    s = jnp.einsum('blhd,bmhd->bhlm', q, mk.astype(F32)) * MEM_HEAD_DIM ** -0.5
    p = jax.nn.softmax(s, axis=-1)
    return jnp.einsum('bhlm,bmhd->blhd', p, mv.astype(F32)).reshape(B, L, MEM_WIDTH)

def setup_inputs(seed: int = 0) -> dict:
    key = jax.random.key(seed)
    ks = jax.random.split(key, 32)

    def nrm(k, shape, scale=1.0):
        return jax.random.normal(k, shape, F32) * scale

    def gain(k, shape):
        return 1.0 + 0.02 * jax.random.normal(k, shape, F32)

    out_scale = (2.0 * DEPTH) ** -0.5
    return {
        'x_prompt': nrm(ks[0], (BATCH, SEQ, D_MODEL)),
        'x_sample': nrm(ks[1], (DEC_BATCH, DEC_SEQ, D_MODEL)),
        'cache_mem_k': nrm(ks[2], (DEPTH, DEC_BATCH, N_MEM, MEM_HEADS, MEM_HEAD_DIM)),
        'cache_mem_v': nrm(ks[3], (DEPTH, DEC_BATCH, N_MEM, MEM_HEADS, MEM_HEAD_DIM)),
        'state_hgrn': nrm(ks[4], (N_HGRN, DEC_BATCH, HG_HEADS, HG_HEAD_DIM, HG_HEAD_DIM), 0.5),
        'cache_swa_k': nrm(ks[5], (N_SWA, DEC_BATCH, WINDOW, SW_KV_HEADS, SW_HEAD_DIM)),
        'cache_swa_v': nrm(ks[6], (N_SWA, DEC_BATCH, WINDOW, SW_KV_HEADS, SW_HEAD_DIM)),
        'mem_prompt': nrm(ks[7], (BATCH, N_MEM, D_MODEL)),
        'norm_mix': gain(ks[8], (DEPTH, D_MODEL)),
        'norm_ffn': gain(ks[9], (DEPTH, D_MODEL)),
        'norm_mem': gain(ks[10], (DEPTH, D_MODEL)),
        'w_in_hgrn': nrm(ks[11], (N_HGRN, D_MODEL, HG_IN), D_MODEL ** -0.5),
        'hgrn_lb_raw': 1.0 + 0.1 * nrm(ks[12], (N_HGRN, TOK_WIDTH)),
        'hgrn_out_norm': gain(ks[13], (N_HGRN, TOK_WIDTH)),
        'w_in_swa': nrm(ks[14], (N_SWA, D_MODEL, SW_IN), D_MODEL ** -0.5),
        'swa_q_norm': gain(ks[15], (N_SWA, SW_HEAD_DIM)),
        'swa_k_norm': gain(ks[16], (N_SWA, SW_HEAD_DIM)),
        'swa_sinks': nrm(ks[17], (N_SWA, SW_Q_HEADS), 0.5),
        'w_mem_kv': nrm(ks[18], (DEPTH, D_MODEL, 2 * MEM_WIDTH), D_MODEL ** -0.5),
        'mem_q_norm': gain(ks[19], (DEPTH, MEM_HEAD_DIM)),
        'mem_k_norm': gain(ks[20], (DEPTH, MEM_HEAD_DIM)),
        'w_out': nrm(ks[21], (DEPTH, MIX_WIDTH, D_MODEL), MIX_WIDTH ** -0.5 * out_scale),
        'w_ffn_in': nrm(ks[22], (DEPTH, D_MODEL, 2 * D_FF), D_MODEL ** -0.5),
        'w_ffn_out': nrm(ks[23], (DEPTH, D_FF, D_MODEL), D_FF ** -0.5 * out_scale),
    }

def reference(x_prompt, x_sample, cache_mem_k, cache_mem_v, state_hgrn, cache_swa_k, cache_swa_v,
              mem_prompt, norm_mix, norm_ffn, norm_mem, w_in_hgrn, hgrn_lb_raw, hgrn_out_norm,
              w_in_swa, swa_q_norm, swa_k_norm, swa_sinks, w_mem_kv, mem_q_norm, mem_k_norm,
              w_out, w_ffn_in, w_ffn_out):
    sm = jax.nn.softmax(hgrn_lb_raw.astype(F32), axis=0)
    lbs = jnp.clip(jnp.cumsum(sm, axis=0) - sm[0], 0.0, LB_MAX)

    def layer(x, i, mk, mv, hg_s0, buf_k, buf_v):
        dt = x.dtype
        B, L, _ = x.shape
        j = i // 2
        h = rmsnorm(x, norm_mix[i])
        if i % 2 == 0:
            p = h @ w_in_hgrn[j]
            tok, st = hgrn_branch(p[..., :4 * TOK_WIDTH], lbs[j], hgrn_out_norm[j], hg_s0)
            new_a, new_b = st.astype(dt), None
            cq = p[..., 4 * TOK_WIDTH:]
        else:
            p = h @ w_in_swa[j]
            nq = SW_Q_HEADS * SW_HEAD_DIM
            nk = SW_KV_HEADS * SW_HEAD_DIM
            q = head_rms(p[..., :nq].reshape(B, L, SW_Q_HEADS, SW_HEAD_DIM), swa_q_norm[j])
            k = head_rms(p[..., nq:nq + nk].reshape(B, L, SW_KV_HEADS, SW_HEAD_DIM), swa_k_norm[j])
            v = p[..., nq + nk:nq + 2 * nk].reshape(B, L, SW_KV_HEADS, SW_HEAD_DIM).astype(F32)
            cq = p[..., nq + 2 * nk:]
            if buf_k is None:
                tok = swa_prompt(q, k, v, swa_sinks[j])
                kb, vb = k[:, -WINDOW:], v[:, -WINDOW:]
            else:
                tok, kb, vb = swa_sample(q, k, v, buf_k, buf_v, swa_sinks[j])
            new_a, new_b = kb.astype(dt), vb.astype(dt)
        mo = mem_attend(cq, mk, mv, mem_q_norm[i])
        x = x + jnp.concatenate([tok.astype(dt), mo.astype(dt)], axis=-1) @ w_out[i]
        gu = rmsnorm(x, norm_ffn[i]) @ w_ffn_in[i]
        g, u = jnp.split(gu, 2, axis=-1)
        x = x + (jax.nn.silu(g) * u) @ w_ffn_out[i]
        return x, new_a, new_b

    dt = x_prompt.dtype
    xp, xs = x_prompt, x_sample
    mk_p, mv_p, hg_p, hg_s, swk_p, swv_p, swk_s, swv_s = [], [], [], [], [], [], [], []
    for i in range(DEPTH):
        j = i // 2
        mkp, mvp = mem_kv(mem_prompt, norm_mem[i], w_mem_kv[i], mem_k_norm[i])
        mk_p.append(mkp.astype(dt))
        mv_p.append(mvp.astype(dt))
        if i % 2 == 0:
            s0 = jnp.zeros((xp.shape[0], HG_HEADS, HG_HEAD_DIM, HG_HEAD_DIM), F32)
            xp, a, _ = layer(xp, i, mkp, mvp, s0, None, None)
            xs, b, _ = layer(xs, i, cache_mem_k[i], cache_mem_v[i], state_hgrn[j], None, None)
            hg_p.append(a)
            hg_s.append(b)
        else:
            xp, kp, vp = layer(xp, i, mkp, mvp, None, None, None)
            xs, ksm, vsm = layer(xs, i, cache_mem_k[i], cache_mem_v[i], None, cache_swa_k[j], cache_swa_v[j])
            swk_p.append(kp)
            swv_p.append(vp)
            swk_s.append(ksm)
            swv_s.append(vsm)

    new_mem_k_prompt = jnp.stack(mk_p)
    new_mem_v_prompt = jnp.stack(mv_p)
    new_hgrn_prompt = jnp.stack(hg_p)
    new_hgrn_sample = jnp.stack(hg_s)
    new_swa_k_prompt = jnp.stack(swk_p)
    new_swa_v_prompt = jnp.stack(swv_p)
    new_swa_k_sample = jnp.stack(swk_s)
    new_swa_v_sample = jnp.stack(swv_s)
    return (xp, xs, new_mem_k_prompt, new_mem_v_prompt, new_hgrn_prompt, new_hgrn_sample,
            new_swa_k_prompt, new_swa_v_prompt, new_swa_k_sample, new_swa_v_sample)


_drawn_inputs = setup_inputs


def setup_inputs(seed=0):
    import zlib

    import numpy as np

    out = dict(_drawn_inputs(seed))
    spreads = {}
    factors = {'norm_ffn': 4.931,
     'norm_mem': 2.853,
     'hgrn_out_norm': 8.0,
     'swa_q_norm': 8.0,
     'swa_sinks': 8.0,
     'mem_q_norm': 8.0,
     'mem_k_norm': 2.943}
    for name, (base, spread) in spreads.items():
        noise = np.random.default_rng([zlib.crc32(name.encode()), seed]).standard_normal(out[name].shape)
        drawn = base * np.exp(spread * noise) if base else spread * noise
        out[name] = __import__('jax').numpy.asarray(drawn.astype(out[name].dtype))
    for name, factor in factors.items():
        out[name] = (out[name] * factor).astype(out[name].dtype)
    return out
```

```python
from contextlib import ExitStack

import numpy as np

import concourse.bass as bass
from concourse import mybir

F32 = mybir.dt.float32
F32R = mybir.dt.float32r
I32 = mybir.dt.int32
ACT = mybir.ActivationFunctionType
ALU = mybir.AluOpType
AX = mybir.AxisListType

P = 128
D = 1024
KT = D // P
SEQ, NB, TQ = 1024, 8, 4
TS = NB * TQ
T = SEQ + TS
NPT = SEQ // P
NT = NPT + 1
N_MEM, HD = 256, 64
HEADS = 6
TOK = HEADS * P
DFF = 2816
NCH = DFF // P
WIN = 128
EPS = 1e-6
NEG = -1e30
TG = 3
TW = T // TG
LEVELS = 7
QG = 3
NPAIR = 1 + 1 + QG

C_ID, C_BLK, C_LVL = 0, P, 2 * P
C_BAND = C_LVL + LEVELS * 64
C_SROW = C_BAND + 2 * 256
C_QB = C_SROW + 160
C_VM = C_QB + 2 * NB * 8
C_END = C_VM + NB

S_MIX, S_FFN, S_MEM = 0, 2 * KT, 4 * KT
S_GN = 6 * KT
S_LB = S_GN + HEADS
S_SQ, S_SK = S_LB + HEADS, S_LB + HEADS + 1
S_MQ, S_MK = S_SK + 1, S_SK + 3
S_SINK = S_MK + 2
S_SROW = S_SINK + 12
S_END = S_SROW + 3
S_L, S_ML, S_GQ = S_END, S_END + HEADS, S_END + 2 * HEADS
S_EPS = S_GQ + 3
S_ALL = S_EPS + 1


def constants():
    c = np.zeros((P, C_END), np.float32)
    p = np.arange(P)
    c[:, C_ID:C_ID + P] = np.eye(P)
    c[:, C_BLK:C_BLK + P] = (p[:, None] // HD == p[None] // HD)
    for l in range(LEVELS):
        w = 1 << l
        t = np.array([t for t in range(P) if (t // w) % 2 == 1])
        ok = (p[:, None] // (2 * w) == t[None] // (2 * w)) & ((p[:, None] // w) % 2 == 0)
        c[:, C_LVL + 64 * l:C_LVL + 64 * l + 64] = ok
    r = np.arange(2 * WIN)[None]
    band = (r > p[:, None]) & (r <= p[:, None] + WIN)
    c[:, C_BAND:C_BAND + 256] = np.where(band & (r >= WIN), 0, NEG)
    c[:, C_BAND + 256:C_BAND + 512] = np.where(band, 0, NEG)
    b, q = p[:, None] // 16, p[:, None] % 4
    r = np.arange(160)[None]
    old = (r < WIN) & (r > q)
    new = (r >= WIN) & ((r - WIN) // TQ == b) & ((r - WIN) % TQ <= q)
    c[:, C_SROW:C_SROW + 160] = np.where(old | new, 0, NEG)
    m = np.zeros((P, 2, NB, 2, 4), np.float32)
    for half in range(2):
        for bb in range(NB):
            for h2 in range(2):
                m[64 * h2:64 * h2 + 64, half, bb, bb % 2, 2 * half + h2] = 1
    c[:, C_QB:C_VM] = m.reshape(P, -1)
    c[:TS, C_VM:] = (np.arange(TS)[:, None] // TQ == np.arange(NB)[None])
    return c


class Steps:

    def __init__(self, sem, names):
        self.sem, self.names, self.len = sem, names, len(names)

    def at(self, n, name):
        return n * self.len + (self.names.index(name) + 1)


MEM_JOBS, PAIR_JOBS, HGRN_JOBS, SWKV_JOBS = 4, 4, 5, 4
MIX_JOBS = [MEM_JOBS + PAIR_JOBS + HGRN_JOBS * HEADS, MEM_JOBS + PAIR_JOBS + SWKV_JOBS + QG * PAIR_JOBS]
FFN_JOBS = 3 * NCH
MIX0 = [0, MIX_JOBS[0] + FFN_JOBS]
FFN0 = [MIX0[0] + MIX_JOBS[0], MIX0[1] + MIX_JOBS[1]]
JOBS = FFN0[1] + FFN_JOBS
ODD, EVEN = (0, 4, 1), (2, 5, 3)
NRAW = 3
OUTG = 2 * NT
MIX_OUTS = [1 + HEADS, 1 + QG]
OUT0 = [0, MIX_OUTS[0] + NCH]
FOUT0 = [MIX_OUTS[0], OUT0[1] + MIX_OUTS[1]]
NORM_MIX = [0, 2 * NT + 2]
NORM_FFN = [NT + 2, 3 * NT + 4]


INIT = 6
EOFF = [sum((T if l < 3 else SEQ) >> l for l in range(n)) for n in range(LEVELS + 1)]
NS0 = 2 + 2 * HEADS
NSTORE = NS0 + 2 + 2 + 2 * NB + 2


def rows(i):
    return P if i < NPT else TS


def hybrid_step(nc, x_prompt, x_sample, cache_mem_k, cache_mem_v, state_hgrn, cache_swa_k, cache_swa_v,
                mem_prompt, w_in_hgrn, w_in_swa, w_mem_kv, w_out, w_ffn_in, w_ffn_out, consts, params,
                y_prompt, y_sample, new_mem_k, new_mem_v, new_hg_p, new_hg_s,
                new_swk_p, new_swv_p, new_swk_s, new_swv_s):
    with ExitStack() as ctx:
        def sb(name, cols, dt=F32):
            return ctx.enter_context(nc.sbuf_tensor(name, [P, cols], dt))

        def sem(name):
            return ctx.enter_context(nc.semaphore(name))

        x = sb("x", NT * D)[:, :].rearrange("p (i d) -> p i d", i=NT)
        hT = [sb("hT_hi", KT * T, F32R)[:, :].rearrange("p (k t) -> p k t", k=KT),
              sb("hT_lo", KT * T, F32R)[:, :].rearrange("p (k t) -> p k t", k=KT)]
        raw = sb("w_raw", NRAW * D)[:, :].rearrange("p (s n) -> p s n", s=NRAW)
        w01 = [sb("w_hi01", 2 * D, F32R), sb("w_lo01", 2 * D, F32R)]
        mm = [sb("m_hi", 2 * T, F32R)[:, :].rearrange("p (a t) -> p a t", a=2),
              sb("m_lo", 2 * T, F32R)[:, :].rearrange("p (a t) -> p a t", a=2)]
        cst = sb("consts", C_END)
        par = sb("params", S_ALL)
        nstat = sb("norm_stats", 40)
        nrstd = sb("norm_rstd", 40)

        ARENA = 71328
        slab = ctx.enter_context(nc.sbuf_tensor("arena", [P, ARENA // 4], F32))
        base = nc.sbuf_base - ARENA

        def at(name, off, cols, dt=F32):
            assert off + 4 * cols <= ARENA, name
            return nc.alloc_sbuf_tensor_at(name, [P, cols], dt, offset=base + off)

        w25 = [at("w_hi25", 0, 4 * D, F32R), at("w_lo25", 16384, 4 * D, F32R)]
        sg = at("gate_silu", 32768, T)
        gated = at("gated", 36992, T)
        xn = at("normed", 41216, 2 * D)[:, :].rearrange("p (a d) -> p a d", a=2)
        gained = at("normed_gained", 49408, D)
        NORM_END = 53504
        xmem = at("mem_rows", NORM_END, 2 * D)[:, :].rearrange("p (i d) -> p i d", i=2)
        memT = [at("memT_hi", 0, KT * N_MEM, F32R)[:, :].rearrange("p (k t) -> p k t", k=KT),
                at("memT_lo", 8192, KT * N_MEM, F32R)[:, :].rearrange("p (k t) -> p k t", k=KT)]
        prob = at("prob", 16384, T)
        probT = at("probT", 20608, T)
        qh = at("q_heads", 24832, 2 * T)[:, :].rearrange("p (a t) -> p a t", a=2)
        kmem = at("k_mem", 33280, 2 * N_MEM)[:, :].rearrange("p (a m) -> p a m", a=2)
        vmem = at("v_mem", 35328, 2 * N_MEM)[:, :].rearrange("p (i c) -> p i c", i=2)
        ktok_mem = at("k_mem_rows", 12288, 2 * N_MEM)[:, :].rearrange("p (i c) -> p i c", i=2)
        qblk = at("q_blocks", 37376, 2 * NB * 32)[:, :].rearrange("p (a b c) -> p a b c", a=2, b=NB)
        sprob = at("sample_prob", 39424, 256)
        sprobT = at("sample_probT", 40448, 256)[:, :].rearrange("p (c r) -> p c r", c=2)
        kcT = at("k_cacheT", 41472, 2 * 512)[:, :].rearrange("p (z n) -> p z n", z=2)
        ast = at("attn_stats", 45568, 40)
        cacheb = at("cache", 45728, NB * 512)
        kpad = at("k_window", 0, 2 * (P + T))[:, :].rearrange("p (a t) -> p a t", a=2)
        vwin = at("v_window", 62112, NT * 256)[:, :].rearrange("p (i c) -> p i c", i=NT)
        ktok = at("k_window_rows", 33280, 2 * 256)[:, :].rearrange("p (i c) -> p i c", i=2)
        Q = at("hg_q", 0, T)
        K = at("hg_k", 4224, T)
        E = at("hg_decay", 8448, 2096)
        tA = at("hg_sig", 16832, T)
        G = at("hg_gate", 21056, T)
        V = at("hg_v", 25280, NT * P)[:, :].rearrange("p (i c) -> p i c", i=NT)
        att = at("hg_att", 29888, T)
        KR = at("hg_k_rows", 34112, NT * P)[:, :].rearrange("p (i c) -> p i c", i=NT)
        O2 = at("hg_o_square", 38720, T)
        R = at("hg_rstd", 42944, T)
        VM = at("hg_v_blocks", 47168, NB * P)
        ones = at("ones", 51264, P)
        S = at("hg_states", NORM_END, NPT * P)[:, :].rearrange("p (i c) -> p i c", i=NPT)
        S0 = at("hg_state_in", NORM_END + 4096, NB * P)
        SN = at("hg_state_out", NORM_END + 8192, NB * P)

        ps = ctx.enter_context(nc.psum_tensor("ps", [P, 8, 512], F32))

        raw_loaded = [sem(f"raw_loaded{s}") for s in range(NRAW)]
        w_hi, w_lo, w_used = sem("w_hi"), sem("w_lo"), sem("w_used")
        small_in, x_in, mem_in, side_in = sem("small_in"), sem("x_in"), sem("mem_in"), sem("side_in")
        stored, stored_y = sem("stored"), sem("stored_y")
        out_ready, x_added = sem("out_ready"), sem("x_added")
        init, lb_exp = sem("init"), sem("lb_exp")
        nA, nH = Steps(sem("norm_stats_act"), ["sq", "std"]), Steps(sem("norm_hi"), ["hi"])
        nV, nG = Steps(sem("norm_rows_vec"), ["rstd", "xn"]), Steps(sem("norm_gain_vec"), ["g0", "g1"])
        nT, nP = Steps(sem("norm_pe"), ["tr"]), Steps(sem("norm_pool"), ["lo"])
        fT, fA, fV = (Steps(sem("ffn_pe"), ["g", "u"]), Steps(sem("ffn_act"), ["silu", "hi"]),
                      Steps(sem("ffn_vec"), ["mul", "lo"]))
        mT = Steps(sem("memkv_pe"), ["k", "v", "ssq", "rows"])
        mA = Steps(sem("memkv_act"), ["sq", "std"])
        mV = Steps(sem("memkv_vec"), ["rstd", "k", "v", "rows"])
        qT, qA, qV = (Steps(sem("headnorm_pe"), ["proj", "ssq"]), Steps(sem("headnorm_act"), ["sq", "std"]),
                      Steps(sem("headnorm_vec"), ["rstd", "n"]))
        aT = Steps(sem("attn_pe"), ["sc", "pt", "pv"])
        aA = Steps(sem("attn_act"), [f"e{i}" for i in range(4)] + ["sink", "pt"])
        aV = Steps(sem("attn_vec"), ["max", "neg", "den", "rinv", "p", "pt", "o"])
        sT = Steps(sem("sample_pe"), [f"kt{b}" for b in range(NB)] + ["sc", "pt", "pv"])
        sA = Steps(sem("sample_act"), [f"kt{b}" for b in range(NB)] + ["exp", "sink"])
        sV = Steps(sem("sample_vec"), ["qb", "max", "neg", "den", "rinv", "p", "pt", "o0", "o1"])
        oA, oV = Steps(sem("pair_out_act"), ["hi"]), Steps(sem("pair_out_vec"), ["lo"])
        kT, kV = Steps(sem("window_pe"), ["v", "rows"]), Steps(sem("window_vec"), ["pad", "v", "rows"])
        hT_ = Steps(sem("hgrn_pe"), ["q", "z", "g", "v", "diag"] + [f"l{l}" for l in range(LEVELS)]
                    + ["kr", "ds", "o", "ssq"])
        hA = Steps(sem("hgrn_act"), ["sq", "f", "k", "sg", "kr", "o2", "std", "hi"])
        hV = Steps(sem("hgrn_vec"), ["q", "e", "k", "g", "v", "vm", "diag", "qf"]
                   + [f"{s}{l}" for l in range(LEVELS) for s in "aq"] + [f"s{i}" for i in range(NPT)]
                   + ["sn", "sd", "rstd", "o", "m", "lo"])
        hP = Steps(sem("hgrn_pool"), [f"{s}{l}" for l in range(LEVELS) for s in "ke"])
        block = ctx.enter_context(nc.Block())

        ident = cst[:, C_ID:C_ID + P]

        def col(c, n=1):
            return par[:, c:c + n]

        def slot(which, s):
            t = w01[which][:, s * D:(s + 1) * D] if s < 2 else w25[which][:, (s - 2) * D:(s - 1) * D]
            return t

        def wait(eng, steps, n, name):
            eng.wait_ge(steps.sem, steps.at(n, name))

        def fm(b0, n=TW):
            return ps[:, b0:b0 + TG, 0:n]

        def three(t):
            return t.rearrange("p (g n) -> p g n", g=TG)

        def w_cols(w, c0, s):
            v, dst = w.rearrange("(k p) n -> p k n", p=P), raw[:, s, :].rearrange("p (k n) -> p k n", k=KT)
            return [(dst[:, 0:4], v[:, 0:4, c0:c0 + P]), (dst[:, 4:8], v[:, 4:8, c0:c0 + P])]

        def w_two_heads(w, ha, hb, s):
            v, dst = w.rearrange("(k p) n -> p k n", p=P), raw[:, s, :].rearrange("p (k n) -> p k n", k=KT)
            return [(dst[:, :, 64 * z:64 * z + 64], v[:, :, 64 * h:64 * h + 64]) for z, h in enumerate((ha, hb))]

        def w_rows(w, ra, rb, s):
            return [(raw[0:64, s, :], w[ra:ra + 64]), (raw[64:P, s, :], w[rb:rb + 64])]

        def mixer_jobs(L):
            wm = w_mem_kv[L]
            jobs = [lambda s, c=c: w_cols(wm, c * P, s) for c in range(4)]
            win, c0 = (w_in_hgrn[0], 4 * TOK) if L == 0 else (w_in_swa[0], 5 * 256)
            jobs += [lambda s, h=h: w_cols(win, c0 + h * P, s) for h in range(2)]
            jobs += [lambda s, h=h: w_rows(w_out[L], TOK + h * P, TOK + h * P + 64, s) for h in range(2)]
            if L == 0:
                for h in range(HEADS):
                    jobs += [lambda s, c=c, h=h: w_cols(win, c * TOK + h * P, s) for c in (0, 1, 3, 2)]
                    jobs += [lambda s, h=h: w_rows(w_out[L], h * P, h * P + 64, s)]
            else:
                jobs += [lambda s, c=c: w_cols(win, TOK + c * P, s) for c in range(4)]
                for g in range(QG):
                    heads = [(3 * 2 * half + g, 3 * (2 * half + 1) + g) for half in range(2)]
                    jobs += [lambda s, hh=hh: w_two_heads(win, hh[0], hh[1], s) for hh in heads]
                    jobs += [lambda s, hh=hh: w_rows(w_out[L], 64 * hh[0], 64 * hh[1], s) for hh in heads]
            assert len(jobs) == MIX_JOBS[L]
            return jobs

        def ffn_job(L, kind, c, s):
            if kind == "o":
                w = w_ffn_out[L]
                return [(raw[64 * z:64 * z + 64, s, :], w[bass.ds(c * P + 64 * z, 64)]) for z in range(2)]
            v = w_ffn_in[L].rearrange("(k p) n -> p k n", p=P)
            dst = raw[:, s, :].rearrange("p (k n) -> p k n", k=KT)
            c0 = c * P + (DFF if kind == "u" else 0)
            return [(dst[:, 4 * z:4 * z + 4], v[:, 4 * z:4 * z + 4, bass.ds(c0, P)]) for z in range(2)]

        @block.sync
        def _(sp):
            def load(j3, n3, jv, parts):
                if not (isinstance(jv, int) and jv < NRAW):
                    sp.wait_ge(w_hi, jv - 2)
                    sp.wait_ge(w_lo, jv - 2)
                for dst, src in parts(j3):
                    sp.dma_start(dst, src).then_inc(raw_loaded[j3], 16)

            def store(dst, src):
                sp.dma_start(dst, src).then_inc(stored, 16)

            def cache_rows(c, L, n):
                return c[L].rearrange("b (i p) h d -> p b i (h d)", p=P)

            sp.dma_start(cst[:, :], consts).then_inc(small_in, 16)
            sp.dma_start(par[:, 0:S_END], params).then_inc(small_in, 16)
            for i in range(NPT):
                sp.dma_start(x[:, i, :], x_prompt[0, i * P:(i + 1) * P, :]).then_inc(x_in, 16)
            sp.dma_start(x[0:TS, NPT, :], x_sample.rearrange("b t d -> (b t) d")).then_inc(x_in, 16)
            for L in range(2):
                if L == 1:
                    sp.wait_ge(stored, 16 * NS0)
                    wait(sp, hT_, HEADS - 1, "o")
                    wait(sp, hT_, HEADS - 1, "o")
                sp.dma_start(xmem, mem_prompt[0].rearrange("(i p) d -> p i d", p=P)).then_inc(mem_in, 16)
                jobs = mixer_jobs(L)
                for n, job in enumerate(jobs):
                    j = MIX0[L] + n
                    if n == MEM_JOBS:
                        wait(sp, nH, NORM_MIX[L] + NT + 1, "hi")
                        wait(sp, nP, NORM_MIX[L] + NT + 1, "lo")
                        for z in range(2):
                            sp.dma_start(cacheb[:, :].rearrange("p (b i c) -> p b i c", b=NB, i=2)[:, 4 * z:4 * z + 4],
                                         cache_rows(cache_mem_k, L, 2)[:, 4 * z:4 * z + 4]).then_inc(side_in, 16)
                    if n == MEM_JOBS + PAIR_JOBS:
                        wait(sp, mV, L, "rows")
                        for z, (t, d) in enumerate(((ktok_mem, new_mem_k), (vmem, new_mem_v))):
                            store(d[L, 0].rearrange("(i p) h d -> p i (h d)", p=P), t)
                        if L == 1:
                            wait(sp, sT, 1, "pv")
                            for z, cc in enumerate((cache_swa_k, cache_swa_v)):
                                sp.dma_start(cacheb[:, z * 2048:(z + 1) * 2048].rearrange("p (b c) -> p b c", b=NB),
                                             cc[0].rearrange("b p h d -> p b (h d)")).then_inc(side_in, 16)
                    if L == 0 and n >= MEM_JOBS + PAIR_JOBS and (n - MEM_JOBS - PAIR_JOBS) % HGRN_JOBS == 0:
                        h = (n - MEM_JOBS - PAIR_JOBS) // HGRN_JOBS
                        if h == 0:
                            wait(sp, sT, 0, "pv")
                        else:
                            wait(sp, hV, h - 1, "sd")
                            store(new_hg_p[0, 0, h - 1], S[:, NPT - 1, :])
                            store(new_hg_s[0, :, h - 1].rearrange("b c v -> c b v"),
                                  SN[:, :].rearrange("p (b v) -> p b v", b=NB))
                            wait(sp, hT_, h - 1, "o")
                        sp.dma_start(S0[:, :].rearrange("p (b v) -> p b v", b=NB),
                                     state_hgrn[0, :, h].rearrange("b c v -> c b v")).then_inc(side_in, 16)
                    load(j % 3, j // 3, j, job)
                if L == 0:
                    wait(sp, hV, HEADS - 1, "sd")
                    store(new_hg_p[0, 0, HEADS - 1], S[:, NPT - 1, :])
                    store(new_hg_s[0, :, HEADS - 1].rearrange("b c v -> c b v"),
                          SN[:, :].rearrange("p (b v) -> p b v", b=NB))
                else:
                    wait(sp, kV, 0, "rows")
                    store(new_swk_p[0, 0].rearrange("w h d -> w (h d)"), ktok[:, 0, :])
                    store(new_swv_p[0, 0].rearrange("w h d -> w (h d)"), vwin[:, NPT - 1, :])
                    for b in range(NB):
                        store(new_swk_s[0, b, WIN - TQ:].rearrange("w h d -> w (h d)"),
                              ktok[TQ * b:TQ * b + TQ, 1, :])
                        store(new_swv_s[0, b, WIN - TQ:].rearrange("w h d -> w (h d)"),
                              vwin[TQ * b:TQ * b + TQ, NPT, :])
                    for z, (o, cc) in enumerate(((new_swk_s, cache_swa_k), (new_swv_s, cache_swa_v))):
                        store(o[0, :, 0:WIN - TQ].rearrange("b w h d -> b (w h d)"),
                              cc[0, :, TQ:].rearrange("b w h d -> b (w h d)"))
                j0 = FFN0[L]

                def ffn_load(d, kind, it, c):
                    j = j0 + d
                    load(j % 3, None, j + 3 * it, lambda s: ffn_job(L, kind, c, s))

                ffn_load(0, "g", 0, 0)
                ffn_load(1, "u", 0, 0)
                with sp.Fori(1, NCH) as c:
                    ffn_load(-1, "g", c, c)
                    ffn_load(0, "o", c, c - 1)
                    ffn_load(1, "u", c, c)
                ffn_load(-1, "o", NCH, NCH - 1)
            for i in range(NT):
                sp.wait_ge(x_added, (FOUT0[1] + NCH - 1) * OUTG + 2 * i + 2)
                dst = y_prompt[0, i * P:(i + 1) * P, :] if i < NPT else y_sample.rearrange("b t d -> (b t) d")
                sp.dma_start(dst, x[0:rows(i), i, :]).then_inc(stored_y, 16)
            sp.wait_ge(stored, 16 * NSTORE)
            sp.wait_ge(stored_y, 16 * NT)

        def mix_slot(L, n):
            return n % 2

        def split_free(L, n):
            j = MIX0[L] + n
            if n < 2:
                return 0 if L == 0 else MIX0[1] - 1
            return j - 1

        def hi_split(act, j3, n3, s, free):
            act.wait_ge(raw_loaded[j3], (n3 + 1) * 32)
            if not (isinstance(free, int) and free <= 0):
                act.wait_ge(w_used, free)
            nc.scalar.activation(slot(0, s), raw[:, j3, :], ACT.Copy).then_inc(w_hi, 1)

        def lo_split(pool, j3, jv, s, free):
            pool.wait_ge(w_hi, jv + 1)
            nc.gpsimd.tensor_tensor(slot(1, s), raw[:, j3, :], slot(0, s).bitcast(F32),
                                    ALU.subtract).then_inc(w_lo, 1)

        class Pump:

            def __init__(self, L, emit):
                self.L, self.n, self.emit = L, 0, emit

            def upto(self, n):
                while self.n < min(n, MIX_JOBS[self.L]):
                    j = MIX0[self.L] + self.n
                    self.emit(j, mix_slot(self.L, self.n), split_free(self.L, self.n))
                    self.n += 1

        def act_emit(act):
            return lambda j, s, free: hi_split(act, j % 3, j // 3, s, free)

        def pool_emit(pool):
            return lambda j, s, free: lo_split(pool, j % 3, j, s, free)

        def ffn_splits(L, split, it, c_par, kinds="gou"):
            slots = ODD if c_par else EVEN
            for k, (kind, d) in enumerate((("g", -1), ("o", 0), ("u", 1))):
                if kind in kinds:
                    split(FFN0[L] + d, it, slots[k], 1 if kind == "g" else 0)

        @block.scalar
        def _(act):
            def A(out, in_, fn, steps, n, name, **kw):
                nc.scalar.activation(out, in_, fn, **kw).then_inc(steps.sem, 1)

            def norm_in(r, src, m):
                if r >= 2:
                    wait(act, nT, r - 2, "tr")
                A(xn[0:m, r % 2, :], src[0:m], ACT.Square, nA, r, "sq", accum_out=nstat[0:m, r:r + 1])
                wait(act, nA, r, "sq")
                A(nstat[0:m, r:r + 1], nstat[0:m, r:r + 1], ACT.Sqrt, nA, r, "std",
                  scale=1.0 / D, bias=col(S_EPS)[0:m])

            def norm_hi(r, dst, c0, m):
                wait(act, nG, r, "g1")
                A(dst[0][:, :, c0:c0 + m], gained[:, 0:KT * m].rearrange("p (k t) -> p k t", k=KT),
                  ACT.Copy, nH, r, "hi")

            def norms(r0, first=None, mem=False):
                srcs = [(x[:, i, :], rows(i), hT, i * P) for i in range(NT)]
                if mem:
                    srcs += [(xmem[:, i, :], P, memT, i * P) for i in range(2)]
                for i in range(len(srcs) + 3):
                    if i < len(srcs):
                        src, m, dst, c0 = srcs[i]
                        if i >= NT:
                            act.wait_ge(mem_in, 16 * (2 if r0 else 1))
                        elif first is None:
                            act.wait_ge(x_in, 16 * NT)
                        else:
                            act.wait_ge(x_added, first * OUTG + 2 * i + 2)
                        norm_in(r0 + i, src, m)
                    if i >= 3:
                        src, m, dst, c0 = srcs[i - 3]
                        norm_hi(r0 + i - 3, dst, c0, m)

            def head_norm(u):
                wait(act, qT, u, "proj")
                A(three(prob[:, :]), fm(0), ACT.Square, qA, u, "sq")
                wait(act, qT, u, "ssq")
                A(three(probT[:, :]), fm(3), ACT.Sqrt, qA, u, "std", scale=1.0 / HD, bias=col(S_EPS))

            def prompt_attn(r, sink):
                wait(act, aV, r, "neg")
                for i in range(4):
                    src = ps[:, i // 2, 256 * (i % 2):256 * (i % 2) + 256] if sink is None \
                        else prob[:, 256 * i:256 * i + 256]
                    A(prob[:, 256 * i:256 * i + 256], src, ACT.Exp, aA, r, f"e{i}",
                      bias=ast[:, 4 + i:5 + i], accum_out=ast[:, 8 + i:9 + i])
                if sink is not None:
                    A(ast[:, 12:16], ast[:, 4:8], ACT.Exp, aA, r, "sink", bias=sink)
                else:
                    A(ast[:, 12:16], ast[:, 4:8], ACT.Copy, aA, r, "sink")
                wait(act, aT, r, "pt")
                A(probT[:, 0:512], ps[:, 4, :], ACT.Copy, aA, r, "pt")

            def sample_attn(p, sink):
                n = 1 if sink is not None else 2
                for b in range(NB):
                    wait(act, sT, p, f"kt{b}")
                    A(kcT[:, b % 2, 0:256 * n], ps[:, 6 + b % 2, 0:256 * n], ACT.Copy, sA, p, f"kt{b}")
                if sink is None:
                    for z in range(2):
                        act.dma_start(cacheb[:, :].rearrange("p (b i c) -> p b i c", b=NB, i=2)[:, 4 * z:4 * z + 4],
                                      cache_mem_v[p].rearrange("b (i p) h d -> p b i (h d)", p=P)[:, 4 * z:4 * z + 4]
                                      ).then_inc(side_in, 16)
                wait(act, sV, p, "neg")
                w = 256 if sink is None else 160
                A(sprob[:, 0:w], ps[:, 0, 0:w] if sink is None else sprob[:, 0:w], ACT.Exp, sA, p, "exp",
                  bias=ast[:, 33:34], accum_out=ast[:, 34:35])
                if sink is not None:
                    A(ast[:, 35:36], ast[:, 33:34], ACT.Exp, sA, p, "sink", bias=sink)
                else:
                    A(ast[:, 35:36], ast[:, 33:34], ACT.Copy, sA, p, "sink")

            def pair(p, u0, pump, n0, g):
                for half in range(2):
                    pump.upto(n0 + half + 2)
                    head_norm(u0 + half)
                pump.upto(n0 + 4)
                for half in range(2):
                    for h2 in range(2):
                        head = 3 * (2 * half + h2) + g if g is not None else None
                        for q in range(2):
                            prompt_attn(8 * p + 4 * half + 2 * h2 + q, None if g is None else col(S_SINK + head))
                sample_attn(p, None if g is None else col(S_SROW + g))
                wait(act, sV, p, "o1")
                A(mm[0][:, :, :], qh, ACT.Copy, oA, p, "hi")

            def ffn(L):
                def split(jb, it, s, extra):
                    hi_split(act, jb % 3, jb // 3 + it, s, jb + 3 * it - 5 + extra)

                def chunk(r, par_, c):
                    wait(act, fT, r, "g")
                    if not (isinstance(r, int) and r == 0):
                        wait(act, fV, r - 1, "mul")
                    A(three(sg[:, :]), fm(0), ACT.Silu, fA, r, "silu")
                    wait(act, fV, r, "mul")
                    A(mm[0][:, par_, :], gated[:, :], ACT.Copy, fA, r, "hi")

                if L == 0:
                    wait(act, hV, HEADS - 1, "lo")
                else:
                    wait(act, oV, NPAIR - 1, "lo")
                    act.wait_ge(stored, 16 * NSTORE)
                for d, s in ((0, EVEN[0]), (1, EVEN[2])):
                    j = FFN0[L] + d
                    hi_split(act, j % 3, j // 3, s, 0)
                norms(NORM_FFN[L], first=FOUT0[L] - 1)
                act.wait_ge(w_used, FFN0[L])
                ffn_splits(L, split, 1, 1)
                chunk(NCH * L, 0, 0)
                with act.Fori(0, (NCH - 2) // 2) as it:
                    for z in range(2):
                        c = 2 * it + 1 + z
                        ffn_splits(L, split, c + 1, z)
                        chunk(c + NCH * L, 1 - z, c)
                ffn_splits(L, split, NCH, 0, "g")
                chunk(NCH * L + NCH - 1, 1, NCH - 1)

            def hgrn_head(h, pump, n0):
                if h == 0:
                    act.wait_ge(stored, 16 * 2)
                pump.upto(n0 + 2)
                wait(act, hT_, h, "q")
                A(three(tA[:, :]), fm(0), ACT.Sigmoid, hA, h, "sq")
                pump.upto(n0 + 3)
                wait(act, hT_, h, "z")
                A(three(E[:, 0:T]), fm(3), ACT.Sigmoid, hA, h, "f")
                A(three(K[:, :]), fm(3), ACT.Sigmoid, hA, h, "k", scale=-1.0)
                pump.upto(n0 + 4)
                wait(act, hT_, h, "g")
                A(three(tA[:, :]), fm(0), ACT.Sigmoid, hA, h, "sg")
                pump.upto(n0 + 5)
                wait(act, hT_, h, "kr")
                nc.scalar.activation(KR[:, 0:4, :], ps[:, 6, :].rearrange("p (i c) -> p i c", i=4), ACT.Copy)
                nc.scalar.activation(KR[:, 4:8, :], ps[:, 7, :].rearrange("p (i c) -> p i c", i=4), ACT.Copy)
                A(KR[0:TS, 8, :], ps[0:TS, 0, 0:P], ACT.Copy, hA, h, "kr")
                wait(act, hT_, h, "o")
                nc.scalar.activation(O2[:, 0:SEQ].rearrange("p (g n) -> p g n", g=2), ps[:, 3:5, :], ACT.Square)
                A(O2[:, SEQ:T], ps[:, 5, 0:TS], ACT.Square, hA, h, "o2")
                wait(act, hT_, h, "ssq")
                A(three(R[:, :]), fm(0), ACT.Sqrt, hA, h, "std", scale=1.0 / P, bias=col(S_EPS))
                wait(act, hV, h, "m")
                A(mm[0][:, 0, :], tA[:, :], ACT.Copy, hA, h, "hi")

            act.wait_ge(small_in, 32)
            act.wait_ge(init, 1)
            nc.scalar.activation(col(S_L, HEADS), col(S_L, HEADS), ACT.Exp).then_inc(lb_exp, 1)
            for L in range(2):
                pump = Pump(L, act_emit(act))
                pump.upto(2)
                norms(NORM_MIX[L], first=None if L == 0 else FOUT0[0] + NCH - 1, mem=True)
                pump.upto(MEM_JOBS)
                wait(act, mT, L, "k")
                A(prob[:, 0:512], ps[:, 0, :], ACT.Square, mA, L, "sq")
                pump.upto(MEM_JOBS + 1)
                wait(act, mT, L, "ssq")
                A(probT[:, 0:512], ps[:, 2, :], ACT.Sqrt, mA, L, "std", scale=1.0 / HD, bias=col(S_EPS))
                pair(L, [0, 2][L], pump, MEM_JOBS, None)
                n0 = MEM_JOBS + PAIR_JOBS
                if L == 0:
                    for h in range(HEADS):
                        hgrn_head(h, pump, n0 + HGRN_JOBS * h)
                else:
                    for half in range(2):
                        pump.upto(n0 + half + 2)
                        head_norm(4 + half)
                    pump.upto(n0 + 4)
                    for g in range(QG):
                        pair(2 + g, 6 + 2 * g, pump, n0 + SWKV_JOBS + PAIR_JOBS * g, g)
                pump.upto(MIX_JOBS[L])
                ffn(L)

        @block.gpsimd
        def _(pool):
            def norms(r0, mem=False):
                for i in range(NT + (2 if mem else 0)):
                    dst, c0, m = (hT, i * P, rows(i)) if i < NT else (memT, (i - NT) * P, P)
                    wait(pool, nH, r0 + i, "hi")
                    nc.gpsimd.tensor_tensor(dst[1][:, :, c0:c0 + m],
                                            gained[:, 0:KT * m].rearrange("p (k t) -> p k t", k=KT),
                                            dst[0][:, :, c0:c0 + m].bitcast(F32), ALU.subtract).then_inc(nP.sem, 1)

            def ffn(L):
                def split(jb, it, s, extra):
                    lo_split(pool, jb % 3, jb + 3 * it, s, None)

                for d, s in ((0, EVEN[0]), (1, EVEN[2])):
                    lo_split(pool, (FFN0[L] + d) % 3, FFN0[L] + d, s, None)
                norms(NORM_FFN[L])
                ffn_splits(L, split, 1, 1)
                with pool.Fori(0, (NCH - 2) // 2) as it:
                    for z in range(2):
                        ffn_splits(L, split, 2 * it + 2 + z, z)
                ffn_splits(L, split, NCH, 0, "g")

            def hgrn_head(h, pump, n0):
                pump.upto(n0 + 5)
                for l in range(LEVELS):
                    w = 1 << l
                    n = T if l < 2 else SEQ
                    Eo = E[:, EOFF[l]:EOFF[l] + n // w].rearrange("p (b z) -> p b z", z=2)
                    wait(pool, hT_, h, f"l{l}")
                    if l:
                        wait(pool, hP, h, f"e{l - 1}")
                    Kv = K[:, 0:n].rearrange("p (b z w) -> p b z w", z=2, w=w)[:, :, 0, :]
                    nc.gpsimd.tensor_tensor(Kv, Kv, Eo[:, :, 1].unsqueeze(2).to_broadcast([P, n // (2 * w), w]),
                                            ALU.mult).then_inc(hP.sem, 1)
                    nc.gpsimd.tensor_tensor(E[:, EOFF[l + 1]:EOFF[l + 1] + n // (2 * w)], Eo[:, :, 0], Eo[:, :, 1],
                                            ALU.mult).then_inc(hP.sem, 1)

            for L in range(2):
                pump = Pump(L, pool_emit(pool))
                pump.upto(2)
                norms(NORM_MIX[L], mem=True)
                if L == 0:
                    pump.upto(MEM_JOBS + PAIR_JOBS)
                    for h in range(HEADS):
                        hgrn_head(h, pump, MEM_JOBS + PAIR_JOBS + HGRN_JOBS * h)
                pump.upto(MIX_JOBS[L])
                ffn(L)

        @block.vector
        def _(dve):
            V_ = nc.vector

            def tt(out, a, b, op=ALU.mult):
                return V_.tensor_tensor(out, a, b, op)

            def stt(out, a, s, b, op0=ALU.mult, op1=ALU.mult):
                return V_.scalar_tensor_tensor(out=out, in0=a, scalar=s, in1=b, op0=op0, op1=op1)

            def add_group(G, i, n):
                dve.wait_ge(out_ready, G + 1)
                if not isinstance(G, int) or G >= OUTG:
                    dve.wait_ge(x_added, G - OUTG + 1)
                xs = x[0:rows(i), i, 512 * n:512 * n + 512]
                tt(xs, xs, ps[0:rows(i), 6 + n, :], ALU.add).then_inc(x_added, 1)

            def adds(o, after=None):
                for i in range(NT):
                    for n in range(2):
                        add_group(o * OUTG + 2 * i + n, i, n)
                    if after:
                        after(i)

            def norms(r0, gain, mem_gain=None, o=None):
                srcs = [(x[:, i, :], rows(i), gain) for i in range(NT)]
                if mem_gain is not None:
                    srcs += [(xmem[:, i, :], P, mem_gain) for i in range(2)]
                for i in range(len(srcs) + 3):
                    if o is not None and i < NT:
                        for n in range(2):
                            add_group(o * OUTG + 2 * i + n, i, n)
                    if 1 <= i <= len(srcs):
                        r, (src, m, _) = r0 + i - 1, srcs[i - 1]
                        wait(dve, nA, r, "std")
                        V_.reciprocal(nrstd[0:m, r:r + 1], nstat[0:m, r:r + 1]).then_inc(nV.sem, 1)
                        wait(dve, nV, r, "rstd")
                        V_.tensor_scalar(xn[0:m, r % 2, :], src[0:m], nrstd[0:m, r:r + 1], None,
                                         ALU.mult).then_inc(nV.sem, 1)
                    if i >= 3:
                        r, (_, m, g) = r0 + i - 3, srcs[i - 3]
                        wait(dve, nT, r, "tr")
                        if r:
                            wait(dve, nP, r - 1, "lo")
                        for z in range(2):
                            b = 2 * (r % 2) + z
                            tt(gained[:, 4 * m * z:4 * m * (z + 1)].rearrange("p (k t) -> p k t", k=4),
                               ps[:, b, 0:4 * m].rearrange("p (k t) -> p k t", k=4),
                               col(g + 4 * z, 4).unsqueeze(2).to_broadcast([P, 4, m])).then_inc(nG.sem, 1)

            def head_norm(u, dst, gain):
                wait(dve, qA, u, "std")
                V_.reciprocal(probT[:, :], probT[:, :]).then_inc(qV.sem, 1)
                wait(dve, qV, u, "rstd")
                stt(three(dst), fm(0), gain, three(probT[:, :])).then_inc(qV.sem, 1)

            def prompt_attn(r, half, h2, q, head):
                wait(dve, aT, r, "sc")
                if head is None:
                    V_.tensor_reduce(ast[:, 0:4], ps[:, 0:2, :].rearrange("p b (i m) -> p (b i) m", i=2),
                                     AX.X, ALU.max).then_inc(aV.sem, 1)
                else:
                    for i in range(4):
                        first = q == 0 and i == 0
                        band = cst[:, C_BAND + (0 if first else 256):C_BAND + (0 if first else 256) + 256]
                        m = V_.tensor_tensor_reduce(prob[:, 256 * i:256 * i + 256],
                                                    ps[:, i // 2, 256 * (i % 2):256 * (i % 2) + 256], band, 1.0,
                                                    col(S_SINK + head), ALU.add, ALU.max, ast[:, i:i + 1])
                    m.then_inc(aV.sem, 1)
                wait(dve, aV, r, "max")
                V_.tensor_scalar(ast[:, 4:8], ast[:, 0:4], -1.0, None, ALU.mult).then_inc(aV.sem, 1)
                wait(dve, aA, r, "sink")
                if head is None:
                    V_.tensor_copy(ast[:, 16:20], ast[:, 8:12]).then_inc(aV.sem, 1)
                else:
                    tt(ast[:, 16:20], ast[:, 8:12], ast[:, 12:16], ALU.add).then_inc(aV.sem, 1)
                wait(dve, aV, r, "den")
                V_.reciprocal(ast[:, 20:24], ast[:, 16:20]).then_inc(aV.sem, 1)
                wait(dve, aV, r, "rinv")
                pv = prob[:, 0:1024].rearrange("p (i m) -> p i m", i=4)
                tt(pv, pv, ast[:, 20:24].unsqueeze(2).to_broadcast([P, 4, 256])).then_inc(aV.sem, 1)
                wait(dve, aT, r, "pt")
                V_.tensor_copy(probT[:, 512:1024], ps[:, 5, :]).then_inc(aV.sem, 1)
                wait(dve, aT, r, "pv")
                V_.tensor_copy(qh[64 * h2:64 * h2 + 64, half, 512 * q:512 * q + 512],
                               ps[64 * h2:64 * h2 + 64, 2, :]).then_inc(aV.sem, 1)

            def sample_attn(p, g):
                for half in range(2):
                    m = tt(qblk[:, half, :, :].rearrange("p b (s q) -> p b s q", q=TQ),
                           qh[:, half, SEQ:T].rearrange("p (b q) -> p b q", q=TQ).unsqueeze(2)
                           .to_broadcast([P, NB, 8, TQ]),
                           cst[:, C_QB + 64 * half:C_QB + 64 * half + 64].rearrange("p (b s) -> p b s", b=NB)
                           .unsqueeze(3).to_broadcast([P, NB, 8, TQ]))
                m.then_inc(sV.sem, 1)
                wait(dve, sT, p, "sc")
                if g is None:
                    V_.tensor_reduce(ast[:, 32:33], ps[:, 0, 0:256], AX.X, ALU.max).then_inc(sV.sem, 1)
                else:
                    V_.tensor_tensor_reduce(sprob[:, 0:160], ps[:, 0, 0:160], cst[:, C_SROW:C_SROW + 160], 1.0,
                                            col(S_SROW + g), ALU.add, ALU.max, ast[:, 32:33]).then_inc(sV.sem, 1)
                wait(dve, sV, p, "max")
                V_.tensor_scalar(ast[:, 33:34], ast[:, 32:33], -1.0, None, ALU.mult).then_inc(sV.sem, 1)
                wait(dve, sA, p, "sink")
                if g is None:
                    V_.tensor_copy(ast[:, 36:37], ast[:, 34:35]).then_inc(sV.sem, 1)
                else:
                    tt(ast[:, 36:37], ast[:, 34:35], ast[:, 35:36], ALU.add).then_inc(sV.sem, 1)
                wait(dve, sV, p, "den")
                V_.reciprocal(ast[:, 37:38], ast[:, 36:37]).then_inc(sV.sem, 1)
                wait(dve, sV, p, "rinv")
                w = 256 if g is None else 160
                V_.tensor_scalar(sprob[:, 0:w], sprob[:, 0:w], ast[:, 37:38], None, ALU.mult).then_inc(sV.sem, 1)
                wait(dve, sT, p, "pt")
                if g is None:
                    V_.tensor_copy(sprobT, ps[:, 1, 0:256].rearrange("p (c r) -> p c r", c=2)).then_inc(sV.sem, 1)
                else:
                    V_.tensor_copy(sprobT[:, 0, :], ps[:, 1, 0:P])
                    V_.tensor_copy(sprobT[0:TS, 1, :], ps[0:TS, 1, P:2 * P]).then_inc(sV.sem, 1)
                wait(dve, sT, p, "pv")
                for h2 in range(2):
                    r = slice(64 * h2, 64 * h2 + 64)
                    V_.tensor_copy(qh[r, :, SEQ:T].rearrange("p a (b q) -> p a b q", q=TQ),
                                   ps[r, 2, 0:P].rearrange("p (a b z q) -> p a b z q", a=2, b=NB, z=2)[:, :, :, h2, :]
                                   ).then_inc(sV.sem, 1)

            def pair(p, u0, g, gain):
                for half in range(2):
                    head_norm(u0 + half, qh[:, half, :], gain)
                wait(dve, qV, u0 + 1, "n")
                for half in range(2):
                    for h2 in range(2):
                        head = 3 * (2 * half + h2) + g if g is not None else None
                        for q in range(2):
                            prompt_attn(8 * p + 4 * half + 2 * h2 + q, half, h2, q, head)
                sample_attn(p, g)
                wait(dve, oA, p, "hi")
                tt(mm[1], qh, mm[0].bitcast(F32), ALU.subtract).then_inc(oV.sem, 1)

            def hgrn_head(h):
                if h == 0:
                    wait(dve, oV, 0, "lo")
                    dve.wait_ge(stored, 16 * 2)
                    V_.memset(ones[:, :], 1.0)
                    V_.memset(att[:, :], 0.0).then_inc(init, 1)
                    dve.wait_ge(init, INIT + 1)
                inc = hV.sem
                wait(dve, hA, h, "sq")
                stt(three(Q[:, :]), fm(0), float(P) ** -0.5, three(tA[:, :])).then_inc(inc, 1)
                wait(dve, hA, h, "k")
                V_.tensor_scalar(E[:, 0:T], E[:, 0:T], col(S_ML + h), col(S_L + h), ALU.mult, ALU.add).then_inc(inc, 1)
                V_.tensor_scalar(K[:, :], K[:, :], col(S_ML + h), None, ALU.mult).then_inc(inc, 1)
                wait(dve, hA, h, "sg")
                tt(three(G[:, :]), fm(0), three(tA[:, :])).then_inc(inc, 1)
                wait(dve, hT_, h, "v")
                V_.tensor_copy(V[:, 0:8, :], ps[:, 3:5, :].rearrange("p b (i c) -> p (b i) c", i=4))
                V_.tensor_copy(V[0:TS, 8, :], ps[0:TS, 5, 0:P]).then_inc(inc, 1)
                wait(dve, hV, h, "v")
                tt(VM[0:TS, :].rearrange("p (b v) -> p b v", b=NB), V[0:TS, 8, :].unsqueeze(1).to_broadcast([TS, NB, P]),
                   cst[0:TS, C_VM:C_VM + NB].unsqueeze(2).to_broadcast([TS, NB, P])).then_inc(inc, 1)
                wait(dve, hT_, h, "diag")
                idm = ident.bitcast(I32)
                V_.copy_predicated(att[:, 0:SEQ].rearrange("p (i t) -> p i t", i=NPT),
                                   idm.unsqueeze(1).to_broadcast([P, NPT, P]),
                                   ps[:, 6:8, :].rearrange("p b (i t) -> p (b i) t", i=4))
                V_.copy_predicated(att[0:TS, SEQ:T], idm[0:TS, 0:TS], ps[0:TS, 0, 0:TS]).then_inc(inc, 1)
                tt(Q[:, :], Q[:, :], E[:, 0:T]).then_inc(inc, 1)
                for l in range(LEVELS):
                    w = 1 << l
                    n = T if l < 2 else SEQ
                    wait(dve, hT_, h, f"l{l}")
                    mask = cst[:, C_LVL + 64 * l:C_LVL + 64 * l + 64].bitcast(I32)
                    av = att[:, 0:SEQ].rearrange("p (i b z w) -> p i b z w", i=NPT, z=2, w=w)[:, :, :, 1, :]
                    ins = V_.copy_predicated(
                        av, mask.rearrange("p (b w) -> p b w", w=w).unsqueeze(1).to_broadcast([P, NPT, 64 // w, w]),
                        ps[:, 6 + l % 2, :].rearrange("p (i b w) -> p i b w", i=NPT, w=w))
                    if l < 2:
                        ins = V_.copy_predicated(
                            att[0:TS, SEQ:T].rearrange("p (b z w) -> p b z w", z=2, w=w)[:, :, 1, :],
                            mask[0:TS, 0:16].rearrange("p (b w) -> p b w", w=w),
                            ps[0:TS, 0, 32 + 16 * l:48 + 16 * l].rearrange("p (b w) -> p b w", w=w))
                    ins.then_inc(inc, 1)
                    if l:
                        wait(dve, hP, h, f"e{l - 1}")
                    wait(dve, hV, h, "qf" if l == 0 else f"q{l - 1}")
                    Qv = Q[:, 0:n].rearrange("p (b z w) -> p b z w", z=2, w=w)[:, :, 1, :]
                    Ee = E[:, EOFF[l]:EOFF[l] + n // w].rearrange("p (b z) -> p b z", z=2)[:, :, 0]
                    tt(Qv, Qv, Ee.unsqueeze(2).to_broadcast([P, n // (2 * w), w])).then_inc(inc, 1)
                wait(dve, hT_, h, "ds")
                wait(dve, hP, h, f"e{LEVELS - 1}")
                if h:
                    dve.wait_ge(stored, 16 * (2 + 2 * h))
                for i in range(NPT):
                    ds = ps[:, 6 + i // 4, P * (i % 4):P * (i % 4) + P]
                    if i == 0:
                        V_.tensor_copy(S[:, 0, :], ds).then_inc(inc, 1)
                    else:
                        wait(dve, hV, h, f"s{i - 1}")
                        stt(S[:, i, :], S[:, i - 1, :], E[:, EOFF[LEVELS] + i:EOFF[LEVELS] + i + 1], ds,
                            ALU.mult, ALU.add).then_inc(inc, 1)
                dve.wait_ge(side_in, 16 * (4 + h + 1))
                sv = SN[:, :].rearrange("p (b v) -> p b v", b=NB)
                tt(sv, S0[:, :].rearrange("p (b v) -> p b v", b=NB),
                   E[:, EOFF[2] + SEQ // 4:EOFF[2] + T // 4].unsqueeze(2).to_broadcast([P, NB, P])).then_inc(inc, 1)
                wait(dve, hV, h, "sn")
                tt(SN[:, :].rearrange("p (b v) -> p b v", b=2), SN[:, :].rearrange("p (b v) -> p b v", b=2),
                   ps[:, 1:3, :], ALU.add).then_inc(inc, 1)
                wait(dve, hA, h, "std")
                V_.reciprocal(R[:, :], R[:, :]).then_inc(inc, 1)
                wait(dve, hV, h, "rstd")
                tt(O2[:, 0:SEQ].rearrange("p (b n) -> p b n", b=2), ps[:, 3:5, :],
                   R[:, 0:SEQ].rearrange("p (b n) -> p b n", b=2))
                tt(O2[:, SEQ:T], ps[:, 5, 0:TS], R[:, SEQ:T]).then_inc(inc, 1)
                wait(dve, hV, h, "o")
                stt(tA[:, :], O2[:, :], col(S_GN + h), G[:, :]).then_inc(inc, 1)
                wait(dve, hA, h, "hi")
                tt(mm[1][:, 0, :], tA[:, :], mm[0][:, 0, :].bitcast(F32), ALU.subtract).then_inc(inc, 1)
                if h < HEADS - 1:
                    adds(OUT0[0] + 1 + h)

            def ffn(L):
                def chunk(r, par_, G0):
                    if G0 is not None:
                        for i in range(NT):
                            for n in range(2):
                                add_group(G0 + 2 * i + n, i, n)
                    wait(dve, fT, r, "u")
                    wait(dve, fA, r, "silu")
                    tt(three(gated[:, :]), fm(3), three(sg[:, :])).then_inc(fV.sem, 1)
                    wait(dve, fA, r, "hi")
                    tt(mm[1][:, par_, :], gated[:, :], mm[0][:, par_, :].bitcast(F32),
                       ALU.subtract).then_inc(fV.sem, 1)

                norms(NORM_FFN[L], S_FFN + KT * L, o=FOUT0[L] - 1)
                chunk(NCH * L, 0, None)
                with dve.Fori(0, (NCH - 2) // 2) as it:
                    for z in range(2):
                        chunk(2 * it + 1 + z + NCH * L, 1 - z, OUTG * 2 * it + OUTG * (z + FOUT0[L]))
                chunk(NCH * L + NCH - 1, 1, OUTG * (FOUT0[L] + NCH - 2))

            def setup():
                n = [0]

                def done(ins):
                    n[0] += 1
                    ins.then_inc(init, 1)
                    return n[0]

                V_.memset(col(S_EPS), EPS)
                dve.wait_ge(small_in, 32)
                lb, ml, rawl = col(S_L, HEADS), col(S_ML, HEADS), col(S_LB, HEADS)
                V_.tensor_scalar(col(S_GQ, 1), col(S_SQ, 1), HD ** -0.5, None, ALU.mult)
                V_.tensor_scalar(col(S_GQ + 1, 2), col(S_MQ, 2), HD ** -0.5, None, ALU.mult)
                k = done(tt(lb, rawl, rawl, ALU.subtract))
                dve.wait_ge(lb_exp, 1)
                k = done(V_.reciprocal(ml, lb))
                dve.wait_ge(init, k)
                k = done(tt(lb, lb, ml))
                dve.wait_ge(init, k)
                k = done(tt(ml, lb, lb, ALU.subtract))
                dve.wait_ge(init, k)
                k = done(V_.tensor_scalar(lb, ml, 0.0, 0.999, ALU.max, ALU.min))
                dve.wait_ge(init, k)
                k = done(V_.tensor_scalar(ml, lb, -1.0, 1.0, ALU.mult, ALU.add))
                dve.wait_ge(init, k)
                assert k == INIT

            setup()
            for L in range(2):
                if L == 0:
                    dve.wait_ge(x_in, 16 * NT)
                norms(NORM_MIX[L], S_MIX + KT * L, S_MEM + KT * L, o=None if L == 0 else FOUT0[0] + NCH - 1)
                wait(dve, mA, L, "std")
                V_.reciprocal(probT[:, 0:512], probT[:, 0:512]).then_inc(mV.sem, 1)
                wait(dve, mV, L, "rstd")
                stt(kmem.rearrange("p a m -> p (a m)"), ps[:, 0, :], col(S_MK + L), probT[:, 0:512]).then_inc(mV.sem, 1)
                V_.tensor_copy(vmem.rearrange("p i c -> p (i c)"), ps[:, 1, :]).then_inc(mV.sem, 1)
                wait(dve, mT, L, "rows")
                V_.tensor_copy(ktok_mem.rearrange("p i c -> p (i c)"), ps[:, 3, :]).then_inc(mV.sem, 1)
                pair(L, [0, 2][L], None, col(S_GQ + 1 + L))
                adds(OUT0[L])
                if L == 0:
                    for h in range(HEADS):
                        hgrn_head(h)
                else:
                    dve.wait_ge(stored, 16 * (NS0 + 2))
                    V_.memset(kpad[:, :, 0:WIN], 0.0).then_inc(kV.sem, 1)
                    for half in range(2):
                        head_norm(4 + half, kpad[:, half, WIN:WIN + T], col(S_SK))
                    wait(dve, kT, 0, "v")
                    V_.tensor_copy(vwin[:, 0:8, :], ps[:, 0:4, :].rearrange("p b (i c) -> p (b i) c", i=2))
                    V_.tensor_copy(vwin[0:TS, 8, :], ps[0:TS, 4, 0:256]).then_inc(kV.sem, 1)
                    wait(dve, kT, 0, "rows")
                    V_.tensor_copy(ktok[:, 0, :], ps[:, 5, 0:256])
                    V_.tensor_copy(ktok[0:TS, 1, :], ps[0:TS, 5, 256:512]).then_inc(kV.sem, 1)
                    for g in range(QG):
                        pair(2 + g, 6 + 2 * g, g, col(S_GQ))
                        if g < QG - 1:
                            adds(OUT0[1] + 1 + g)
                ffn(L)
            adds(FOUT0[1] + NCH - 1)

        @block.tensor
        def _(pe):
            mmul = nc.tensor.matmul
            PASS = ((0, 0), (0, 1), (1, 0))

            def feat_mm(s, b0, m):
                k, (a, b), g = m // 9, PASS[m % 9 // 3], m % 3
                return mmul(ps[:, b0 + g, 0:TW], slot(a, s)[:, P * k:P * k + P], hT[b][:, k, TW * g:TW * g + TW],
                            start=m < 3, stop=m >= 69)

            def feat(j, s, b0, steps, n, name):
                pe.wait_ge(w_lo, j + 1)
                for m in range(71):
                    feat_mm(s, b0, m)
                feat_mm(s, b0, 71).then_inc(w_used, 1)
                pe.wait_ge(w_used, j + 1)
                pe.sem_inc(steps.sem, 1)

            def row_major(j, s, act, tiles, place):
                pe.wait_ge(w_lo, j + 1)
                for i, m in tiles:
                    for k in range(KT):
                        for q, (a, b) in enumerate(PASS):
                            ins = mmul(place(i, m), act[b][:, k, P * i:P * i + m], slot(a, s)[:, P * k:P * k + P],
                                       start=k == 0 and q == 0, stop=k == KT - 1 and q == 2)
                ins.then_inc(w_used, 1)

            def out_group(G, i, n, srcs):
                if not isinstance(G, int) or G >= 2:
                    pe.wait_ge(x_added, G - 1)
                steps = [(p, s, a, b) for p, s in srcs for a, b in PASS]
                for q, (p, s, a, b) in enumerate(steps):
                    ins = mmul(ps[0:rows(i), 6 + n, :], mm[b][:, p, P * i:P * i + rows(i)],
                               slot(a, s)[:, 512 * n:512 * n + 512], start=q == 0, stop=q == len(steps) - 1)
                return ins.then_inc(out_ready, 1)

            def outs(o, j, srcs, after=None):
                pe.wait_ge(w_lo, j + len(srcs))
                for i in range(NT):
                    for n in range(2):
                        out_group(o * OUTG + 2 * i + n, i, n, srcs)
                    if after:
                        after(i)
                pe.wait_ge(out_ready, (o + 1) * OUTG)
                pe.sem_inc(w_used, len(srcs))

            def transposes(r, i):
                m = rows(i) if i < NT else P
                wait(pe, nV, r, "xn")
                if r >= 2:
                    wait(pe, nG, r - 2, "g1")
                for k in range(KT):
                    ins = nc.tensor.transpose(ps[:, 2 * (r % 2) + k // 4, m * (k % 4):m * (k % 4) + m],
                                              xn[0:m, r % 2, P * k:P * k + P], ident[0:m, 0:m])
                ins.then_inc(nT.sem, 1)

            def norms(r0, mem=False, out=None):
                n = NT + (2 if mem else 0)

                def after(i):
                    if i >= 2:
                        transposes(r0 + i - 2, i - 2)

                if out:
                    outs(*out, after=after)
                for i in range(NT if out else 2, n + 2):
                    after(i)
                wait(pe, nP, r0 + n - 1, "lo")

            def head_norm(u, j, s):
                feat(j, s, 0, qT, u, "proj")
                wait(pe, qA, u, "sq")
                for g in range(TG):
                    ins = mmul(ps[:, 3 + g, 0:TW], cst[:, C_BLK:C_BLK + P], prob[:, TW * g:TW * g + TW],
                               start=True, stop=True)
                ins.then_inc(qT.sem, 1)
                wait(pe, qV, u, "n")

            def prompt_attn(r, half, h2, q, window):
                hs = slice(64 * h2, 64 * h2 + 64)
                for i in range(4):
                    t = 4 * q + i
                    rhs = kpad[hs, half, P * t:P * t + 256] if window else kmem[hs, half, :]
                    ins = mmul(ps[:, i // 2, 256 * (i % 2):256 * (i % 2) + 256], qh[hs, half, P * t:P * t + P], rhs,
                               start=True, stop=True)
                ins.then_inc(aT.sem, 1)
                wait(pe, aV, r, "p")
                for i in range(4):
                    for c in range(2):
                        ins = nc.tensor.transpose(ps[:, 4 + c, P * i:P * i + P],
                                                  prob[:, 256 * i + P * c:256 * i + P * c + P], ident)
                ins.then_inc(aT.sem, 1)
                wait(pe, aV, r, "pt")
                wait(pe, aA, r, "pt")
                for i in range(4):
                    t = 4 * q + i
                    cs = [c for c in range(2) if not window or t + c > 0]
                    for c in cs:
                        head_cols = slice(P * half + 64 * h2, P * half + 64 * h2 + 64)
                        lhsT = vwin[:, t - 1 + c, head_cols] if window else vmem[:, c, head_cols]
                        ins = mmul(ps[hs, 2, P * i:P * i + P], lhsT, probT[:, 512 * c + P * i:512 * c + P * i + P],
                                   start=c == cs[0], stop=c == 1)
                ins.then_inc(aT.sem, 1)
                wait(pe, aV, r, "o")

            def sample_attn(p, window):
                n = 1 if window else 2
                pe.wait_ge(side_in, 16 * [2, 12, 16, 16, 16][p])
                wait(pe, sV, p, "qb")

                def scores(b):
                    wait(pe, sA, p, f"kt{b}")
                    grp, e = b // 2, b % 2
                    out = slice(32 * grp, 32 * grp + 32)
                    for half in range(2):
                        mmul(ps[out, 0, 0:P * n], qblk[:, half, b, :], kcT[:, b % 2, P * n * half:P * n * (half + 1)],
                             start=e == 0 and half == 0, stop=e == 1 and half == 1)
                    if window and e:
                        for z, bb in enumerate((b - 1, b)):
                            for half in range(2):
                                mmul(ps[out, 0, P:P + TS], qblk[:, half, bb, :], kpad[:, half, WIN + SEQ:WIN + T],
                                     start=z == 0 and half == 0, stop=z == 1 and half == 1)

                for b in range(NB):
                    if b >= 2:
                        wait(pe, sA, p, f"kt{b - 2}")
                    for half in range(2):
                        for i in range(n):
                            c0 = (b * n + i) * 256 + P * half
                            o0 = P * n * half + P * i
                            ins = nc.tensor.transpose(ps[:, 6 + b % 2, o0:o0 + P], cacheb[:, c0:c0 + P], ident)
                    ins.then_inc(sT.sem, 1)
                    if b:
                        scores(b - 1)
                scores(NB - 1)
                pe.drain().then_inc(sT.sem, 1)
                wait(pe, sV, p, "p")
                nc.tensor.transpose(ps[:, 1, 0:P], sprob[:, 0:P], ident)
                w = TS if window else P
                nc.tensor.transpose(ps[0:w, 1, P:2 * P], sprob[:, P:P + w], ident).then_inc(sT.sem, 1)
                wait(pe, sV, p, "pt")
                if not window:
                    pe.wait_ge(side_in, 16 * [4, 14][p])
                for half in range(2):
                    for b in range(NB):
                        r0 = 16 * b + 8 * half
                        out = ps[:, 2, 64 * half + 8 * b:64 * half + 8 * b + 8]
                        for c in range(2):
                            if window:
                                lhsT = vwin[0:TS, NPT, P * half:P * half + P] if c else \
                                    cacheb[:, 2048 + 256 * b + P * half:2048 + 256 * b + P * half + P]
                            else:
                                c0 = (2 * b + c) * 256 + P * half
                                lhsT = cacheb[:, c0:c0 + P]
                            k = TS if window and c else P
                            ins = mmul(out, lhsT, sprobT[0:k, c, r0:r0 + 8], start=c == 0, stop=c == 1)
                ins.then_inc(sT.sem, 1)

            def pair(p, u0, j, window):
                for half in range(2):
                    head_norm(u0 + half, j + half, (j - MIX0[1 if p else 0] + half) % 2)
                for half in range(2):
                    for h2 in range(2):
                        for q in range(2):
                            prompt_attn(8 * p + 4 * half + 2 * h2 + q, half, h2, q, window)
                sample_attn(p, window)
                wait(pe, oV, p, "lo")

            def hgrn_head(h, j):
                inc = hT_.sem
                n0 = j - MIX0[0]
                feat(j, n0 % 2, 0, hT_, h, "q")
                feat(j + 1, (n0 + 1) % 2, 3, hT_, h, "z")
                wait(pe, hV, h, "q")
                feat(j + 2, n0 % 2, 0, hT_, h, "g")
                wait(pe, hA, h, "k")
                row_major(j + 3, (n0 + 1) % 2, hT, [(i, rows(i)) for i in range(NT)],
                          lambda i, m: ps[0:m, 3 + i // 4, P * (i % 4):P * (i % 4) + P])
                pe.wait_ge(w_used, j + 4)
                pe.sem_inc(inc, 1)
                wait(pe, hV, h, "g")
                for i in range(NPT):
                    mmul(ps[:, 6 + i // 4, P * (i % 4):P * (i % 4) + P], K[:, P * i:P * i + P], Q[:, P * i:P * i + P],
                         start=True, stop=True)
                mmul(ps[0:TS, 0, 0:TS], K[:, SEQ:T], Q[:, SEQ:T], start=True, stop=True).then_inc(inc, 1)
                for l in range(LEVELS):
                    w = 1 << l
                    wait(pe, hV, h, "qf" if l == 0 else f"q{l - 1}")
                    if l:
                        wait(pe, hP, h, f"k{l - 1}")
                    for i in range(NPT):
                        qv = Q[:, P * i:P * i + P].rearrange("p (b z w) -> p b z w", z=2, w=w)[:, :, 1, :]
                        ins = mmul(ps[:, 6 + l % 2, 64 * i:64 * i + 64].rearrange("p (b w) -> p b w", w=w),
                                   K[:, P * i:P * i + P], qv, start=True, stop=True)
                    if l < 2:
                        qv = Q[:, SEQ:T].rearrange("p (b z w) -> p b z w", z=2, w=w)[:, :, 1, :]
                        ins = mmul(ps[0:TS, 0, 32 + 16 * l:48 + 16 * l].rearrange("p (b w) -> p b w", w=w),
                                   K[:, SEQ:T], qv, start=True, stop=True)
                    ins.then_inc(inc, 1)
                wait(pe, hV, h, f"q{LEVELS - 1}")
                wait(pe, hP, h, f"k{LEVELS - 1}")
                for i in range(NPT):
                    nc.tensor.transpose(ps[:, 6 + i // 4, P * (i % 4):P * (i % 4) + P], K[:, P * i:P * i + P], ident)
                nc.tensor.transpose(ps[0:TS, 0, 0:P], K[:, SEQ:T], ident).then_inc(inc, 1)
                wait(pe, hA, h, "kr")
                for i in range(NPT):
                    mmul(ps[:, 6 + i // 4, P * (i % 4):P * (i % 4) + P], KR[:, i, :], V[:, i, :], start=True, stop=True)
                for z in range(2):
                    ins = mmul(ps[:, 1 + z, :], KR[0:TS, 8, :], VM[0:TS, 512 * z:512 * z + 512], start=True, stop=True)
                ins.then_inc(inc, 1)
                wait(pe, hV, h, "sd")
                for i in range(NPT):
                    out = ps[:, 3 + i // 4, P * (i % 4):P * (i % 4) + P]
                    mmul(out, V[:, i, :], att[:, P * i:P * i + P], start=True, stop=i == 0)
                    if i:
                        mmul(out, S[:, i - 1, :], Q[:, P * i:P * i + P], start=False, stop=True)
                mmul(ps[:, 5, 0:TS], V[0:TS, 8, :], att[0:TS, SEQ:T], start=True, stop=False, skip_group_check=True)
                for b in range(NB):
                    ins = mmul(ps[:, 5, TQ * b:TQ * b + TQ], S0[:, P * b:P * b + P], Q[:, SEQ + TQ * b:SEQ + TQ * b + TQ],
                               start=False, stop=b == NB - 1, skip_group_check=True)
                ins.then_inc(inc, 1)
                wait(pe, hA, h, "o2")
                for g in range(TG):
                    ins = mmul(ps[:, g, 0:TW], ones[:, :], O2[:, TW * g:TW * g + TW], start=True, stop=True)
                ins.then_inc(inc, 1)
                wait(pe, hV, h, "lo")

            def ffn(L, first_out):
                def chunk(r, c_par, jg, ju, slots, prev):
                    pe.wait_ge(w_lo, jg + 1)
                    if prev is not None or L:
                        wait(pe, fA, r - 1, "silu")
                    G0, so = prev if prev is not None else (None, None)
                    g = 0
                    for m in range(144):
                        if m == 72:
                            pe.wait_ge(w_lo, ju + 1)
                            if prev is not None or L:
                                wait(pe, fV, r - 1, "mul")
                        ins = feat_mm(slots[0], 0, m) if m < 72 else feat_mm(slots[2], 3, m - 72)
                        if m == 71:
                            ins.then_inc(fT.sem, 1)
                        if prev is not None and m >= 34 and (m - 34) % 6 == 0 and g < OUTG:
                            if g == 0:
                                pe.wait_ge(w_lo, jg + 2)
                                wait(pe, fV, r - 1, "lo")
                            out_group(G0 + g, g // 2, g % 2, [(1 - c_par, so)])
                            g += 1
                    assert prev is None or g == OUTG
                    ins.then_inc(fT.sem, 1)
                    wait(pe, fT, r, "u")
                    pe.sem_inc(w_used, 3 if prev is not None else 2)

                F0 = FFN0[L]
                norms(NORM_FFN[L], out=first_out)
                chunk(NCH * L, 0, F0, F0 + 1, EVEN, None)
                with pe.Fori(0, (NCH - 2) // 2) as it:
                    for z in range(2):
                        jg = 6 * it + (F0 + 2 + 3 * z)
                        slots = EVEN if z else ODD
                        chunk(2 * it + (1 + z + NCH * L), 1 - z, jg, jg + 2, slots,
                              (2 * OUTG * it + OUTG * (z + FOUT0[L]), slots[1]))
                jg = F0 + 3 * (NCH - 1) - 1
                chunk(NCH * L + NCH - 1, 1, jg, jg + 2, ODD, (OUTG * (FOUT0[L] + NCH - 2), ODD[1]))
                wait(pe, fV, NCH * L + NCH - 1, "lo")

            pe.wait_ge(small_in, 32)
            pe.wait_ge(init, 1)
            last_out = None
            for L in range(2):
                norms(NORM_MIX[L], mem=True, out=last_out)
                J = MIX0[L]
                pe.wait_ge(w_lo, J + 2)
                for h in range(2):
                    for k in range(KT):
                        for q, (a, b) in enumerate(PASS):
                            ins = mmul(ps[:, 0, N_MEM * h:N_MEM * (h + 1)], slot(a, h)[:, P * k:P * k + P],
                                       memT[b][:, k, :], start=k == 0 and q == 0, stop=k == KT - 1 and q == 2)
                    ins.then_inc(w_used, 1)
                pe.wait_ge(w_used, J + 2)
                pe.sem_inc(mT.sem, 1)
                for h in range(2):
                    row_major(J + 2 + h, h, memT, [(0, P), (1, P)],
                              lambda i, m: ps[:, 1, 256 * i + P * h:256 * i + P * h + P])
                pe.wait_ge(w_used, J + 4)
                pe.sem_inc(mT.sem, 1)
                wait(pe, mA, L, "sq")
                mmul(ps[:, 2, :], cst[:, C_BLK:C_BLK + P], prob[:, 0:512], start=True, stop=True).then_inc(mT.sem, 1)
                wait(pe, mV, L, "k")
                for i in range(2):
                    for h in range(2):
                        ins = nc.tensor.transpose(ps[:, 3, 256 * i + P * h:256 * i + P * h + P],
                                                  kmem[:, h, P * i:P * i + P], ident)
                ins.then_inc(mT.sem, 1)
                wait(pe, mV, L, "rows")
                J += MEM_JOBS
                pair(L, [0, 2][L], J, False)
                outs(OUT0[L], J + 2, [(0, 0), (1, 1)])
                pe.wait_ge(x_added, (OUT0[L] + 1) * OUTG)
                J += PAIR_JOBS
                if L == 0:
                    for h in range(HEADS):
                        hgrn_head(h, J)
                        o = (OUT0[0] + 1 + h, J + 4, [(0, (J + 4) % 2)])
                        if h < HEADS - 1:
                            outs(*o)
                            pe.wait_ge(x_added, (OUT0[L] + 2 + h) * OUTG)
                        J += HGRN_JOBS
                    ffn(L, o)
                else:
                    for half in range(2):
                        head_norm(4 + half, J + half, half)
                    for half in range(2):
                        row_major(J + 2 + half, half, hT, [(i, rows(i)) for i in range(NT)],
                                  lambda i, m: ps[0:m, i // 2, 256 * (i % 2) + P * half:256 * (i % 2) + P * half + P])
                    pe.wait_ge(w_used, J + 4)
                    pe.sem_inc(kT.sem, 1)
                    for h in range(2):
                        nc.tensor.transpose(ps[:, 5, P * h:P * h + P], kpad[:, h, SEQ:SEQ + P], ident)
                        ins = nc.tensor.transpose(ps[0:TS, 5, 256 + P * h:256 + P * h + P],
                                                  kpad[:, h, WIN + SEQ:WIN + T], ident)
                    ins.then_inc(kT.sem, 1)
                    wait(pe, kV, 0, "rows")
                    J += SWKV_JOBS
                    for g in range(QG):
                        pair(2 + g, 6 + 2 * g, J, True)
                        o = (OUT0[1] + 1 + g, J + 2, [(0, 0), (1, 1)])
                        if g < QG - 1:
                            outs(*o)
                            pe.wait_ge(x_added, (OUT0[L] + 2 + g) * OUTG)
                        J += PAIR_JOBS
                    ffn(L, o)
                last_out = (FOUT0[L] + NCH - 1, FFN0[L] + FFN_JOBS - 1, [(1, EVEN[0])])
            outs(*last_out)


_SHAPES = dict(
    y_prompt=(1, SEQ, D), y_sample=(NB, TQ, D), new_mem_k=(2, 1, N_MEM, 4, HD), new_mem_v=(2, 1, N_MEM, 4, HD),
    new_hg_p=(1, 1, HEADS, P, P), new_hg_s=(1, NB, HEADS, P, P), new_swk_p=(1, 1, WIN, 4, HD),
    new_swv_p=(1, 1, WIN, 4, HD), new_swk_s=(1, NB, WIN, 4, HD), new_swv_s=(1, NB, WIN, 4, HD))
_INS = ['x_prompt', 'x_sample', 'cache_mem_k', 'cache_mem_v', 'state_hgrn', 'cache_swa_k', 'cache_swa_v',
        'mem_prompt', 'w_in_hgrn', 'w_in_swa', 'w_mem_kv', 'w_out', 'w_ffn_in', 'w_ffn_out']


def _params(a):
    cols = [np.asarray(a[n]).reshape(2 * KT, P).T for n in ('norm_mix', 'norm_ffn', 'norm_mem')]
    cols += [np.asarray(a[n]).reshape(HEADS, P).T for n in ('hgrn_out_norm', 'hgrn_lb_raw')]
    cols += [np.tile(np.asarray(a[n]), (1, 2)).T for n in ('swa_q_norm', 'swa_k_norm', 'mem_q_norm', 'mem_k_norm')]
    sinks = np.asarray(a['swa_sinks']).reshape(1, 12)
    cols += [np.broadcast_to(sinks, (P, 12))]
    cols += [np.tile(np.repeat(sinks.reshape(4, QG), TQ, axis=0), (NB, 1))]
    return np.ascontiguousarray(np.concatenate(cols, axis=1))


def kernel(**inputs):
    import concourse.bacc as _bacc
    from concourse.bass_utils import run_bass_kernel_spmd as _run

    nc = _bacc.Bacc("TRN2", target_bir_lowering=False, num_devices=1,
                     dynamic_dma_scratch_size=1024)
    arrays, args = {}, []
    data = [(n, np.ascontiguousarray(inputs[n])) for n in _INS]
    data += [("constants", constants()), ("params", _params(inputs))]
    for name, a in data:
        arrays[f"in_{name}_dram"] = a
        args.append(nc.dram_tensor(f"in_{name}_dram", a.shape, mybir.dt.from_np(a.dtype), kind="ExternalInput").ap())
    for name, shape in _SHAPES.items():
        args.append(nc.dram_tensor(f"out_{name}_dram", shape, F32, kind="ExternalOutput").ap())
    hybrid_step(nc, *args)
    r = _run(nc, [arrays], core_ids=[0])
    return tuple(r.results[0][f"out_{name}_dram"] for name in _SHAPES)
```

```python
from contextlib import ExitStack

import numpy as np

import concourse.bass as bass
from concourse import mybir

F32 = mybir.dt.float32
F32R = mybir.dt.float32r
I32 = mybir.dt.int32
ACT = mybir.ActivationFunctionType
ALU = mybir.AluOpType
AX = mybir.AxisListType

P = 128
D = 1024
KT = D // P
SEQ, NB, TQ = 1024, 8, 4
TS = NB * TQ
T = SEQ + TS
NPT = SEQ // P
NT = NPT + 1
N_MEM, HD = 256, 64
HEADS = 6
TOK = HEADS * P
DFF = 2816
NCH = DFF // P
WIN = 128
EPS = 1e-6
NEG = -1e30
TG = 3
TW = T // TG
LEVELS = 7
QG = 3
NPAIR = 1 + 1 + QG

C_ID, C_BLK, C_LVL = 0, P, 2 * P
C_BAND = C_LVL + LEVELS * 64
C_SROW = C_BAND + 2 * 256
C_QB = C_SROW + 160
C_VM = C_QB + 2 * NB * 8
C_END = C_VM + NB

S_MIX, S_FFN, S_MEM = 0, 2 * KT, 4 * KT
S_GN = 6 * KT
S_LB = S_GN + HEADS
S_SQ, S_SK = S_LB + HEADS, S_LB + HEADS + 1
S_MQ, S_MK = S_SK + 1, S_SK + 3
S_SINK = S_MK + 2
S_SROW = S_SINK + 12
S_END = S_SROW + 3
S_L, S_ML, S_GQ = S_END, S_END + HEADS, S_END + 2 * HEADS
S_EPS = S_GQ + 3
S_ALL = S_EPS + 1


def constants():
    c = np.zeros((P, C_END), np.float32)
    p = np.arange(P)
    c[:, C_ID:C_ID + P] = np.eye(P)
    c[:, C_BLK:C_BLK + P] = (p[:, None] // HD == p[None] // HD)
    for l in range(LEVELS):
        w = 1 << l
        t = np.array([t for t in range(P) if (t // w) % 2 == 1])
        ok = (p[:, None] // (2 * w) == t[None] // (2 * w)) & ((p[:, None] // w) % 2 == 0)
        c[:, C_LVL + 64 * l:C_LVL + 64 * l + 64] = ok
    r = np.arange(2 * WIN)[None]
    band = (r > p[:, None]) & (r <= p[:, None] + WIN)
    c[:, C_BAND:C_BAND + 256] = np.where(band & (r >= WIN), 0, NEG)
    c[:, C_BAND + 256:C_BAND + 512] = np.where(band, 0, NEG)
    b, q = p[:, None] // 16, p[:, None] % 4
    r = np.arange(160)[None]
    old = (r < WIN) & (r > q)
    new = (r >= WIN) & ((r - WIN) // TQ == b) & ((r - WIN) % TQ <= q)
    c[:, C_SROW:C_SROW + 160] = np.where(old | new, 0, NEG)
    m = np.zeros((P, 2, NB, 2, 4), np.float32)
    for half in range(2):
        for bb in range(NB):
            for h2 in range(2):
                m[64 * h2:64 * h2 + 64, half, bb, bb % 2, 2 * half + h2] = 1
    c[:, C_QB:C_VM] = m.reshape(P, -1)
    c[:TS, C_VM:] = (np.arange(TS)[:, None] // TQ == np.arange(NB)[None])
    return c


class Steps:

    def __init__(self, sem, names):
        self.sem, self.names, self.len = sem, names, len(names)

    def at(self, n, name):
        return n * self.len + (self.names.index(name) + 1)


MEM_JOBS, PAIR_JOBS, HGRN_JOBS, SWKV_JOBS = 4, 4, 5, 4
MIX_JOBS = [MEM_JOBS + PAIR_JOBS + HGRN_JOBS * HEADS, MEM_JOBS + PAIR_JOBS + SWKV_JOBS + QG * PAIR_JOBS]
FFN_JOBS = 3 * NCH
MIX0 = [0, MIX_JOBS[0] + FFN_JOBS]
FFN0 = [MIX0[0] + MIX_JOBS[0], MIX0[1] + MIX_JOBS[1]]
JOBS = FFN0[1] + FFN_JOBS
ODD, EVEN = (0, 4, 1), (2, 5, 3)
NRAW = 3
OUTG = 2 * NT
J_MQ, J_FILL, J_MO, J_TOK = MEM_JOBS, MEM_JOBS + 2, MEM_JOBS + 4, MEM_JOBS + 6
MIX_OUTS = [1 + HEADS, 1 + QG]
OUT0 = [0, MIX_OUTS[0] + NCH]
FOUT0 = [MIX_OUTS[0], OUT0[1] + MIX_OUTS[1]]
NORM_MIX = [0, 2 * NT + 2]
NORM_FFN = [NT + 2, 3 * NT + 4]


INIT = 6
EOFF = [sum((T if l < 3 else SEQ) >> l for l in range(n)) for n in range(LEVELS + 1)]
NS0 = 2 + 2 * HEADS
NSTORE = NS0 + 2 + 2 + 2 * NB + 2


def rows(i):
    return P if i < NPT else TS


def hybrid_step(nc, x_prompt, x_sample, cache_mem_k, cache_mem_v, state_hgrn, cache_swa_k, cache_swa_v,
                mem_prompt, w_in_hgrn, w_in_swa, w_mem_kv, w_out, w_ffn_in, w_ffn_out, consts, params,
                y_prompt, y_sample, new_mem_k, new_mem_v, new_hg_p, new_hg_s,
                new_swk_p, new_swv_p, new_swk_s, new_swv_s):
    with ExitStack() as ctx:
        def sb(name, cols, dt=F32):
            return ctx.enter_context(nc.sbuf_tensor(name, [P, cols], dt))

        def sem(name):
            return ctx.enter_context(nc.semaphore(name))

        x = sb("x", NT * D)[:, :].rearrange("p (i d) -> p i d", i=NT)
        hT = [sb("hT_hi", KT * T, F32R)[:, :].rearrange("p (k t) -> p k t", k=KT),
              sb("hT_lo", KT * T, F32R)[:, :].rearrange("p (k t) -> p k t", k=KT)]
        raw = sb("w_raw", NRAW * D)[:, :].rearrange("p (s n) -> p s n", s=NRAW)
        w01 = [sb("w_hi01", 2 * D, F32R), sb("w_lo01", 2 * D, F32R)]
        mm = [sb("m_hi", 2 * T, F32R)[:, :].rearrange("p (a t) -> p a t", a=2),
              sb("m_lo", 2 * T, F32R)[:, :].rearrange("p (a t) -> p a t", a=2)]
        cst = sb("consts", C_END)
        par = sb("params", S_ALL)
        nstat = sb("norm_stats", 40)
        nrstd = sb("norm_rstd", 40)

        ARENA = 71328
        slab = ctx.enter_context(nc.sbuf_tensor("arena", [P, ARENA // 4], F32))
        base = nc.sbuf_base - ARENA

        def at(name, off, cols, dt=F32):
            assert off + 4 * cols <= ARENA, name
            return nc.alloc_sbuf_tensor_at(name, [P, cols], dt, offset=base + off)

        w25 = [at("w_hi25", 0, 4 * D, F32R), at("w_lo25", 16384, 4 * D, F32R)]
        sg = at("gate_silu", 32768, T)
        gated = at("gated", 36992, T)
        xn = at("normed", 41216, 2 * D)[:, :].rearrange("p (a d) -> p a d", a=2)
        gained = at("normed_gained", 49408, D)
        NORM_END = 53504
        xmem = at("mem_rows", NORM_END, 2 * D)[:, :].rearrange("p (i d) -> p i d", i=2)
        memT = [at("memT_hi", 0, KT * N_MEM, F32R)[:, :].rearrange("p (k t) -> p k t", k=KT),
                at("memT_lo", 8192, KT * N_MEM, F32R)[:, :].rearrange("p (k t) -> p k t", k=KT)]
        prob = at("prob", 16384, T)
        probT = at("probT", 20608, T)
        prob2 = at("prob2", 9472, T)
        orow = at("attn_rows", 13568, 4 * P)[:, :].rearrange("p (i c) -> p i c", i=4)
        st = at("attn_round_stats", 15616, 4 * 20)
        qh = at("q_heads", 24832, 2 * T)[:, :].rearrange("p (a t) -> p a t", a=2)
        kmem = at("k_mem", 33280, 2 * N_MEM)[:, :].rearrange("p (a m) -> p a m", a=2)
        vmem = at("v_mem", 35328, 2 * N_MEM)[:, :].rearrange("p (i c) -> p i c", i=2)
        ktok_mem = at("k_mem_rows", 0, 2 * N_MEM)[:, :].rearrange("p (i c) -> p i c", i=2)
        qblk = at("q_blocks", 37376, 2 * NB * 32)[:, :].rearrange("p (a b c) -> p a b c", a=2, b=NB)
        sprob = at("sample_prob", 39424, 256)
        sprobT = at("sample_probT", 40448, 256)[:, :].rearrange("p (c r) -> p c r", c=2)
        kcT = at("k_cacheT", 41472, 2 * 512)[:, :].rearrange("p (z n) -> p z n", z=2)
        ast = at("attn_stats", 45568, 40)
        cacheb = at("cache", 45728, NB * 512)
        kpad = at("k_window", 0, 2 * (P + T))[:, :].rearrange("p (a t) -> p a t", a=2)
        vwin = at("v_window", 62112, NT * 256)[:, :].rearrange("p (i c) -> p i c", i=NT)
        ktok = at("k_window_rows", 33280, 2 * 256)[:, :].rearrange("p (i c) -> p i c", i=2)
        Q = at("hg_q", 0, T)
        K = at("hg_k", 4224, T)
        E = at("hg_decay", 8448, 2096)
        tA = at("hg_sig", 16832, T)
        G = at("hg_gate", 21056, T)
        V = at("hg_v", 25280, NT * P)[:, :].rearrange("p (i c) -> p i c", i=NT)
        att = at("hg_att", 29888, T)
        KR = at("hg_k_rows", 34112, NT * P)[:, :].rearrange("p (i c) -> p i c", i=NT)
        O2 = at("hg_o_square", 38720, T)
        R = at("hg_rstd", 42944, T)
        VM = at("hg_v_blocks", 47168, NB * P)
        ones = at("ones", 51264, P)
        S = at("hg_states", NORM_END, NPT * P)[:, :].rearrange("p (i c) -> p i c", i=NPT)
        S0 = at("hg_state_in", NORM_END + 4096, NB * P)
        SN = at("hg_state_out", NORM_END + 8192, NB * P)

        ps = ctx.enter_context(nc.psum_tensor("ps", [P, 8, 512], F32))

        raw_loaded = [sem(f"raw_loaded{s}") for s in range(NRAW)]
        w_hi, w_lo, w_used = sem("w_hi"), sem("w_lo"), sem("w_used")
        small_in, x_in, mem_in, side_in = sem("small_in"), sem("x_in"), sem("mem_in"), sem("side_in")
        stored, stored_y = sem("stored"), sem("stored_y")
        out_ready, x_added = sem("out_ready"), sem("x_added")
        init, lb_exp = sem("init"), sem("lb_exp")
        nA, nH = Steps(sem("norm_stats_act"), ["sq", "std"]), Steps(sem("norm_hi"), ["hi"])
        nV, nG = Steps(sem("norm_rows_vec"), ["rstd", "xn"]), Steps(sem("norm_gain_vec"), ["g0", "g1"])
        nT, nP = Steps(sem("norm_pe"), ["tr"]), Steps(sem("norm_pool"), ["lo"])
        fT, fA, fV = (Steps(sem("ffn_pe"), ["g", "u"]), Steps(sem("ffn_act"), ["silu", "hi"]),
                      Steps(sem("ffn_vec"), ["mul", "lo"]))
        mT = Steps(sem("memkv_pe"), ["k", "v", "ssq", "rows"])
        mA = Steps(sem("memkv_act"), ["sq", "std"])
        mV = Steps(sem("memkv_vec"), ["rstd", "k", "v", "rows"])
        qT, qA, qV = (Steps(sem("headnorm_pe"), ["proj0", "proj1", "ssq0", "ssq1"]),
                      Steps(sem("headnorm_act"), ["sq0", "sq1", "std0", "std1"]),
                      Steps(sem("headnorm_vec"), ["rstd0", "n0", "rstd1", "n1"]))
        aSC, aPT, aPV, aOT = (Steps(sem("scores_pe"), ["sc"]), Steps(sem("probT_pe"), ["pt"]),
                              Steps(sem("attn_rows_pe"), ["pv"]), Steps(sem("attn_turn_pe"), ["ot"]))
        aE, aSK, aC = (Steps(sem("exp_act"), ["exp"]), Steps(sem("sink_act"), ["sink"]),
                       Steps(sem("probT_act"), ["pt"]))
        vM, vD, vR, vC, vO, vOT = (Steps(sem("max_vec"), ["max", "neg"]), Steps(sem("den_vec"), ["den"]),
                                   Steps(sem("rinv_vec"), ["rinv"]), Steps(sem("probT_vec"), ["pt"]),
                                   Steps(sem("attn_rows_vec"), ["o"]), Steps(sem("attn_turn_vec"), ["ot"]))
        sT = Steps(sem("sample_pe"), [f"kt{b}" for b in range(NB)] + ["sc", "pt", "pv"])
        sA = Steps(sem("sample_act"), [f"kt{b}" for b in range(NB)] + ["exp", "sink"])
        sV = Steps(sem("sample_vec"), ["qb", "max", "neg", "den", "rinv", "p", "pt", "o0", "o1"])
        oA, oV = Steps(sem("pair_out_act"), ["hi"]), Steps(sem("pair_out_vec"), ["lo"])
        kT, kV = Steps(sem("window_pe"), ["v", "rows"]), Steps(sem("window_vec"), ["pad", "v", "rows"])
        hQ, hZ = Steps(sem("hgrn_query_pe"), ["q"]), Steps(sem("hgrn_forget_pe"), ["z"])
        hT_ = Steps(sem("hgrn_pe"), ["diag", "l0", "l1", "l2", "g", "l3", "l4", "l5", "l6", "v",
                                     "kr", "ds", "ds8", "o", "ssq"])
        hA = Steps(sem("hgrn_act"), ["sq", "f", "k", "e", "ks", "sg", "kr", "o2", "std", "hi"])
        hV = Steps(sem("hgrn_vec"), ["q", "diag", "qf"]
                   + [f"{s}{l}" for l in range(LEVELS) for s in "aq"] + ["g", "v", "vm"]
                   + [f"s{i}" for i in range(NPT)] + ["sn", "sd", "rstd", "o", "m", "lo"])
        hP = Steps(sem("hgrn_pool"), [f"{s}{l}" for l in range(LEVELS) for s in "ke"])
        block = ctx.enter_context(nc.Block())

        ident = cst[:, C_ID:C_ID + P]

        def col(c, n=1):
            return par[:, c:c + n]

        def slot(which, s):
            t = w01[which][:, s * D:(s + 1) * D] if s < 2 else w25[which][:, (s - 2) * D:(s - 1) * D]
            return t

        def wait(eng, steps, n, name):
            eng.wait_ge(steps.sem, steps.at(n, name))

        def fm(b0, n=TW):
            return ps[:, b0:b0 + TG, 0:n]

        def three(t):
            return t.rearrange("p (g n) -> p g n", g=TG)

        def w_cols(w, c0, s):
            v, dst = w.rearrange("(k p) n -> p k n", p=P), raw[:, s, :].rearrange("p (k n) -> p k n", k=KT)
            return [(dst[:, 0:4], v[:, 0:4, c0:c0 + P]), (dst[:, 4:8], v[:, 4:8, c0:c0 + P])]

        def w_two_heads(w, ha, hb, s):
            v, dst = w.rearrange("(k p) n -> p k n", p=P), raw[:, s, :].rearrange("p (k n) -> p k n", k=KT)
            return [(dst[:, :, 64 * z:64 * z + 64], v[:, :, 64 * h:64 * h + 64]) for z, h in enumerate((ha, hb))]

        def w_rows(w, ra, rb, s):
            return [(raw[0:64, s, :], w[ra:ra + 64]), (raw[64:P, s, :], w[rb:rb + 64])]

        def mixer_jobs(L):
            wm = w_mem_kv[L]
            jobs = [lambda s, c=c: w_cols(wm, c * P, s) for c in range(4)]
            win, c0 = (w_in_hgrn[0], 4 * TOK) if L == 0 else (w_in_swa[0], 5 * 256)
            jobs += [lambda s, h=h: w_cols(win, c0 + h * P, s) for h in range(2)]
            mem_out = [lambda s, h=h: w_rows(w_out[L], TOK + h * P, TOK + h * P + 64, s) for h in range(2)]
            if L == 0:
                cols = lambda kind, h: [lambda s: w_cols(win, "qfvg".index(kind) * TOK + h * P, s)]
                jobs += cols("f", 0) + cols("q", 0) + mem_out
                for h in range(HEADS):
                    jobs += cols("g", h) + cols("v", h)
                    if h < HEADS - 1:
                        jobs += cols("q", h + 1) + cols("f", h + 1)
                    jobs += [lambda s, h=h: w_rows(w_out[L], h * P, h * P + 64, s)]
            else:
                heads = [[(3 * 2 * half + g, 3 * (2 * half + 1) + g) for half in range(2)] for g in range(QG)]
                queries = lambda g: [lambda s, hh=hh: w_two_heads(win, hh[0], hh[1], s) for hh in heads[g]]
                jobs += [lambda s, c=c: w_cols(win, TOK + c * P, s) for c in range(2)] + mem_out
                jobs += [lambda s, c=c: w_cols(win, TOK + c * P, s) for c in range(2, 4)] + queries(0)
                for g in range(QG):
                    if g < QG - 1:
                        jobs += queries(g + 1)
                    jobs += [lambda s, hh=hh: w_rows(w_out[L], 64 * hh[0], 64 * hh[1], s) for hh in heads[g]]
            assert len(jobs) == MIX_JOBS[L]
            return jobs

        def ffn_job(L, kind, c, s):
            if kind == "o":
                w = w_ffn_out[L]
                return [(raw[64 * z:64 * z + 64, s, :], w[bass.ds(c * P + 64 * z, 64)]) for z in range(2)]
            v = w_ffn_in[L].rearrange("(k p) n -> p k n", p=P)
            dst = raw[:, s, :].rearrange("p (k n) -> p k n", k=KT)
            c0 = c * P + (DFF if kind == "u" else 0)
            return [(dst[:, 4 * z:4 * z + 4], v[:, 4 * z:4 * z + 4, bass.ds(c0, P)]) for z in range(2)]

        @block.sync
        def _(sp):
            def load(j3, n3, jv, parts):
                if not (isinstance(jv, int) and jv < NRAW):
                    sp.wait_ge(w_hi, jv - 2)
                    sp.wait_ge(w_lo, jv - 2)
                for dst, src in parts(j3):
                    sp.dma_start(dst, src).then_inc(raw_loaded[j3], 16)

            def store(dst, src):
                sp.dma_start(dst, src).then_inc(stored, 16)

            def cache_rows(c, L, n):
                return c[L].rearrange("b (i p) h d -> p b i (h d)", p=P)

            sp.dma_start(cst[:, :], consts).then_inc(small_in, 16)
            sp.dma_start(par[:, 0:S_END], params).then_inc(small_in, 16)
            for i in range(NPT):
                sp.dma_start(x[:, i, :], x_prompt[0, i * P:(i + 1) * P, :]).then_inc(x_in, 16)
            sp.dma_start(x[0:TS, NPT, :], x_sample.rearrange("b t d -> (b t) d")).then_inc(x_in, 16)
            for L in range(2):
                if L == 1:
                    sp.wait_ge(stored, 16 * NS0)
                    wait(sp, hT_, HEADS - 1, "o")
                    wait(sp, hT_, HEADS - 1, "o")
                sp.dma_start(xmem, mem_prompt[0].rearrange("(i p) d -> p i d", p=P)).then_inc(mem_in, 16)
                jobs = mixer_jobs(L)
                for n, job in enumerate(jobs):
                    j = MIX0[L] + n
                    if n == MEM_JOBS:
                        wait(sp, nH, NORM_MIX[L] + NT + 1, "hi")
                        wait(sp, nP, NORM_MIX[L] + NT + 1, "lo")
                        for z in range(2):
                            sp.dma_start(cacheb[:, :].rearrange("p (b i c) -> p b i c", b=NB, i=2)[:, 4 * z:4 * z + 4],
                                         cache_rows(cache_mem_k, L, 2)[:, 4 * z:4 * z + 4]).then_inc(side_in, 16)
                    if n == J_MO:
                        wait(sp, mV, L, "rows")
                        for z, (t, d) in enumerate(((ktok_mem, new_mem_k), (vmem, new_mem_v))):
                            store(d[L, 0].rearrange("(i p) h d -> p i (h d)", p=P), t)
                    if n == J_TOK:
                        if L == 1:
                            wait(sp, sT, 1, "pv")
                            for z, cc in enumerate((cache_swa_k, cache_swa_v)):
                                sp.dma_start(cacheb[:, z * 2048:(z + 1) * 2048].rearrange("p (b c) -> p b c", b=NB),
                                             cc[0].rearrange("b p h d -> p b (h d)")).then_inc(side_in, 16)
                    if L == 0 and n >= J_TOK and (n - J_TOK) % HGRN_JOBS == 0:
                        h = (n - J_TOK) // HGRN_JOBS
                        if h == 0:
                            wait(sp, sT, 0, "pv")
                        else:
                            wait(sp, hV, h - 1, "sd")
                            store(new_hg_p[0, 0, h - 1], S[:, NPT - 1, :])
                            store(new_hg_s[0, :, h - 1].rearrange("b c v -> c b v"),
                                  SN[:, :].rearrange("p (b v) -> p b v", b=NB))
                            wait(sp, hT_, h - 1, "o")
                        sp.dma_start(S0[:, :].rearrange("p (b v) -> p b v", b=NB),
                                     state_hgrn[0, :, h].rearrange("b c v -> c b v")).then_inc(side_in, 16)
                    load(j % 3, j // 3, j, job)
                if L == 0:
                    wait(sp, hV, HEADS - 1, "sd")
                    store(new_hg_p[0, 0, HEADS - 1], S[:, NPT - 1, :])
                    store(new_hg_s[0, :, HEADS - 1].rearrange("b c v -> c b v"),
                          SN[:, :].rearrange("p (b v) -> p b v", b=NB))
                else:
                    wait(sp, kV, 0, "rows")
                    store(new_swk_p[0, 0].rearrange("w h d -> w (h d)"), ktok[:, 0, :])
                    store(new_swv_p[0, 0].rearrange("w h d -> w (h d)"), vwin[:, NPT - 1, :])
                    for b in range(NB):
                        store(new_swk_s[0, b, WIN - TQ:].rearrange("w h d -> w (h d)"),
                              ktok[TQ * b:TQ * b + TQ, 1, :])
                        store(new_swv_s[0, b, WIN - TQ:].rearrange("w h d -> w (h d)"),
                              vwin[TQ * b:TQ * b + TQ, NPT, :])
                    for z, (o, cc) in enumerate(((new_swk_s, cache_swa_k), (new_swv_s, cache_swa_v))):
                        store(o[0, :, 0:WIN - TQ].rearrange("b w h d -> b (w h d)"),
                              cc[0, :, TQ:].rearrange("b w h d -> b (w h d)"))
                j0 = FFN0[L]

                def ffn_load(d, kind, it, c):
                    j = j0 + d
                    load(j % 3, None, j + 3 * it, lambda s: ffn_job(L, kind, c, s))

                ffn_load(0, "g", 0, 0)
                ffn_load(1, "u", 0, 0)
                with sp.Fori(1, NCH) as c:
                    ffn_load(-1, "g", c, c)
                    ffn_load(0, "o", c, c - 1)
                    ffn_load(1, "u", c, c)
                ffn_load(-1, "o", NCH, NCH - 1)
            for i in range(NT):
                sp.wait_ge(x_added, (FOUT0[1] + NCH - 1) * OUTG + 2 * i + 2)
                dst = y_prompt[0, i * P:(i + 1) * P, :] if i < NPT else y_sample.rearrange("b t d -> (b t) d")
                sp.dma_start(dst, x[0:rows(i), i, :]).then_inc(stored_y, 16)
            sp.wait_ge(stored, 16 * NSTORE)
            sp.wait_ge(stored_y, 16 * NT)

        def mix_slot(L, n):
            return n % 2

        def split_free(L, n):
            j = MIX0[L] + n
            if n < 2:
                return 0 if L == 0 else MIX0[1] - 1
            return j - 1

        def hi_split(act, j3, n3, s, free):
            act.wait_ge(raw_loaded[j3], (n3 + 1) * 32)
            if not (isinstance(free, int) and free <= 0):
                act.wait_ge(w_used, free)
            nc.scalar.activation(slot(0, s), raw[:, j3, :], ACT.Copy).then_inc(w_hi, 1)

        def lo_split(pool, j3, jv, s, free):
            pool.wait_ge(w_hi, jv + 1)
            nc.gpsimd.tensor_tensor(slot(1, s), raw[:, j3, :], slot(0, s).bitcast(F32),
                                    ALU.subtract).then_inc(w_lo, 1)

        class Pump:

            def __init__(self, L, emit):
                self.L, self.n, self.emit = L, 0, emit

            def upto(self, n):
                while self.n < min(n, MIX_JOBS[self.L]):
                    j = MIX0[self.L] + self.n
                    self.emit(j, mix_slot(self.L, self.n), split_free(self.L, self.n))
                    self.n += 1

        def act_emit(act):
            return lambda j, s, free: hi_split(act, j % 3, j // 3, s, free)

        def pool_emit(pool):
            return lambda j, s, free: lo_split(pool, j % 3, j, s, free)

        def ffn_splits(L, split, it, c_par, kinds="gou"):
            slots = ODD if c_par else EVEN
            for k, (kind, d) in enumerate((("g", -1), ("o", 0), ("u", 1))):
                if kind in kinds:
                    split(FFN0[L] + d, it, slots[k], 1 if kind == "g" else 0)

        @block.scalar
        def _(act):
            def A(out, in_, fn, steps, n, name, **kw):
                nc.scalar.activation(out, in_, fn, **kw).then_inc(steps.sem, 1)

            def norm_in(r, src, m):
                if r >= 2:
                    wait(act, nT, r - 2, "tr")
                A(xn[0:m, r % 2, :], src[0:m], ACT.Square, nA, r, "sq", accum_out=nstat[0:m, r:r + 1])
                wait(act, nA, r, "sq")
                A(nstat[0:m, r:r + 1], nstat[0:m, r:r + 1], ACT.Sqrt, nA, r, "std",
                  scale=1.0 / D, bias=col(S_EPS)[0:m])

            def norm_hi(r, dst, c0, m):
                wait(act, nG, r, "g1")
                A(dst[0][:, :, c0:c0 + m], gained[:, 0:KT * m].rearrange("p (k t) -> p k t", k=KT),
                  ACT.Copy, nH, r, "hi")

            def norms(r0, first=None, mem=False):
                srcs = [(x[:, i, :], rows(i), hT, i * P) for i in range(NT)]
                if mem:
                    srcs += [(xmem[:, i, :], P, memT, i * P) for i in range(2)]
                for i in range(len(srcs) + 3):
                    if i < len(srcs):
                        src, m, dst, c0 = srcs[i]
                        if i >= NT:
                            act.wait_ge(mem_in, 16 * (2 if r0 else 1))
                        elif first is None:
                            act.wait_ge(x_in, 16 * NT)
                        else:
                            act.wait_ge(x_added, first * OUTG + 2 * i + 2)
                        norm_in(r0 + i, src, m)
                    if i >= 3:
                        src, m, dst, c0 = srcs[i - 3]
                        norm_hi(r0 + i - 3, dst, c0, m)

            def head_squares(u):
                for z, t in enumerate((prob, prob2)):
                    wait(act, qT, u, f"proj{z}")
                    A(three(t[:, :]), fm(3 - 3 * z), ACT.Square, qA, u, f"sq{z}")

            def head_stds(u):
                for z in range(2):
                    wait(act, qT, u, f"ssq{z}")
                    nc.scalar.activation(probT[:, 0:SEQ].rearrange("p (b n) -> p b n", b=2), ps[:, 6:8, :], ACT.Sqrt,
                                         scale=1.0 / HD, bias=col(S_EPS))
                    A(probT[:, SEQ:T], ps[:, 2 + 3 * z, TW:TW + TS], ACT.Sqrt, qA, u, f"std{z}",
                      scale=1.0 / HD, bias=col(S_EPS))

            def prompt_exp(r, sink):
                buf, s = (prob, prob2)[r % 2], 20 * (r % 4)
                wait(act, vM, r, "neg")
                if r >= 2:
                    wait(act, aPT, r - 2, "pt")
                if r >= 4:
                    wait(act, vO, r - 4, "o")
                for i in range(4):
                    src = ps[:, 2 * (r % 2) + i // 2, 256 * (i % 2):256 * (i % 2) + 256] if sink is None \
                        else buf[:, 256 * i:256 * i + 256]
                    ins = nc.scalar.activation(buf[:, 256 * i:256 * i + 256], src, ACT.Exp,
                                               bias=st[:, s + 4 + i:s + 5 + i], accum_out=st[:, s + 8 + i:s + 9 + i])
                ins.then_inc(aE.sem, 1)
                if sink is not None:
                    A(st[:, s + 12:s + 16], st[:, s + 4:s + 8], ACT.Exp, aSK, r, "sink", bias=sink)

            def prompt_turn(r):
                wait(act, aPT, r, "pt")
                if r >= 1:
                    wait(act, aPV, r - 1, "pv")
                A(probT[:, 0:512], ps[:, 4, :], ACT.Copy, aC, r, "pt")

            def sample_attn(p, sink):
                n = 1 if sink is not None else 2
                for b in range(NB):
                    wait(act, sT, p, f"kt{b}")
                    A(kcT[:, b % 2, 0:256 * n], ps[:, 6 + b % 2, 0:256 * n], ACT.Copy, sA, p, f"kt{b}")
                if sink is None:
                    for z in range(2):
                        act.dma_start(cacheb[:, :].rearrange("p (b i c) -> p b i c", b=NB, i=2)[:, 4 * z:4 * z + 4],
                                      cache_mem_v[p].rearrange("b (i p) h d -> p b i (h d)", p=P)[:, 4 * z:4 * z + 4]
                                      ).then_inc(side_in, 16)
                wait(act, sV, p, "neg")
                w = 256 if sink is None else 160
                A(sprob[:, 0:w], ps[:, 0, 0:w] if sink is None else sprob[:, 0:w], ACT.Exp, sA, p, "exp",
                  bias=ast[:, 33:34], accum_out=ast[:, 34:35])
                if sink is not None:
                    A(ast[:, 35:36], ast[:, 33:34], ACT.Exp, sA, p, "sink", bias=sink)
                else:
                    A(ast[:, 35:36], ast[:, 33:34], ACT.Copy, sA, p, "sink")

            def pair(p, pump, n_next, n_out, g, u_next):
                pump.upto(n_next)
                for s in range(8 + 2):
                    if s < 8:
                        half, q, h2 = s // 4, s // 2 % 2, s % 2
                        prompt_exp(8 * p + s, None if g is None else col(S_SINK + 3 * (2 * half + h2) + g))
                    if s >= 2:
                        prompt_turn(8 * p + s - 2)
                sample_attn(p, None if g is None else col(S_SROW + g))
                pump.upto(n_out + 1)
                wait(act, sV, p, "o1")
                A(mm[0][:, :, :], qh, ACT.Copy, oA, p, "hi")
                pump.upto(n_out + 2)
                if u_next is not None:
                    head_squares(u_next)
                    head_stds(u_next)

            def ffn(L):
                def split(jb, it, s, extra):
                    hi_split(act, jb % 3, jb // 3 + it, s, jb + 3 * it - 5 + extra)

                def chunk(r, par_, c):
                    wait(act, fT, r, "g")
                    if not (isinstance(r, int) and r == 0):
                        wait(act, fV, r - 1, "mul")
                    A(three(sg[:, :]), fm(0), ACT.Silu, fA, r, "silu")
                    wait(act, fV, r, "mul")
                    A(mm[0][:, par_, :], gated[:, :], ACT.Copy, fA, r, "hi")

                if L == 0:
                    wait(act, hV, HEADS - 1, "lo")
                else:
                    wait(act, oV, NPAIR - 1, "lo")
                    act.wait_ge(stored, 16 * NSTORE)
                for d, s in ((0, EVEN[0]), (1, EVEN[2])):
                    j = FFN0[L] + d
                    hi_split(act, j % 3, j // 3, s, 0)
                norms(NORM_FFN[L], first=FOUT0[L] - 1)
                act.wait_ge(w_used, FFN0[L])
                ffn_splits(L, split, 1, 1)
                chunk(NCH * L, 0, 0)
                with act.Fori(0, (NCH - 2) // 2) as it:
                    for z in range(2):
                        c = 2 * it + 1 + z
                        ffn_splits(L, split, c + 1, z)
                        chunk(c + NCH * L, 1 - z, c)
                ffn_splits(L, split, NCH, 0, "g")
                chunk(NCH * L + NCH - 1, 1, NCH - 1)

            def hgrn_head(h, pump, n0):
                if h == 0:
                    act.wait_ge(stored, 16 * 2)
                else:
                    wait(act, hV, h - 1, "lo")
                pump.upto(n0 + 1)
                wait(act, hQ, h, "q")
                A(three(tA[:, :]), fm(0), ACT.Sigmoid, hA, h, "sq")
                wait(act, hZ, h, "z")
                A(three(E[:, 0:T]), fm(3), ACT.Sigmoid, hA, h, "f")
                A(three(K[:, :]), fm(3), ACT.Sigmoid, hA, h, "k", scale=-1.0)
                wait(act, hA, h, "k")
                A(E[:, 0:T], E[:, 0:T], ACT.Identity, hA, h, "e", scale=col(S_ML + h), bias=col(S_L + h))
                A(K[:, :], K[:, :], ACT.Copy, hA, h, "ks", scale=col(S_ML + h))
                pump.upto(n0 + 2)
                last = h == HEADS - 1
                wait(act, hT_, h, "g")
                wait(act, hV, h, "q")
                A(three(tA[:, :]), fm(0), ACT.Sigmoid, hA, h, "sg")
                if not last:
                    pump.upto(n0 + 4)
                else:
                    pump.upto(n0 + 3)
                wait(act, hT_, h, "kr")
                nc.scalar.activation(KR[:, 0:4, :], ps[:, 6, :].rearrange("p (i c) -> p i c", i=4), ACT.Copy)
                nc.scalar.activation(KR[:, 4:8, :], ps[:, 7, :].rearrange("p (i c) -> p i c", i=4), ACT.Copy)
                A(KR[0:TS, 8, :], ps[0:TS, 5, P:2 * P], ACT.Copy, hA, h, "kr")
                wait(act, hT_, h, "o")
                nc.scalar.activation(O2[:, 0:SEQ].rearrange("p (g n) -> p g n", g=2), ps[:, 3:5, :], ACT.Square)
                A(O2[:, SEQ:T], ps[:, 5, 0:TS], ACT.Square, hA, h, "o2")
                wait(act, hT_, h, "ssq")
                nc.scalar.activation(R[:, 0:SEQ].rearrange("p (g n) -> p g n", g=2), ps[:, 6:8, :], ACT.Sqrt,
                                     scale=1.0 / P, bias=col(S_EPS))
                A(R[:, SEQ:T], ps[:, 5, 64:64 + TS], ACT.Sqrt, hA, h, "std", scale=1.0 / P, bias=col(S_EPS))
                pump.upto(n0 + (3 if last else 5))
                wait(act, hV, h, "m")
                A(mm[0][:, 0, :], tA[:, :], ACT.Copy, hA, h, "hi")

            act.wait_ge(small_in, 32)
            act.wait_ge(init, 1)
            nc.scalar.activation(col(S_L, HEADS), col(S_L, HEADS), ACT.Exp).then_inc(lb_exp, 1)
            for L in range(2):
                pump = Pump(L, act_emit(act))
                pump.upto(2)
                norms(NORM_MIX[L], first=None if L == 0 else FOUT0[0] + NCH - 1, mem=True)
                pump.upto(MEM_JOBS)
                wait(act, mT, L, "k")
                A(prob[:, 0:512], ps[:, 0, :], ACT.Square, mA, L, "sq")
                wait(act, mT, L, "ssq")
                A(probT[:, 0:512], ps[:, 2, :], ACT.Sqrt, mA, L, "std", scale=1.0 / HD, bias=col(S_EPS))
                pump.upto(J_MQ + 2)
                head_squares([0, 1][L])
                head_stds([0, 1][L])
                pair(L, pump, J_FILL + 2, J_MO, None, [None, 2][L])
                n0 = J_TOK
                if L == 0:
                    for h in range(HEADS):
                        hgrn_head(h, pump, n0 + HGRN_JOBS * h)
                else:
                    pump.upto(n0 + 4)
                    head_squares(3)
                    head_stds(3)
                    for g in range(QG):
                        no = n0 + 4 + PAIR_JOBS * g + (2 if g < QG - 1 else 0)
                        pair(2 + g, pump, no, no, g, 4 + g if g < QG - 1 else None)
                pump.upto(MIX_JOBS[L])
                ffn(L)

        @block.gpsimd
        def _(pool):
            def norms(r0, mem=False):
                for i in range(NT + (2 if mem else 0)):
                    dst, c0, m = (hT, i * P, rows(i)) if i < NT else (memT, (i - NT) * P, P)
                    wait(pool, nH, r0 + i, "hi")
                    nc.gpsimd.tensor_tensor(dst[1][:, :, c0:c0 + m],
                                            gained[:, 0:KT * m].rearrange("p (k t) -> p k t", k=KT),
                                            dst[0][:, :, c0:c0 + m].bitcast(F32), ALU.subtract).then_inc(nP.sem, 1)

            def ffn(L):
                def split(jb, it, s, extra):
                    lo_split(pool, jb % 3, jb + 3 * it, s, None)

                for d, s in ((0, EVEN[0]), (1, EVEN[2])):
                    lo_split(pool, (FFN0[L] + d) % 3, FFN0[L] + d, s, None)
                norms(NORM_FFN[L])
                ffn_splits(L, split, 1, 1)
                with pool.Fori(0, (NCH - 2) // 2) as it:
                    for z in range(2):
                        ffn_splits(L, split, 2 * it + 2 + z, z)
                ffn_splits(L, split, NCH, 0, "g")

            def hgrn_head(h, pump, n0):
                pump.upto(n0 + 2)
                last = h == HEADS - 1
                for l in range(LEVELS):
                    w = 1 << l
                    n = T if l < 2 else SEQ
                    Eo = E[:, EOFF[l]:EOFF[l] + n // w].rearrange("p (b z) -> p b z", z=2)
                    wait(pool, hT_, h, f"l{l}")
                    if l:
                        wait(pool, hP, h, f"e{l - 1}")
                    Kv = K[:, 0:n].rearrange("p (b z w) -> p b z w", z=2, w=w)[:, :, 0, :]
                    nc.gpsimd.tensor_tensor(Kv, Kv, Eo[:, :, 1].unsqueeze(2).to_broadcast([P, n // (2 * w), w]),
                                            ALU.mult).then_inc(hP.sem, 1)
                    nc.gpsimd.tensor_tensor(E[:, EOFF[l + 1]:EOFF[l + 1] + n // (2 * w)], Eo[:, :, 0], Eo[:, :, 1],
                                            ALU.mult).then_inc(hP.sem, 1)
                    if l == 4 and not last:
                        pump.upto(n0 + 3)
                pump.upto(n0 + (3 if last else 5))

            for L in range(2):
                pump = Pump(L, pool_emit(pool))
                pump.upto(2)
                norms(NORM_MIX[L], mem=True)
                if L == 0:
                    pump.upto(J_TOK)
                    for h in range(HEADS):
                        hgrn_head(h, pump, J_TOK + HGRN_JOBS * h)
                pump.upto(MIX_JOBS[L])
                ffn(L)

        @block.vector
        def _(dve):
            V_ = nc.vector

            def tt(out, a, b, op=ALU.mult):
                return V_.tensor_tensor(out, a, b, op)

            def stt(out, a, s, b, op0=ALU.mult, op1=ALU.mult):
                return V_.scalar_tensor_tensor(out=out, in0=a, scalar=s, in1=b, op0=op0, op1=op1)

            def add_group(G, i, n):
                dve.wait_ge(out_ready, G + 1)
                if not isinstance(G, int) or G >= OUTG:
                    dve.wait_ge(x_added, G - OUTG + 1)
                xs = x[0:rows(i), i, 512 * n:512 * n + 512]
                tt(xs, xs, ps[0:rows(i), 6 + n, :], ALU.add).then_inc(x_added, 1)

            def adds(o, tiles=range(NT)):
                for i in tiles:
                    for n in range(2):
                        add_group(o * OUTG + 2 * i + n, i, n)

            def norms(r0, gain, mem_gain=None, o=None):
                srcs = [(x[:, i, :], rows(i), gain) for i in range(NT)]
                if mem_gain is not None:
                    srcs += [(xmem[:, i, :], P, mem_gain) for i in range(2)]
                for i in range(len(srcs) + 3):
                    if o is not None and i < NT:
                        for n in range(2):
                            add_group(o * OUTG + 2 * i + n, i, n)
                    if 1 <= i <= len(srcs):
                        r, (src, m, _) = r0 + i - 1, srcs[i - 1]
                        wait(dve, nA, r, "std")
                        V_.reciprocal(nrstd[0:m, r:r + 1], nstat[0:m, r:r + 1]).then_inc(nV.sem, 1)
                        wait(dve, nV, r, "rstd")
                        V_.tensor_scalar(xn[0:m, r % 2, :], src[0:m], nrstd[0:m, r:r + 1], None,
                                         ALU.mult).then_inc(nV.sem, 1)
                    if i >= 3:
                        r, (_, m, g) = r0 + i - 3, srcs[i - 3]
                        wait(dve, nT, r, "tr")
                        if r:
                            wait(dve, nP, r - 1, "lo")
                        for z in range(2):
                            b = 2 * (r % 2) + z
                            tt(gained[:, 4 * m * z:4 * m * (z + 1)].rearrange("p (k t) -> p k t", k=4),
                               ps[:, b, 0:4 * m].rearrange("p (k t) -> p k t", k=4),
                               col(g + 4 * z, 4).unsqueeze(2).to_broadcast([P, 4, m])).then_inc(nG.sem, 1)

            def head_norm(u, dsts, gain):
                for z, dst in enumerate(dsts):
                    wait(dve, qA, u, f"std{z}")
                    V_.reciprocal(probT[:, :], probT[:, :]).then_inc(qV.sem, 1)
                    wait(dve, qV, u, f"rstd{z}")
                    stt(three(dst), fm(3 - 3 * z), gain, three(probT[:, :])).then_inc(qV.sem, 1)

            def prompt_max(r, first, head):
                buf, s = (prob, prob2)[r % 2], 20 * (r % 4)
                wait(dve, aSC, r, "sc")
                if r >= 2:
                    wait(dve, aPT, r - 2, "pt")
                b0 = 2 * (r % 2)
                if head is None:
                    V_.tensor_reduce(st[:, s:s + 4], ps[:, b0:b0 + 2, :].rearrange("p b (i m) -> p (b i) m", i=2),
                                     AX.X, ALU.max).then_inc(vM.sem, 1)
                else:
                    for i in range(4):
                        c = C_BAND + (0 if first and i == 0 else 256)
                        m = V_.tensor_tensor_reduce(buf[:, 256 * i:256 * i + 256],
                                                    ps[:, b0 + i // 2, 256 * (i % 2):256 * (i % 2) + 256],
                                                    cst[:, c:c + 256], 1.0, col(S_SINK + head),
                                                    ALU.add, ALU.max, st[:, s + i:s + i + 1])
                    m.then_inc(vM.sem, 1)
                wait(dve, vM, r, "max")
                V_.tensor_scalar(st[:, s + 4:s + 8], st[:, s:s + 4], -1.0, None, ALU.mult).then_inc(vM.sem, 1)

            def prompt_rinv(r, window):
                s = 20 * (r % 4)
                wait(dve, aE, r, "exp")
                den = st[:, s + 8:s + 12]
                if window:
                    wait(dve, aSK, r - 16, "sink")
                    tt(den, den, st[:, s + 12:s + 16], ALU.add).then_inc(vD.sem, 1)
                    wait(dve, vD, r - 16, "den")
                V_.reciprocal(st[:, s + 16:s + 20], den).then_inc(vR.sem, 1)

            def prompt_turn(r):
                wait(dve, aPT, r, "pt")
                if r >= 1:
                    wait(dve, aPV, r - 1, "pv")
                V_.tensor_copy(probT[:, 512:1024], ps[:, 5, :]).then_inc(vC.sem, 1)

            def prompt_rows(r, h2):
                s = 20 * (r % 4)
                wait(dve, aPV, r, "pv")
                if r >= 2:
                    wait(dve, aOT, r // 2 - 1, "ot")
                wait(dve, vR, r, "rinv")
                tt(orow[:, :, 64 * h2:64 * h2 + 64], ps[:, 6, 256 * h2:256 * h2 + 256].rearrange("p (i d) -> p i d", i=4),
                   st[:, s + 16:s + 20].unsqueeze(2).to_broadcast([P, 4, HD])).then_inc(vO.sem, 1)

            def prompt_out(r, half, q):
                wait(dve, aOT, r // 2, "ot")
                V_.tensor_copy(qh[:, half, 512 * q:512 * q + 512], ps[:, 7, :]).then_inc(vOT.sem, 1)

            def sample_attn(p, g):
                for half in range(2):
                    m = tt(qblk[:, half, :, :].rearrange("p b (s q) -> p b s q", q=TQ),
                           qh[:, half, SEQ:T].rearrange("p (b q) -> p b q", q=TQ).unsqueeze(2)
                           .to_broadcast([P, NB, 8, TQ]),
                           cst[:, C_QB + 64 * half:C_QB + 64 * half + 64].rearrange("p (b s) -> p b s", b=NB)
                           .unsqueeze(3).to_broadcast([P, NB, 8, TQ]))
                m.then_inc(sV.sem, 1)
                wait(dve, sT, p, "sc")
                if g is None:
                    V_.tensor_reduce(ast[:, 32:33], ps[:, 0, 0:256], AX.X, ALU.max).then_inc(sV.sem, 1)
                else:
                    V_.tensor_tensor_reduce(sprob[:, 0:160], ps[:, 0, 0:160], cst[:, C_SROW:C_SROW + 160], 1.0,
                                            col(S_SROW + g), ALU.add, ALU.max, ast[:, 32:33]).then_inc(sV.sem, 1)
                wait(dve, sV, p, "max")
                V_.tensor_scalar(ast[:, 33:34], ast[:, 32:33], -1.0, None, ALU.mult).then_inc(sV.sem, 1)
                wait(dve, sA, p, "sink")
                if g is None:
                    V_.tensor_copy(ast[:, 36:37], ast[:, 34:35]).then_inc(sV.sem, 1)
                else:
                    tt(ast[:, 36:37], ast[:, 34:35], ast[:, 35:36], ALU.add).then_inc(sV.sem, 1)
                wait(dve, sV, p, "den")
                V_.reciprocal(ast[:, 37:38], ast[:, 36:37]).then_inc(sV.sem, 1)
                wait(dve, sV, p, "rinv")
                w = 256 if g is None else 160
                V_.tensor_scalar(sprob[:, 0:w], sprob[:, 0:w], ast[:, 37:38], None, ALU.mult).then_inc(sV.sem, 1)
                wait(dve, sT, p, "pt")
                if g is None:
                    V_.tensor_copy(sprobT, ps[:, 1, 0:256].rearrange("p (c r) -> p c r", c=2)).then_inc(sV.sem, 1)
                else:
                    V_.tensor_copy(sprobT[:, 0, :], ps[:, 1, 0:P])
                    V_.tensor_copy(sprobT[0:TS, 1, :], ps[0:TS, 1, P:2 * P]).then_inc(sV.sem, 1)
                wait(dve, sT, p, "pv")
                for h2 in range(2):
                    r = slice(64 * h2, 64 * h2 + 64)
                    V_.tensor_copy(qh[r, :, SEQ:T].rearrange("p a (b q) -> p a b q", q=TQ),
                                   ps[r, 2, 0:P].rearrange("p (a b z q) -> p a b z q", a=2, b=NB, z=2)[:, :, :, h2, :]
                                   ).then_inc(sV.sem, 1)

            def pair(p, g):
                for s in range(8 + 4):
                    if s < 8:
                        half, q, h2 = s // 4, s // 2 % 2, s % 2
                        prompt_max(8 * p + s, q == 0, None if g is None else 3 * (2 * half + h2) + g)
                    if 1 <= s < 9:
                        prompt_rinv(8 * p + s - 1, g is not None)
                    if 2 <= s < 10:
                        prompt_turn(8 * p + s - 2)
                    if 3 <= s < 11:
                        prompt_rows(8 * p + s - 3, (s - 3) % 2)
                    if s >= 4 and s % 2:
                        prompt_out(8 * p + s - 4, (s - 4) // 4, (s - 4) // 2 % 2)
                sample_attn(p, g)
                wait(dve, oA, p, "hi")
                tt(mm[1], qh, mm[0].bitcast(F32), ALU.subtract).then_inc(oV.sem, 1)

            def hgrn_head(h):
                if h == 0:
                    wait(dve, oV, 0, "lo")
                    dve.wait_ge(stored, 16 * 2)
                    V_.memset(ones[:, :], 1.0)
                    V_.memset(att[:, :], 0.0).then_inc(init, 1)
                    dve.wait_ge(init, INIT + 1)
                inc = hV.sem
                wait(dve, hA, h, "sq")
                stt(three(Q[:, :]), fm(0), float(P) ** -0.5, three(tA[:, :])).then_inc(inc, 1)
                if h:
                    adds(OUT0[0] + h, range(4, NT))
                wait(dve, hT_, h, "diag")
                idm = ident.bitcast(I32)
                V_.copy_predicated(att[:, 0:SEQ].rearrange("p (i t) -> p i t", i=NPT),
                                   idm.unsqueeze(1).to_broadcast([P, NPT, P]),
                                   ps[:, 6:8, :].rearrange("p b (i t) -> p (b i) t", i=4))
                V_.copy_predicated(att[0:TS, SEQ:T], idm[0:TS, 0:TS], ps[0:TS, 5, 256:256 + TS]).then_inc(inc, 1)
                wait(dve, hV, h, "q")
                tt(Q[:, :], Q[:, :], E[:, 0:T]).then_inc(inc, 1)
                for l in range(LEVELS):
                    w = 1 << l
                    n = T if l < 2 else SEQ
                    wait(dve, hT_, h, f"l{l}")
                    mask = cst[:, C_LVL + 64 * l:C_LVL + 64 * l + 64].bitcast(I32)
                    av = att[:, 0:SEQ].rearrange("p (i b z w) -> p i b z w", i=NPT, z=2, w=w)[:, :, :, 1, :]
                    ins = V_.copy_predicated(
                        av, mask.rearrange("p (b w) -> p b w", w=w).unsqueeze(1).to_broadcast([P, NPT, 64 // w, w]),
                        ps[:, 6 + l % 2, :].rearrange("p (i b w) -> p i b w", i=NPT, w=w))
                    if l < 2:
                        ins = V_.copy_predicated(
                            att[0:TS, SEQ:T].rearrange("p (b z w) -> p b z w", z=2, w=w)[:, :, 1, :],
                            mask[0:TS, 0:16].rearrange("p (b w) -> p b w", w=w),
                            ps[0:TS, 5, 288 + 16 * l:304 + 16 * l].rearrange("p (b w) -> p b w", w=w))
                    ins.then_inc(inc, 1)
                    if l:
                        wait(dve, hP, h, f"e{l - 1}")
                    wait(dve, hV, h, "qf" if l == 0 else f"q{l - 1}")
                    Qv = Q[:, 0:n].rearrange("p (b z w) -> p b z w", z=2, w=w)[:, :, 1, :]
                    Ee = E[:, EOFF[l]:EOFF[l] + n // w].rearrange("p (b z) -> p b z", z=2)[:, :, 0]
                    tt(Qv, Qv, Ee.unsqueeze(2).to_broadcast([P, n // (2 * w), w])).then_inc(inc, 1)
                wait(dve, hA, h, "sg")
                tt(three(G[:, :]), fm(0), three(tA[:, :])).then_inc(inc, 1)
                wait(dve, hT_, h, "v")
                V_.tensor_copy(V[:, 0:8, :], ps[:, 3:5, :].rearrange("p b (i c) -> p (b i) c", i=4))
                V_.tensor_copy(V[0:TS, 8, :], ps[0:TS, 5, 0:P]).then_inc(inc, 1)
                wait(dve, hV, h, "v")
                tt(VM[0:TS, :].rearrange("p (b v) -> p b v", b=NB), V[0:TS, 8, :].unsqueeze(1).to_broadcast([TS, NB, P]),
                   cst[0:TS, C_VM:C_VM + NB].unsqueeze(2).to_broadcast([TS, NB, P])).then_inc(inc, 1)
                wait(dve, hT_, h, "ds")
                wait(dve, hP, h, f"e{LEVELS - 1}")
                if h:
                    dve.wait_ge(stored, 16 * (2 + 2 * h))
                for i in range(NPT):
                    ds = ps[:, 6 + i // 4, P * (i % 4):P * (i % 4) + P]
                    if i == 0:
                        V_.tensor_copy(S[:, 0, :], ds).then_inc(inc, 1)
                    else:
                        wait(dve, hV, h, f"s{i - 1}")
                        stt(S[:, i, :], S[:, i - 1, :], E[:, EOFF[LEVELS] + i:EOFF[LEVELS] + i + 1], ds,
                            ALU.mult, ALU.add).then_inc(inc, 1)
                dve.wait_ge(side_in, 16 * (4 + h + 1))
                sv = SN[:, :].rearrange("p (b v) -> p b v", b=NB)
                tt(sv, S0[:, :].rearrange("p (b v) -> p b v", b=NB),
                   E[:, EOFF[2] + SEQ // 4:EOFF[2] + T // 4].unsqueeze(2).to_broadcast([P, NB, P])).then_inc(inc, 1)
                wait(dve, hV, h, "sn")
                wait(dve, hT_, h, "ds8")
                tt(SN[:, :].rearrange("p (b v) -> p b v", b=2), SN[:, :].rearrange("p (b v) -> p b v", b=2),
                   ps[:, 6:8, :], ALU.add).then_inc(inc, 1)
                wait(dve, hA, h, "std")
                V_.reciprocal(R[:, :], R[:, :]).then_inc(inc, 1)
                wait(dve, hV, h, "rstd")
                tt(O2[:, 0:SEQ].rearrange("p (b n) -> p b n", b=2), ps[:, 3:5, :],
                   R[:, 0:SEQ].rearrange("p (b n) -> p b n", b=2))
                tt(O2[:, SEQ:T], ps[:, 5, 0:TS], R[:, SEQ:T]).then_inc(inc, 1)
                wait(dve, hV, h, "o")
                stt(tA[:, :], O2[:, :], col(S_GN + h), G[:, :]).then_inc(inc, 1)
                wait(dve, hA, h, "hi")
                tt(mm[1][:, 0, :], tA[:, :], mm[0][:, 0, :].bitcast(F32), ALU.subtract).then_inc(inc, 1)
                if h < HEADS - 1:
                    adds(OUT0[0] + 1 + h, range(4))

            def ffn(L):
                def chunk(r, par_, G0):
                    if G0 is not None:
                        for i in range(NT):
                            for n in range(2):
                                add_group(G0 + 2 * i + n, i, n)
                    wait(dve, fT, r, "u")
                    wait(dve, fA, r, "silu")
                    tt(three(gated[:, :]), fm(3), three(sg[:, :])).then_inc(fV.sem, 1)
                    wait(dve, fA, r, "hi")
                    tt(mm[1][:, par_, :], gated[:, :], mm[0][:, par_, :].bitcast(F32),
                       ALU.subtract).then_inc(fV.sem, 1)

                norms(NORM_FFN[L], S_FFN + KT * L, o=FOUT0[L] - 1)
                chunk(NCH * L, 0, None)
                with dve.Fori(0, (NCH - 2) // 2) as it:
                    for z in range(2):
                        chunk(2 * it + 1 + z + NCH * L, 1 - z, OUTG * 2 * it + OUTG * (z + FOUT0[L]))
                chunk(NCH * L + NCH - 1, 1, OUTG * (FOUT0[L] + NCH - 2))

            def setup():
                n = [0]

                def done(ins):
                    n[0] += 1
                    ins.then_inc(init, 1)
                    return n[0]

                V_.memset(col(S_EPS), EPS)
                dve.wait_ge(small_in, 32)
                lb, ml, rawl = col(S_L, HEADS), col(S_ML, HEADS), col(S_LB, HEADS)
                V_.tensor_scalar(col(S_GQ, 1), col(S_SQ, 1), HD ** -0.5, None, ALU.mult)
                V_.tensor_scalar(col(S_GQ + 1, 2), col(S_MQ, 2), HD ** -0.5, None, ALU.mult)
                k = done(tt(lb, rawl, rawl, ALU.subtract))
                dve.wait_ge(lb_exp, 1)
                k = done(V_.reciprocal(ml, lb))
                dve.wait_ge(init, k)
                k = done(tt(lb, lb, ml))
                dve.wait_ge(init, k)
                k = done(tt(ml, lb, lb, ALU.subtract))
                dve.wait_ge(init, k)
                k = done(V_.tensor_scalar(lb, ml, 0.0, 0.999, ALU.max, ALU.min))
                dve.wait_ge(init, k)
                k = done(V_.tensor_scalar(ml, lb, -1.0, 1.0, ALU.mult, ALU.add))
                dve.wait_ge(init, k)
                assert k == INIT

            setup()
            for L in range(2):
                if L == 0:
                    dve.wait_ge(x_in, 16 * NT)
                norms(NORM_MIX[L], S_MIX + KT * L, S_MEM + KT * L, o=None if L == 0 else FOUT0[0] + NCH - 1)
                wait(dve, mA, L, "std")
                V_.reciprocal(probT[:, 0:512], probT[:, 0:512]).then_inc(mV.sem, 1)
                wait(dve, mV, L, "rstd")
                stt(kmem.rearrange("p a m -> p (a m)"), ps[:, 0, :], col(S_MK + L), probT[:, 0:512]).then_inc(mV.sem, 1)
                V_.tensor_copy(vmem.rearrange("p i c -> p (i c)"), ps[:, 1, :]).then_inc(mV.sem, 1)
                wait(dve, mT, L, "rows")
                V_.tensor_copy(ktok_mem.rearrange("p i c -> p (i c)"), ps[:, 3, :]).then_inc(mV.sem, 1)
                heads_of_qh = [qh[:, half, :] for half in range(2)]
                head_norm([0, 1][L], heads_of_qh, col(S_GQ + 1 + L))
                wait(dve, qV, [0, 1][L], "n1")
                pair(L, None)
                adds(OUT0[L])
                if L == 0:
                    for h in range(HEADS):
                        hgrn_head(h)
                else:
                    dve.wait_ge(stored, 16 * (NS0 + 2))
                    V_.memset(kpad[:, :, 0:WIN], 0.0).then_inc(kV.sem, 1)
                    head_norm(2, [kpad[:, half, WIN:WIN + T] for half in range(2)], col(S_SK))
                    wait(dve, kT, 0, "v")
                    V_.tensor_copy(vwin[:, 0:8, :], ps[:, 0:4, :].rearrange("p b (i c) -> p (b i) c", i=2))
                    V_.tensor_copy(vwin[0:TS, 8, :], ps[0:TS, 4, 0:256]).then_inc(kV.sem, 1)
                    wait(dve, kT, 0, "rows")
                    V_.tensor_copy(ktok[:, 0, :], ps[:, 5, 0:256])
                    V_.tensor_copy(ktok[0:TS, 1, :], ps[0:TS, 5, 256:512]).then_inc(kV.sem, 1)
                    head_norm(3, heads_of_qh, col(S_GQ))
                    for g in range(QG):
                        wait(dve, qV, 3 + g, "n1")
                        pair(2 + g, g)
                        if g < QG - 1:
                            adds(OUT0[1] + 1 + g)
                            head_norm(4 + g, heads_of_qh, col(S_GQ))
                ffn(L)
            adds(FOUT0[1] + NCH - 1)

        @block.tensor
        def _(pe):
            mmul = nc.tensor.matmul
            PASS = ((0, 0), (0, 1), (1, 0))

            def feat_mm(s, b0, m):
                k, (a, b), g = m // 9, PASS[m % 9 // 3], m % 3
                return mmul(ps[:, b0 + g, 0:TW], slot(a, s)[:, P * k:P * k + P], hT[b][:, k, TW * g:TW * g + TW],
                            start=m < 3, stop=m >= 69)

            def feat(j, s, b0, steps, part=(0, 1)):
                a, b = part
                if a == 0:
                    pe.wait_ge(w_lo, j + 1)
                for m in range(72 * a // b, 72 * (a + 1) // b):
                    ins = feat_mm(s, b0, m)
                if a == b - 1:
                    ins.then_inc(steps.sem, 1)
                    used(j)

            def used(j):
                pe.drain().then_inc(w_used, 1)

            def row_major(j, s, act, tiles, place):
                if tiles[0][0] == 0:
                    pe.wait_ge(w_lo, j + 1)
                for i, m in tiles:
                    for k in range(KT):
                        for q, (a, b) in enumerate(PASS):
                            ins = mmul(place(i, m), act[b][:, k, P * i:P * i + m], slot(a, s)[:, P * k:P * k + P],
                                       start=k == 0 and q == 0, stop=k == KT - 1 and q == 2)
                return ins

            def out_group(G, i, n, srcs):
                if not isinstance(G, int) or G >= 2:
                    pe.wait_ge(x_added, G - 1)
                steps = [(p, s, a, b) for p, s in srcs for a, b in PASS]
                for q, (p, s, a, b) in enumerate(steps):
                    ins = mmul(ps[0:rows(i), 6 + n, :], mm[b][:, p, P * i:P * i + rows(i)],
                               slot(a, s)[:, 512 * n:512 * n + 512], start=q == 0, stop=q == len(steps) - 1)
                return ins.then_inc(out_ready, 1)

            def outs(o, j, srcs, after=None):
                pe.wait_ge(w_lo, j + len(srcs))
                for i in range(NT):
                    for n in range(2):
                        out_group(o * OUTG + 2 * i + n, i, n, srcs)
                    if after:
                        after(i)
                pe.drain().then_inc(w_used, len(srcs))

            def transposes(r, i):
                m = rows(i) if i < NT else P
                wait(pe, nV, r, "xn")
                if r >= 2:
                    wait(pe, nG, r - 2, "g1")
                for k in range(KT):
                    ins = nc.tensor.transpose(ps[:, 2 * (r % 2) + k // 4, m * (k % 4):m * (k % 4) + m],
                                              xn[0:m, r % 2, P * k:P * k + P], ident[0:m, 0:m])
                ins.then_inc(nT.sem, 1)

            def norms(r0, mem=False, out=None):
                n = NT + (2 if mem else 0)

                def after(i):
                    if i >= 2:
                        transposes(r0 + i - 2, i - 2)

                if out:
                    outs(*out, after=after)
                for i in range(NT if out else 2, n + 2):
                    after(i)
                wait(pe, nP, r0 + n - 1, "lo")

            def head_sums(u, after=None):
                for z, t in enumerate((prob, prob2)):
                    wait(pe, qA, u, "sq1")
                    if z:
                        wait(pe, qV, u, "n0")
                    for b in range(2):
                        mmul(ps[:, 6 + b, :], cst[:, C_BLK:C_BLK + P], t[:, 512 * b:512 * b + 512], start=True, stop=True)
                    mmul(ps[:, 2 + 3 * z, TW:TW + TS], cst[:, C_BLK:C_BLK + P], t[:, SEQ:T],
                         start=True, stop=True).then_inc(qT.sem, 1)

            def prompt_scores(r, half, h2, q, window):
                hs = slice(64 * h2, 64 * h2 + 64)
                if r % 8 >= 2:
                    wait(pe, vM, r - 2, "max") if window else wait(pe, aE, r - 2, "exp")
                for i in range(4):
                    t = 4 * q + i
                    rhs = kpad[hs, half, P * t:P * t + 256] if window else kmem[hs, half, :]
                    b = 2 * (r % 2) + i // 2
                    ins = mmul(ps[:, b, 256 * (i % 2):256 * (i % 2) + 256], qh[hs, half, P * t:P * t + P], rhs,
                               start=True, stop=True)
                ins.then_inc(aSC.sem, 1)

            def prompt_turn(r):
                buf = (prob, prob2)[r % 2]
                wait(pe, aE, r, "exp")
                if r >= 1:
                    wait(pe, vC, r - 1, "pt")
                    wait(pe, aC, r - 1, "pt")
                for i in range(4):
                    for c in range(2):
                        ins = nc.tensor.transpose(ps[:, 4 + c, P * i:P * i + P],
                                                  buf[:, 256 * i + P * c:256 * i + P * c + P], ident)
                ins.then_inc(aPT.sem, 1)

            def prompt_rows(r, half, h2, q, window):
                wait(pe, vC, r, "pt")
                wait(pe, aC, r, "pt")
                if r >= 1:
                    wait(pe, vO, r - 1, "o")
                for i in range(4):
                    t = 4 * q + i
                    cs = [c for c in range(2) if not window or t + c > 0]
                    for c in cs:
                        hc = slice(P * half + 64 * h2, P * half + 64 * h2 + 64)
                        rhs = vwin[:, t - 1 + c, hc] if window else vmem[:, c, hc]
                        ins = mmul(ps[:, 6, 256 * h2 + 64 * i:256 * h2 + 64 * i + 64],
                                   probT[:, 512 * c + P * i:512 * c + P * i + P], rhs,
                                   start=c == cs[0], stop=c == 1)
                ins.then_inc(aPV.sem, 1)

            def prompt_out(r):
                wait(pe, vO, r, "o")
                if r >= 2:
                    wait(pe, vOT, r // 2 - 1, "ot")
                for i in range(4):
                    ins = nc.tensor.transpose(ps[:, 7, P * i:P * i + P], orow[:, i, :], ident)
                ins.then_inc(aOT.sem, 1)

            def sample_attn(p, window, fill):
                n = 1 if window else 2
                pe.wait_ge(side_in, 16 * [2, 12, 16, 16, 16][p])
                wait(pe, vOT, 4 * p + 3, "ot")
                wait(pe, sV, p, "qb")

                def scores(b):
                    wait(pe, sA, p, f"kt{b}")
                    grp, e = b // 2, b % 2
                    out = slice(32 * grp, 32 * grp + 32)
                    for half in range(2):
                        mmul(ps[out, 0, 0:P * n], qblk[:, half, b, :], kcT[:, b % 2, P * n * half:P * n * (half + 1)],
                             start=e == 0 and half == 0, stop=e == 1 and half == 1)
                    if window and e:
                        for z, bb in enumerate((b - 1, b)):
                            for half in range(2):
                                mmul(ps[out, 0, P:P + TS], qblk[:, half, bb, :], kpad[:, half, WIN + SEQ:WIN + T],
                                     start=z == 0 and half == 0, stop=z == 1 and half == 1)

                for b in range(NB):
                    if b >= 2:
                        wait(pe, sA, p, f"kt{b - 2}")
                    for half in range(2):
                        for i in range(n):
                            c0 = (b * n + i) * 256 + P * half
                            o0 = P * n * half + P * i
                            ins = nc.tensor.transpose(ps[:, 6 + b % 2, o0:o0 + P], cacheb[:, c0:c0 + P], ident)
                    ins.then_inc(sT.sem, 1)
                    if b:
                        fill(b - 1, 10)
                        scores(b - 1)
                fill(7, 10)
                scores(NB - 1)
                pe.drain().then_inc(sT.sem, 1)
                fill(8, 10)
                fill(9, 10)
                wait(pe, sV, p, "p")
                nc.tensor.transpose(ps[:, 1, 0:P], sprob[:, 0:P], ident)
                w = TS if window else P
                nc.tensor.transpose(ps[0:w, 1, P:2 * P], sprob[:, P:P + w], ident).then_inc(sT.sem, 1)
                wait(pe, sV, p, "pt")
                if not window:
                    pe.wait_ge(side_in, 16 * [4, 14][p])
                for half in range(2):
                    for b in range(NB):
                        r0 = 16 * b + 8 * half
                        out = ps[:, 2, 64 * half + 8 * b:64 * half + 8 * b + 8]
                        for c in range(2):
                            if window:
                                lhsT = vwin[0:TS, NPT, P * half:P * half + P] if c else \
                                    cacheb[:, 2048 + 256 * b + P * half:2048 + 256 * b + P * half + P]
                            else:
                                c0 = (2 * b + c) * 256 + P * half
                                lhsT = cacheb[:, c0:c0 + P]
                            k = TS if window and c else P
                            ins = mmul(out, lhsT, sprobT[0:k, c, r0:r0 + 8], start=c == 0, stop=c == 1)
                ins.then_inc(sT.sem, 1)

            def pair(p, window, fills):
                wait(pe, qV, [0, 1, 3, 4, 5][p], "n1")
                for s in range(8 + 4):
                    at_ = lambda s: (8 * p + s, s // 4, s % 2, s // 2 % 2)
                    if s < 8:
                        prompt_scores(*at_(s), window)
                    if 3 <= s < 11:
                        prompt_rows(*at_(s - 3), window)
                    if 2 <= s < 10:
                        prompt_turn(8 * p + s - 2)
                    if s >= 4 and s % 2:
                        prompt_out(8 * p + s - 4)

                def fill(a, b):
                    if fills:
                        feat(fills[0][0], fills[0][1], 3, fills[0][2], (a, b))

                sample_attn(p, window, fill)
                if fills:
                    wait(pe, sV, p, "o1")
                    feat(fills[1][0], fills[1][1], 0, fills[1][2])
                wait(pe, oV, p, "lo")

            def hgrn_head(h, j):
                inc = hT_.sem
                n0 = j - MIX0[0]
                last = h == HEADS - 1
                wait(pe, hV, h, "q")
                wait(pe, hA, h, "ks")
                for i in range(NPT):
                    mmul(ps[:, 6 + i // 4, P * (i % 4):P * (i % 4) + P], K[:, P * i:P * i + P], Q[:, P * i:P * i + P],
                         start=True, stop=True)
                mmul(ps[0:TS, 5, 256:256 + TS], K[:, SEQ:T], Q[:, SEQ:T], start=True, stop=True).then_inc(inc, 1)
                feat(j, n0 % 2, 0, hT_, (0, 4))
                for l in range(LEVELS):
                    w = 1 << l
                    wait(pe, hV, h, "qf" if l == 0 else f"q{l - 1}")
                    if l:
                        wait(pe, hP, h, f"k{l - 1}")
                    for i in range(NPT):
                        qv = Q[:, P * i:P * i + P].rearrange("p (b z w) -> p b z w", z=2, w=w)[:, :, 1, :]
                        ins = mmul(ps[:, 6 + l % 2, 64 * i:64 * i + 64].rearrange("p (b w) -> p b w", w=w),
                                   K[:, P * i:P * i + P], qv, start=True, stop=True)
                    if l < 2:
                        qv = Q[:, SEQ:T].rearrange("p (b z w) -> p b z w", z=2, w=w)[:, :, 1, :]
                        ins = mmul(ps[0:TS, 5, 288 + 16 * l:304 + 16 * l].rearrange("p (b w) -> p b w", w=w),
                                   K[:, SEQ:T], qv, start=True, stop=True)
                    ins.then_inc(inc, 1)
                    if l < 3:
                        feat(j, n0 % 2, 0, hT_, (l + 1, 4))
                    else:
                        tiles = range(2 * (l - 3), 2 * (l - 2) if l < LEVELS - 1 else NT)
                        ins = row_major(j + 1, (n0 + 1) % 2, hT, [(i, rows(i)) for i in tiles],
                                        lambda i, m: ps[0:m, 3 + i // 4, P * (i % 4):P * (i % 4) + P])
                ins.then_inc(inc, 1)
                used(j + 1)

                def fill(a):
                    if not last:
                        if a == 0:
                            wait(pe, hV, h, "g")
                        feat(j + 2, n0 % 2, 0, hQ, (a, 4))

                wait(pe, hV, h, f"q{LEVELS - 1}")
                wait(pe, hP, h, f"k{LEVELS - 1}")
                for i in range(NPT):
                    nc.tensor.transpose(ps[:, 6 + i // 4, P * (i % 4):P * (i % 4) + P], K[:, P * i:P * i + P], ident)
                wait(pe, hV, h, "v")
                nc.tensor.transpose(ps[0:TS, 5, P:2 * P], K[:, SEQ:T], ident).then_inc(inc, 1)
                fill(0)
                wait(pe, hA, h, "kr")
                for i in range(NPT):
                    ins = mmul(ps[:, 6 + i // 4, P * (i % 4):P * (i % 4) + P], KR[:, i, :], V[:, i, :],
                               start=True, stop=True)
                ins.then_inc(inc, 1)
                fill(1)
                wait(pe, hV, h, f"s{NPT - 1}")
                for z in range(2):
                    ins = mmul(ps[:, 6 + z, :], KR[0:TS, 8, :], VM[0:TS, 512 * z:512 * z + 512], start=True, stop=True)
                ins.then_inc(inc, 1)
                for i in range(NPT):
                    out = ps[:, 3 + i // 4, P * (i % 4):P * (i % 4) + P]
                    mmul(out, V[:, i, :], att[:, P * i:P * i + P], start=True, stop=i == 0)
                    if i:
                        mmul(out, S[:, i - 1, :], Q[:, P * i:P * i + P], start=False, stop=True)
                mmul(ps[:, 5, 0:TS], V[0:TS, 8, :], att[0:TS, SEQ:T], start=True, stop=False, skip_group_check=True)
                for b in range(NB):
                    ins = mmul(ps[:, 5, TQ * b:TQ * b + TQ], S0[:, P * b:P * b + P], Q[:, SEQ + TQ * b:SEQ + TQ * b + TQ],
                               start=False, stop=b == NB - 1, skip_group_check=True)
                ins.then_inc(inc, 1)
                fill(2)
                wait(pe, hA, h, "o2")
                wait(pe, hV, h, "sd")
                for b in range(2):
                    mmul(ps[:, 6 + b, :], ones[:, :], O2[:, 512 * b:512 * b + 512], start=True, stop=True)
                mmul(ps[:, 5, 64:64 + TS], ones[:, :], O2[:, SEQ:T], start=True, stop=True).then_inc(inc, 1)
                fill(3)
                if not last:
                    wait(pe, hV, h, "o")
                    feat(j + 3, (n0 + 1) % 2, 3, hZ)
                wait(pe, hV, h, "lo")

            def ffn(L, first_out):
                def chunk(r, c_par, jg, ju, slots, prev):
                    pe.wait_ge(w_lo, jg + 1)
                    if prev is not None or L:
                        wait(pe, fA, r - 1, "silu")
                    G0, so = prev if prev is not None else (None, None)
                    g = 0
                    for m in range(144):
                        if m == 72:
                            pe.wait_ge(w_lo, ju + 1)
                            if prev is not None or L:
                                wait(pe, fV, r - 1, "mul")
                        ins = feat_mm(slots[0], 0, m) if m < 72 else feat_mm(slots[2], 3, m - 72)
                        if m == 71:
                            ins.then_inc(fT.sem, 1)
                        if prev is not None and m >= 34 and (m - 34) % 6 == 0 and g < OUTG:
                            if g == 0:
                                pe.wait_ge(w_lo, jg + 2)
                                wait(pe, fV, r - 1, "lo")
                            out_group(G0 + g, g // 2, g % 2, [(1 - c_par, so)])
                            g += 1
                    assert prev is None or g == OUTG
                    ins.then_inc(fT.sem, 1)
                    wait(pe, fT, r, "u")
                    pe.sem_inc(w_used, 3 if prev is not None else 2)

                F0 = FFN0[L]
                norms(NORM_FFN[L], out=first_out)
                chunk(NCH * L, 0, F0, F0 + 1, EVEN, None)
                with pe.Fori(0, (NCH - 2) // 2) as it:
                    for z in range(2):
                        jg = 6 * it + (F0 + 2 + 3 * z)
                        slots = EVEN if z else ODD
                        chunk(2 * it + (1 + z + NCH * L), 1 - z, jg, jg + 2, slots,
                              (2 * OUTG * it + OUTG * (z + FOUT0[L]), slots[1]))
                jg = F0 + 3 * (NCH - 1) - 1
                chunk(NCH * L + NCH - 1, 1, jg, jg + 2, ODD, (OUTG * (FOUT0[L] + NCH - 2), ODD[1]))
                wait(pe, fV, NCH * L + NCH - 1, "lo")

            pe.wait_ge(small_in, 32)
            pe.wait_ge(init, 1)
            last_out = None
            for L in range(2):
                norms(NORM_MIX[L], mem=True, out=last_out)
                J = MIX0[L]
                pe.wait_ge(w_lo, J + 2)
                for h in range(2):
                    for k in range(KT):
                        for q, (a, b) in enumerate(PASS):
                            ins = mmul(ps[:, 0, N_MEM * h:N_MEM * (h + 1)], slot(a, h)[:, P * k:P * k + P],
                                       memT[b][:, k, :], start=k == 0 and q == 0, stop=k == KT - 1 and q == 2)
                    ins.then_inc(w_used, 1)
                pe.drain().then_inc(mT.sem, 1)
                for h in range(2):
                    row_major(J + 2 + h, h, memT, [(0, P), (1, P)],
                              lambda i, m: ps[:, 1, 256 * i + P * h:256 * i + P * h + P]).then_inc(w_used, 1)
                pe.drain().then_inc(mT.sem, 1)
                wait(pe, mA, L, "sq")
                mmul(ps[:, 2, :], cst[:, C_BLK:C_BLK + P], prob[:, 0:512], start=True, stop=True).then_inc(mT.sem, 1)
                wait(pe, mV, L, "k")
                for i in range(2):
                    for h in range(2):
                        ins = nc.tensor.transpose(ps[:, 3, 256 * i + P * h:256 * i + P * h + P],
                                                  kmem[:, h, P * i:P * i + P], ident)
                ins.then_inc(mT.sem, 1)
                wait(pe, mV, L, "rows")
                J += J_MQ
                feat(J, 0, 3, qT)
                feat(J + 1, 1, 0, qT)
                head_sums([0, 1][L])
                pair(L, False, [(J + 2, 0, hZ), (J + 3, 1, hQ)] if L == 0 else [(J + 2, 0, qT), (J + 3, 1, qT)])
                outs(OUT0[L], J + 4, [(0, 0), (1, 1)])
                pe.wait_ge(x_added, (OUT0[L] + 1) * OUTG)
                J += 6
                if L == 0:
                    for h in range(HEADS):
                        hgrn_head(h, J)
                        n = 4 if h < HEADS - 1 else 2
                        o = (OUT0[0] + 1 + h, J + n, [(0, (J + n) % 2)])
                        if h < HEADS - 1:
                            outs(*o)
                            pe.wait_ge(x_added, (OUT0[L] + 2 + h) * OUTG)
                        J += HGRN_JOBS
                    ffn(L, o)
                else:
                    head_sums(2)
                    wait(pe, qV, 2, "n1")
                    for half in range(2):
                        row_major(J + half, half, hT, [(i, rows(i)) for i in range(NT)],
                                  lambda i, m: ps[0:m, i // 2, 256 * (i % 2) + P * half:256 * (i % 2) + P * half + P])
                        used(J + half)
                    pe.drain().then_inc(kT.sem, 1)
                    for h in range(2):
                        nc.tensor.transpose(ps[:, 5, P * h:P * h + P], kpad[:, h, SEQ:SEQ + P], ident)
                        ins = nc.tensor.transpose(ps[0:TS, 5, 256 + P * h:256 + P * h + P],
                                                  kpad[:, h, WIN + SEQ:WIN + T], ident)
                    ins.then_inc(kT.sem, 1)
                    wait(pe, kV, 0, "rows")
                    J += 2
                    feat(J, 0, 3, qT)
                    feat(J + 1, 1, 0, qT)
                    head_sums(3)
                    J += 2
                    for g in range(QG):
                        more = g < QG - 1
                        pair(2 + g, True, [(J, 0, qT), (J + 1, 1, qT)] if more else None)
                        J += 2 if more else 0
                        o = (OUT0[1] + 1 + g, J, [(0, 0), (1, 1)])
                        if more:
                            outs(*o)
                            pe.wait_ge(x_added, (OUT0[L] + 2 + g) * OUTG)
                            head_sums(4 + g)
                        J += 2
                    ffn(L, o)
                last_out = (FOUT0[L] + NCH - 1, FFN0[L] + FFN_JOBS - 1, [(1, EVEN[0])])
            outs(*last_out)


_SHAPES = dict(
    y_prompt=(1, SEQ, D), y_sample=(NB, TQ, D), new_mem_k=(2, 1, N_MEM, 4, HD), new_mem_v=(2, 1, N_MEM, 4, HD),
    new_hg_p=(1, 1, HEADS, P, P), new_hg_s=(1, NB, HEADS, P, P), new_swk_p=(1, 1, WIN, 4, HD),
    new_swv_p=(1, 1, WIN, 4, HD), new_swk_s=(1, NB, WIN, 4, HD), new_swv_s=(1, NB, WIN, 4, HD))
_INS = ['x_prompt', 'x_sample', 'cache_mem_k', 'cache_mem_v', 'state_hgrn', 'cache_swa_k', 'cache_swa_v',
        'mem_prompt', 'w_in_hgrn', 'w_in_swa', 'w_mem_kv', 'w_out', 'w_ffn_in', 'w_ffn_out']


def _params(a):
    cols = [np.asarray(a[n]).reshape(2 * KT, P).T for n in ('norm_mix', 'norm_ffn', 'norm_mem')]
    cols += [np.asarray(a[n]).reshape(HEADS, P).T for n in ('hgrn_out_norm', 'hgrn_lb_raw')]
    cols += [np.tile(np.asarray(a[n]), (1, 2)).T for n in ('swa_q_norm', 'swa_k_norm', 'mem_q_norm', 'mem_k_norm')]
    sinks = np.asarray(a['swa_sinks']).reshape(1, 12)
    cols += [np.broadcast_to(sinks, (P, 12))]
    cols += [np.tile(np.repeat(sinks.reshape(4, QG), TQ, axis=0), (NB, 1))]
    return np.ascontiguousarray(np.concatenate(cols, axis=1))


def kernel(**inputs):
    import concourse.bacc as _bacc
    from concourse.bass_utils import run_bass_kernel_spmd as _run

    nc = _bacc.Bacc("TRN2", target_bir_lowering=False, num_devices=1,
                     dynamic_dma_scratch_size=1024)
    arrays, args = {}, []
    data = [(n, np.ascontiguousarray(inputs[n])) for n in _INS]
    data += [("constants", constants()), ("params", _params(inputs))]
    for name, a in data:
        arrays[f"in_{name}_dram"] = a
        args.append(nc.dram_tensor(f"in_{name}_dram", a.shape, mybir.dt.from_np(a.dtype), kind="ExternalInput").ap())
    for name, shape in _SHAPES.items():
        args.append(nc.dram_tensor(f"out_{name}_dram", shape, F32, kind="ExternalOutput").ap())
    hybrid_step(nc, *args)
    r = _run(nc, [arrays], core_ids=[0])
    return tuple(r.results[0][f"out_{name}_dram"] for name in _SHAPES)
```

```python
from contextlib import ExitStack

import numpy as np

import concourse.bass as bass
from concourse import mybir

F32 = mybir.dt.float32
F32R = mybir.dt.float32r
I32 = mybir.dt.int32
ACT = mybir.ActivationFunctionType
ALU = mybir.AluOpType
AX = mybir.AxisListType

P = 128
D = 1024
KT = D // P
SEQ, NB, TQ = 1024, 8, 4
TS = NB * TQ
T = SEQ + TS
NPT = SEQ // P
NT = NPT + 1
N_MEM, HD = 256, 64
HEADS = 6
TOK = HEADS * P
DFF = 2816
NCH = DFF // P
WIN = 128
EPS = 1e-6
NEG = -1e30
TG = 3
TW = T // TG
LEVELS = 7
QG = 3
NPAIR = 1 + 1 + QG

C_ID, C_BLK, C_LVL = 0, P, 2 * P
C_BAND = C_LVL + LEVELS * 64
C_SROW = C_BAND + 2 * 256
C_QB = C_SROW + 160
C_VM = C_QB + 2 * NB * 8
C_END = C_VM + NB

S_MIX, S_FFN, S_MEM = 0, 2 * KT, 4 * KT
S_GN = 6 * KT
S_LB = S_GN + HEADS
S_SQ, S_SK = S_LB + HEADS, S_LB + HEADS + 1
S_MQ, S_MK = S_SK + 1, S_SK + 3
S_SINK = S_MK + 2
S_SROW = S_SINK + 12
S_END = S_SROW + 3
S_L, S_ML, S_GQ = S_END, S_END + HEADS, S_END + 2 * HEADS
S_NS = S_GQ + 3
S_EPS = S_NS + 12
S_ALL = S_EPS + 1


def constants():
    c = np.zeros((P, C_END), np.float32)
    p = np.arange(P)
    c[:, C_ID:C_ID + P] = np.eye(P)
    c[:, C_BLK:C_BLK + P] = (p[:, None] // HD == p[None] // HD)
    for l in range(LEVELS):
        w = 1 << l
        t = np.array([t for t in range(P) if (t // w) % 2 == 1])
        ok = (p[:, None] // (2 * w) == t[None] // (2 * w)) & ((p[:, None] // w) % 2 == 0)
        c[:, C_LVL + 64 * l:C_LVL + 64 * l + 64] = ok
    r = np.arange(2 * WIN)[None]
    band = (r > p[:, None]) & (r <= p[:, None] + WIN)
    c[:, C_BAND:C_BAND + 256] = np.where(band & (r >= WIN), 0, NEG)
    c[:, C_BAND + 256:C_BAND + 512] = np.where(band, 0, NEG)
    b, q = p[:, None] // 16, p[:, None] % 4
    r = np.arange(160)[None]
    old = (r < WIN) & (r > q)
    new = (r >= WIN) & ((r - WIN) // TQ == b) & ((r - WIN) % TQ <= q)
    c[:, C_SROW:C_SROW + 160] = np.where(old | new, 0, NEG)
    m = np.zeros((P, 2, NB, 2, 4), np.float32)
    for half in range(2):
        for bb in range(NB):
            for h2 in range(2):
                m[64 * h2:64 * h2 + 64, half, bb, bb % 2, 2 * half + h2] = 1
    c[:, C_QB:C_VM] = m.reshape(P, -1)
    c[:TS, C_VM:] = (np.arange(TS)[:, None] // TQ == np.arange(NB)[None])
    return c


class Steps:

    def __init__(self, sem, names):
        self.sem, self.names, self.len = sem, names, len(names)

    def at(self, n, name):
        return n * self.len + (self.names.index(name) + 1)


MEM_JOBS, PAIR_JOBS, HGRN_JOBS, SWKV_JOBS = 4, 4, 5, 4
MIX_JOBS = [MEM_JOBS + PAIR_JOBS + HGRN_JOBS * HEADS, MEM_JOBS + PAIR_JOBS + SWKV_JOBS + QG * PAIR_JOBS]
FFN_JOBS = 3 * NCH
MIX0 = [0, MIX_JOBS[0] + FFN_JOBS]
FFN0 = [MIX0[0] + MIX_JOBS[0], MIX0[1] + MIX_JOBS[1]]
USED0 = [0, MIX_JOBS[0]]
ODD, EVEN = (0, 4, 1), (2, 5, 3)
LAST_SLOT = EVEN[2]
NRAW = 3
OUTG = 2 * NT
J_MQ, J_FILL, J_MO, J_TOK = MEM_JOBS, MEM_JOBS + 2, MEM_JOBS + 4, MEM_JOBS + 6
MIX_OUTS = [1 + HEADS, 1 + QG]
OUT0 = [0, MIX_OUTS[0] + NCH]
FOUT0 = [MIX_OUTS[0], OUT0[1] + MIX_OUTS[1]]
NORM_MIX = [0, 2 * NT + 2]
NORM_FFN = [NT + 2, 3 * NT + 4]
U_KEYS = 2


INIT = 6
C_SD, C_SL = 384, 416
C_HS, C_HR = TW, TW + 2 * TS
EOFF = [sum((T if l < 3 else SEQ) >> l for l in range(n)) for n in range(LEVELS + 1)]
NS0 = 2 + 2 * HEADS
NSTORE = NS0 + 2 + 2 + 2 * NB + 2


def rows(i):
    return P if i < NPT else TS


def hybrid_step(nc, x_prompt, x_sample, cache_mem_k, cache_mem_v, state_hgrn, cache_swa_k, cache_swa_v,
                mem_prompt, w_in_hgrn, w_in_swa, w_mem_kv, w_out, w_ffn_in, w_ffn_out, consts, params,
                y_prompt, y_sample, new_mem_k, new_mem_v, new_hg_p, new_hg_s,
                new_swk_p, new_swv_p, new_swk_s, new_swv_s):
    with ExitStack() as ctx:
        def sb(name, cols, dt=F32):
            return ctx.enter_context(nc.sbuf_tensor(name, [P, cols], dt))

        def sem(name):
            return ctx.enter_context(nc.semaphore(name))

        x = sb("x", NT * D)[:, :].rearrange("p (i d) -> p i d", i=NT)
        hT = [sb("hT_hi", KT * T, F32R)[:, :].rearrange("p (k t) -> p k t", k=KT),
              sb("hT_lo", KT * T, F32R)[:, :].rearrange("p (k t) -> p k t", k=KT)]
        raw = sb("w_raw", NRAW * D)[:, :].rearrange("p (s n) -> p s n", s=NRAW)
        w01 = [sb("w_hi01", 2 * D, F32R), sb("w_lo01", 2 * D, F32R)]
        mm = [sb("m_hi", 2 * T, F32R)[:, :].rearrange("p (a t) -> p a t", a=2),
              sb("m_lo", 2 * T, F32R)[:, :].rearrange("p (a t) -> p a t", a=2)]
        cst = sb("consts", C_END)
        par = sb("params", S_ALL)
        nstat = sb("norm_stats", 40)
        nrstd = sb("norm_rstd", 40)

        ARENA = 71328
        slab = ctx.enter_context(nc.sbuf_tensor("arena", [P, ARENA // 4], F32))
        base = nc.sbuf_base - ARENA

        def at(name, off, cols, dt=F32):
            assert off + 4 * cols <= ARENA, name
            return nc.alloc_sbuf_tensor_at(name, [P, cols], dt, offset=base + off)

        w25 = [at("w_hi25", 0, 4 * D, F32R), at("w_lo25", 16384, 4 * D, F32R)]
        sg = at("gate_silu", 32768, T)
        gated = at("gated", 36992, T)
        xn = at("normed", 41216, 2 * D)[:, :].rearrange("p (a d) -> p a d", a=2)
        NORM_END = 53504
        gained = [at("normed_gained0", 49408, D), at("normed_gained1", NORM_END + 8192, D)]
        xmem = at("mem_rows", NORM_END, 2 * D)[:, :].rearrange("p (i d) -> p i d", i=2)
        memT = [at("memT_hi", 24832, KT * N_MEM, F32R)[:, :].rearrange("p (k t) -> p k t", k=KT),
                at("memT_lo", 8192, KT * N_MEM, F32R)[:, :].rearrange("p (k t) -> p k t", k=KT)]
        HS = at("q_row_rstd", 15936, 4 * 2 * NPT)
        prob = at("prob", 16384, T)
        probT = at("probT", 20608, T)
        prob2 = at("prob2", 9472, T)
        orow = at("attn_rows", 13568, 4 * P)[:, :].rearrange("p (i c) -> p i c", i=4)
        st = at("attn_round_stats", 15616, 4 * 20)
        qh = at("q_heads", 24832, 2 * T)[:, :].rearrange("p (a t) -> p a t", a=2)
        kmem = at("k_mem", 33280, 2 * N_MEM)[:, :].rearrange("p (a m) -> p a m", a=2)
        vmem = at("v_mem", 35328, 2 * N_MEM)[:, :].rearrange("p (i c) -> p i c", i=2)
        kmem_sq = at("k_mem_squares", 37376, 2 * N_MEM)
        kmem_rstd = at("k_mem_rstd", 2048, 2 * N_MEM)
        ktok_mem = at("k_mem_rows", 0, 2 * N_MEM)[:, :].rearrange("p (i c) -> p i c", i=2)
        qblk = at("q_blocks", 37376, 2 * NB * 32)[:, :].rearrange("p (a b c) -> p a b c", a=2, b=NB)
        sprob = at("sample_prob", 39424, 256)
        sprobT = at("sample_probT", 40448, 256)[:, :].rearrange("p (c r) -> p c r", c=2)
        kcT = at("k_cacheT", 41472, 2 * 512)[:, :].rearrange("p (z n) -> p z n", z=2)
        ast = at("attn_stats", 45568, 40)
        cacheb = at("cache", 45728, NB * 512)
        kpad = at("k_window", 0, 2 * (P + T))[:, :].rearrange("p (a t) -> p a t", a=2)
        vwin = at("v_window", 62112, NT * 256)[:, :].rearrange("p (i c) -> p i c", i=NT)
        ktok = at("k_window_rows", 33280, 2 * 256)[:, :].rearrange("p (i c) -> p i c", i=2)
        Q = at("hg_q", 0, T)
        K = at("hg_k", 4224, T)
        E = at("hg_decay", 8448, 2096)
        tA = at("hg_sig", 16832, T)
        G = at("hg_gate", 21056, T)
        V = at("hg_v", 25280, NT * P)[:, :].rearrange("p (i c) -> p i c", i=NT)
        att = at("hg_att", 29888, T)
        KR = at("hg_k_rows", 34112, NT * P)[:, :].rearrange("p (i c) -> p i c", i=NT)
        O2 = at("hg_o_square", 38720, T)
        VF = at("hg_v_features", 42944, T)
        VM = at("hg_v_blocks", 47168, NB * P)
        ones = at("ones", 51264, 1)
        S = at("hg_states", NORM_END, NPT * P)[:, :].rearrange("p (i c) -> p i c", i=NPT)
        S0 = at("hg_state_in", NORM_END + 4096, NB * P)
        SN = at("hg_state_out", NORM_END + 8192, NB * P)
        HR = at("hg_row_rstd", NORM_END + 12288, 2 * NT)

        ps = ctx.enter_context(nc.psum_tensor("ps", [P, 8, 512], F32))

        raw_loaded = [sem(f"raw_loaded{s}") for s in range(NRAW)]
        w_hi, w_lo, w_used = sem("w_hi"), sem("w_lo"), sem("w_used")
        small_in, masks_in, mem_in, side_in = sem("small_in"), sem("masks_in"), sem("mem_in"), sem("side_in")
        x_in = [sem(f"x_in{i}") for i in range(NT)]
        stored, stored_y = sem("stored"), sem("stored_y")
        out_ready, x_added = sem("out_ready"), sem("x_added")
        init, lb_exp = sem("init"), sem("lb_exp")
        nA, nH = Steps(sem("norm_stats_act"), ["sq", "std"]), Steps(sem("norm_hi"), ["hi"])
        nV, nG = Steps(sem("norm_rows_vec"), ["rstd", "xn"]), Steps(sem("norm_gain_vec"), ["g0", "g1"])
        nT, nP = Steps(sem("norm_pe"), ["tr"]), Steps(sem("norm_pool"), ["lo"])
        fT, fA, fV = (Steps(sem("ffn_pe"), ["g", "u"]), Steps(sem("ffn_act"), ["silu", "hi"]),
                      Steps(sem("ffn_vec"), ["mul", "lo"]))
        mT = Steps(sem("memkv_pe"), ["k", "v", "ssq", "rows"])
        mA = Steps(sem("memkv_act"), ["sq", "std"])
        mV = Steps(sem("memkv_vec"), ["g", "v", "rstd", "k", "rows"])
        qT, qA, qV = (Steps(sem("headnorm_pe"), ["proj0", "proj1", "ssq0", "ssq1"]),
                      Steps(sem("headnorm_act"), ["sq0", "sq1", "std0", "std1"]),
                      Steps(sem("headnorm_vec"), ["g0", "g1", "rstd0", "n0", "rstd1", "n1"]))
        aSC, aPT, aPV, aOT = (Steps(sem("scores_pe"), ["sc"]), Steps(sem("probT_pe"), ["pt"]),
                              Steps(sem("attn_rows_pe"), ["pv"]), Steps(sem("attn_turn_pe"), ["ot"]))
        aE, aSK, aC = (Steps(sem("exp_act"), ["exp"]), Steps(sem("sink_act"), ["sink"]),
                       Steps(sem("probT_act"), ["pt"]))
        vM, vS, vD, vR, vC, vO, vOT = (Steps(sem("max_vec"), ["max", "neg"]), Steps(sem("scaled_max_vec"), ["max"]),
                                       Steps(sem("den_vec"), ["den"]),
                                   Steps(sem("rinv_vec"), ["rinv"]), Steps(sem("probT_vec"), ["pt"]),
                                   Steps(sem("attn_rows_vec"), ["o"]), Steps(sem("attn_turn_vec"), ["ot"]))
        sT = Steps(sem("sample_pe"), [f"kt{b}" for b in range(NB)] + ["sc", "pt", "pv"])
        sA = Steps(sem("sample_act"), [f"kt{b}" for b in range(NB)] + ["exp", "sink"])
        sV = Steps(sem("sample_vec"), ["qb", "max", "neg", "den", "rinv", "p", "pt", "o0", "o1"])
        oA, oV = Steps(sem("pair_out_act"), ["hi"]), Steps(sem("pair_out_vec"), ["lo"])
        kT, kV = Steps(sem("window_pe"), ["v", "rows"]), Steps(sem("window_vec"), ["pad", "v", "rows"])
        hQ, hZ = Steps(sem("hgrn_query_pe"), ["q"]), Steps(sem("hgrn_forget_pe"), ["z"])
        hT_ = Steps(sem("hgrn_pe"), ["diag", "l0", "l1", "l2", "g", "l3", "l4", "l5", "l6", "v",
                                     "kr", "vr", "ds", "ds8", "o", "ssq"])
        hA = Steps(sem("hgrn_act"), ["sq", "f", "k", "e", "ks", "sg", "vf", "kr", "hi", "o2", "std"])
        hV = Steps(sem("hgrn_vec"), ["q", "diag", "qf"]
                   + [f"{s}{l}" for l in range(LEVELS) for s in "aq"] + ["g", "v", "vm"]
                   + [f"s{i}" for i in range(NPT)] + ["sn", "sd", "m", "lo", "rstd"])
        hP = Steps(sem("hgrn_pool"), [f"{s}{l}" for l in range(LEVELS) for s in "ke"])
        block = ctx.enter_context(nc.Block())

        ident = cst[:, C_ID:C_ID + P]

        def col(c, n=1):
            return par[:, c:c + n]

        def slot(which, s):
            t = w01[which][:, s * D:(s + 1) * D] if s < 2 else w25[which][:, (s - 2) * D:(s - 1) * D]
            return t

        def wait(eng, steps, n, name):
            eng.wait_ge(steps.sem, steps.at(n, name))

        def row_scale(r, i):
            half, q, h2 = r % 8 // 4, r // 2 % 2, r % 2
            return 4 * NPT + 2 * NPT * half + 2 * (4 * q + i) + h2

        def fm(b0, n=TW):
            return ps[:, b0:b0 + TG, 0:n]

        def three(t):
            return t.rearrange("p (g n) -> p g n", g=TG)

        def w_cols(w, c0, s):
            v, dst = w.rearrange("(k p) n -> p k n", p=P), raw[:, s, :].rearrange("p (k n) -> p k n", k=KT)
            return [(dst[:, 0:4], v[:, 0:4, c0:c0 + P]), (dst[:, 4:8], v[:, 4:8, c0:c0 + P])]

        def w_two_heads(w, ha, hb, s):
            v, dst = w.rearrange("(k p) n -> p k n", p=P), raw[:, s, :].rearrange("p (k n) -> p k n", k=KT)
            return [(dst[:, :, 64 * z:64 * z + 64], v[:, :, 64 * h:64 * h + 64]) for z, h in enumerate((ha, hb))]

        def w_rows(w, ra, rb, s):
            return [(raw[0:64, s, :], w[ra:ra + 64]), (raw[64:P, s, :], w[rb:rb + 64])]

        def mixer_jobs(L):
            wm = w_mem_kv[L]
            jobs = [lambda s, c=c: w_cols(wm, c * P, s) for c in range(4)]
            win, c0 = (w_in_hgrn[0], 4 * TOK) if L == 0 else (w_in_swa[0], 5 * 256)
            jobs += [lambda s, h=h: w_cols(win, c0 + h * P, s) for h in range(2)]
            mem_out = [lambda s, h=h: w_rows(w_out[L], TOK + h * P, TOK + h * P + 64, s) for h in range(2)]
            if L == 0:
                cols = lambda kind, h: [lambda s: w_cols(win, "qfvg".index(kind) * TOK + h * P, s)]
                jobs += cols("f", 0) + cols("q", 0) + mem_out
                for h in range(HEADS):
                    jobs += cols("g", h) + cols("v", h)
                    if h < HEADS - 1:
                        jobs += cols("q", h + 1) + cols("f", h + 1)
                    jobs += [lambda s, h=h: w_rows(w_out[L], h * P, h * P + 64, s)]
            else:
                heads = [[(3 * 2 * half + g, 3 * (2 * half + 1) + g) for half in range(2)] for g in range(QG)]
                queries = lambda g: [lambda s, hh=hh: w_two_heads(win, hh[0], hh[1], s) for hh in heads[g]]
                jobs += [lambda s, c=c: w_cols(win, TOK + c * P, s) for c in range(2)] + mem_out
                jobs += [lambda s, c=c: w_cols(win, TOK + c * P, s) for c in range(2, 4)] + queries(0)
                for g in range(QG):
                    if g < QG - 1:
                        jobs += queries(g + 1)
                    jobs += [lambda s, hh=hh: w_rows(w_out[L], 64 * hh[0], 64 * hh[1], s) for hh in heads[g]]
            assert len(jobs) == MIX_JOBS[L]
            return jobs

        def ffn_job(L, kind, c, s):
            if kind == "o":
                w = w_ffn_out[L]
                return [(raw[64 * z:64 * z + 64, s, :], w[bass.ds(c * P + 64 * z, 64)]) for z in range(2)]
            v = w_ffn_in[L].rearrange("(k p) n -> p k n", p=P)
            dst = raw[:, s, :].rearrange("p (k n) -> p k n", k=KT)
            c0 = c * P + (DFF if kind == "u" else 0)
            return [(dst[:, 4 * z:4 * z + 4], v[:, 4 * z:4 * z + 4, bass.ds(c0, P)]) for z in range(2)]

        @block.sync
        def _(sp):
            def load(j3, n3, jv, parts):
                if not (isinstance(jv, int) and jv < NRAW):
                    sp.wait_ge(w_hi, jv - 2)
                    sp.wait_ge(w_lo, jv - 2)
                for dst, src in parts(j3):
                    sp.dma_start(dst, src).then_inc(raw_loaded[j3], 16)

            def store(dst, src):
                sp.dma_start(dst, src).then_inc(stored, 16)

            def cache_rows(c, L, n):
                return c[L].rearrange("b (i p) h d -> p b i (h d)", p=P)

            def load_mem():
                sp.dma_start(xmem, mem_prompt[0].rearrange("(i p) d -> p i d", p=P)).then_inc(mem_in, 16)

            def load_x(i):
                src = x_prompt[0, i * P:(i + 1) * P, :] if i < NPT else x_sample.rearrange("b t d -> (b t) d")
                sp.dma_start(x[0:rows(i), i, :], src).then_inc(x_in[i], 16)

            sp.dma_start(par[:, 0:S_END], params).then_inc(small_in, 16)
            sp.dma_start(cst[:, 0:C_LVL], consts[:, 0:C_LVL]).then_inc(small_in, 16)
            load_mem()
            load_x(0)
            sp.dma_start(cst[:, C_LVL:C_END], consts[:, C_LVL:C_END]).then_inc(masks_in, 16)
            for i in range(1, NT):
                load_x(i)
            for L in range(2):
                if L == 1:
                    sp.wait_ge(stored, 16 * NS0)
                    wait(sp, hT_, HEADS - 1, "o")
                    load_mem()
                jobs = mixer_jobs(L)
                for n, job in enumerate(jobs):
                    j = MIX0[L] + n
                    if n == J_MQ + 2:
                        wait(sp, nH, NORM_MIX[L] + NT + 1, "hi")
                        wait(sp, nP, NORM_MIX[L] + NT + 1, "lo")
                        for z in range(2):
                            sp.dma_start(cacheb[:, :].rearrange("p (b i c) -> p b i c", b=NB, i=2)[:, 4 * z:4 * z + 4],
                                         cache_rows(cache_mem_k, L, 2)[:, 4 * z:4 * z + 4]).then_inc(side_in, 16)
                    if n == J_MO:
                        wait(sp, mV, L, "rows")
                        for z, (t, d) in enumerate(((ktok_mem, new_mem_k), (vmem, new_mem_v))):
                            store(d[L, 0].rearrange("(i p) h d -> p i (h d)", p=P), t)
                    if n == J_TOK:
                        if L == 1:
                            wait(sp, sT, 1, "pv")
                            for z, cc in enumerate((cache_swa_k, cache_swa_v)):
                                sp.dma_start(cacheb[:, z * 2048:(z + 1) * 2048].rearrange("p (b c) -> p b c", b=NB),
                                             cc[0].rearrange("b p h d -> p b (h d)")).then_inc(side_in, 16)
                    if L == 0 and n >= J_TOK and (n - J_TOK) % HGRN_JOBS == 0:
                        h = (n - J_TOK) // HGRN_JOBS
                        if h == 0:
                            wait(sp, sT, 0, "pv")
                        else:
                            wait(sp, hV, h - 1, "sd")
                            store(new_hg_p[0, 0, h - 1], S[:, NPT - 1, :])
                            store(new_hg_s[0, :, h - 1].rearrange("b c v -> c b v"),
                                  SN[:, :].rearrange("p (b v) -> p b v", b=NB))
                            wait(sp, hT_, h - 1, "o")
                        sp.dma_start(S0[:, :].rearrange("p (b v) -> p b v", b=NB),
                                     state_hgrn[0, :, h].rearrange("b c v -> c b v")).then_inc(side_in, 16)
                    load(j % 3, j // 3, j, job)
                if L == 0:
                    wait(sp, hV, HEADS - 1, "sd")
                    store(new_hg_p[0, 0, HEADS - 1], S[:, NPT - 1, :])
                    store(new_hg_s[0, :, HEADS - 1].rearrange("b c v -> c b v"),
                          SN[:, :].rearrange("p (b v) -> p b v", b=NB))
                else:
                    wait(sp, kV, 0, "rows")
                    store(new_swk_p[0, 0].rearrange("w h d -> w (h d)"), ktok[:, 0, :])
                    store(new_swv_p[0, 0].rearrange("w h d -> w (h d)"), vwin[:, NPT - 1, :])
                    for b in range(NB):
                        store(new_swk_s[0, b, WIN - TQ:].rearrange("w h d -> w (h d)"),
                              ktok[TQ * b:TQ * b + TQ, 1, :])
                        store(new_swv_s[0, b, WIN - TQ:].rearrange("w h d -> w (h d)"),
                              vwin[TQ * b:TQ * b + TQ, NPT, :])
                    for z, (o, cc) in enumerate(((new_swk_s, cache_swa_k), (new_swv_s, cache_swa_v))):
                        store(o[0, :, 0:WIN - TQ].rearrange("b w h d -> b (w h d)"),
                              cc[0, :, TQ:].rearrange("b w h d -> b (w h d)"))
                j0 = FFN0[L]

                def ffn_load(d, kind, it, c):
                    j = j0 + d
                    load(j % 3, None, j + 3 * it, lambda s: ffn_job(L, kind, c, s))

                ffn_load(0, "g", 0, 0)
                ffn_load(1, "u", 0, 0)
                with sp.Fori(1, NCH) as c:
                    ffn_load(-1, "g", c, c)
                    ffn_load(0, "o", c, c - 1)
                    ffn_load(1, "u", c, c)
                ffn_load(-1, "o", NCH, NCH - 1)
            for i in range(NT):
                sp.wait_ge(x_added, (FOUT0[1] + NCH - 1) * OUTG + 2 * i + 2)
                dst = y_prompt[0, i * P:(i + 1) * P, :] if i < NPT else y_sample.rearrange("b t d -> (b t) d")
                sp.dma_start(dst, x[0:rows(i), i, :]).then_inc(stored_y, 16)
            sp.wait_ge(stored, 16 * NSTORE)
            sp.wait_ge(stored_y, 16 * NT)

        def mix_slot(L, n):
            return n % 2

        def split_free(L, n):
            return USED0[L] + n - 1 if n >= 2 else 0

        def hi_split(act, j3, n3, s, free):
            act.wait_ge(raw_loaded[j3], (n3 + 1) * 32)
            if not (isinstance(free, int) and free <= 0):
                act.wait_ge(w_used, free)
            nc.scalar.activation(slot(0, s), raw[:, j3, :], ACT.Copy).then_inc(w_hi, 1)

        def lo_split(pool, j3, jv, s):
            pool.wait_ge(w_hi, jv + 1)
            nc.gpsimd.tensor_tensor(slot(1, s), raw[:, j3, :], slot(0, s).bitcast(F32),
                                    ALU.subtract).then_inc(w_lo, 1)

        class Pump:

            def __init__(self, L, emit):
                self.L, self.n, self.emit = L, 0, emit

            def upto(self, n):
                while self.n < min(n, MIX_JOBS[self.L]):
                    j = MIX0[self.L] + self.n
                    self.emit(j, mix_slot(self.L, self.n), split_free(self.L, self.n))
                    self.n += 1

        def act_emit(act):
            return lambda j, s, free: hi_split(act, j % 3, j // 3, s, free)

        def pool_emit(pool):
            return lambda j, s, free: lo_split(pool, j % 3, j, s)

        def ffn_splits(L, split, it, c_par):
            slots = ODD if c_par else EVEN
            for k, d in enumerate((-1, 0, 1)):
                split(FFN0[L] + d, it, slots[k])

        @block.scalar
        def _(act):
            def A(out, in_, fn, steps, n, name, **kw):
                nc.scalar.activation(out, in_, fn, **kw).then_inc(steps.sem, 1)

            def norm_in(r, src, m):
                if r >= 2:
                    wait(act, nT, r - 2, "tr")
                A(xn[0:m, r % 2, :], src[0:m], ACT.Square, nA, r, "sq", accum_out=nstat[0:m, r:r + 1])
                wait(act, nA, r, "sq")
                A(nstat[0:m, r:r + 1], nstat[0:m, r:r + 1], ACT.Sqrt, nA, r, "std",
                  scale=1.0 / D, bias=col(S_EPS)[0:m])

            def norm_hi(r, dst, c0, m):
                wait(act, nG, r, "g1")
                A(dst[0][:, :, c0:c0 + m], gained[r % 2][:, 0:KT * m].rearrange("p (k t) -> p k t", k=KT),
                  ACT.Copy, nH, r, "hi")

            def norms(r0, first=None, mem=None):
                srcs = [(x[:, i, :], rows(i), hT, i * P) for i in range(NT)]
                if mem:
                    srcs = [(xmem[:, i, :], P, memT, i * P) for i in range(2)] + srcs
                for i in range(len(srcs) + 3):
                    if i < len(srcs):
                        src, m, dst, c0 = srcs[i]
                        t = i - 2 if mem else i
                        if t < 0:
                            act.wait_ge(mem_in, 16 * (2 if r0 else 1))
                        elif first is None:
                            act.wait_ge(x_in[t], 16)
                        else:
                            act.wait_ge(x_added, first * OUTG + 2 * t + 2)
                        norm_in(r0 + i, src, m)
                    if i >= 3:
                        src, m, dst, c0 = srcs[i - 3]
                        norm_hi(r0 + i - 3, dst, c0, m)
                    if mem:
                        mem(i)

            def mem_keys(L, pump, i):
                if i == 4 and L == 0:
                    pump.upto(2)
                if i == 7:
                    pump.upto(MEM_JOBS)
                if i == 8:
                    wait(act, mT, L, "k")
                    A(kmem_sq[:, :], ps[:, 4, :], ACT.Square, mA, L, "sq")
                if i == 11:
                    pump.upto(J_MQ + 1)
                if i == 12:
                    pump.upto(J_MQ + 2)
                    wait(act, mT, L, "ssq")
                    A(kmem_rstd[:, :], ps[:, 5, :], ACT.Sqrt, mA, L, "std", scale=1.0 / HD, bias=col(S_EPS))

            def head_squares(u):
                for z, t in enumerate((prob, prob2)):
                    wait(act, qT, u, f"proj{z}")
                    A(three(t[:, :]), fm(3 - 3 * z), ACT.Square, qA, u, f"sq{z}")

            def key_std(u, z):
                wait(act, qT, u, f"ssq{z}")
                nc.scalar.activation(probT[:, 0:SEQ].rearrange("p (b n) -> p b n", b=2), ps[:, 6:8, :], ACT.Sqrt,
                                     scale=1.0 / HD, bias=col(S_EPS))
                A(probT[:, SEQ:T], ps[:, 5 - 3 * z, TW:TW + TS], ACT.Sqrt, qA, u, f"std{z}",
                  scale=1.0 / HD, bias=col(S_EPS))

            def query_stds(u):
                wait(act, qT, u, "ssq1")
                n = 2 * NPT
                A(HS[:, 0:2 * n], ps[:, 5, C_HR:C_HR + 2 * n], ACT.Sqrt, qA, u, "std0", scale=1.0 / HD, bias=col(S_EPS))
                for z, t in enumerate((prob, prob2)):
                    ins = nc.scalar.activation(t[:, SEQ:T], ps[:, 5, C_HS + TS * z:C_HS + TS * (z + 1)], ACT.Sqrt,
                                               scale=1.0 / HD, bias=col(S_EPS))
                ins.then_inc(qA.sem, 1)

            def prompt_exp(r, sink):
                buf, s = (prob, prob2)[r % 2], 20 * (r % 4)
                wait(act, vM, r, "neg")
                if r >= 2:
                    wait(act, aPT, r - 2, "pt")
                if r >= 4:
                    wait(act, vO, r - 4, "o")
                for i in range(4):
                    src = ps[:, 2 * (r % 2) + i // 2, 256 * (i % 2):256 * (i % 2) + 256] if sink is None \
                        else buf[:, 256 * i:256 * i + 256]
                    ins = nc.scalar.activation(buf[:, 256 * i:256 * i + 256], src, ACT.Exp,
                                               bias=st[:, s + 4 + i:s + 5 + i],
                                               scale=HS[:, row_scale(r, i):row_scale(r, i) + 1],
                                               accum_out=st[:, s + 8 + i:s + 9 + i])
                ins.then_inc(aE.sem, 1)
                if sink is not None:
                    A(st[:, s + 12:s + 16], st[:, s + 4:s + 8], ACT.Exp, aSK, r, "sink", bias=sink)

            def prompt_turn(r):
                wait(act, aPT, r, "pt")
                if r >= 1:
                    wait(act, aPV, r - 1, "pv")
                A(probT[:, 0:512], ps[:, 4, :], ACT.Copy, aC, r, "pt")

            def sample_attn(p, sink):
                n = 1 if sink is not None else 2
                for b in range(NB):
                    wait(act, sT, p, f"kt{b}")
                    A(kcT[:, b % 2, 0:256 * n], ps[:, 6 + b % 2, 0:256 * n], ACT.Copy, sA, p, f"kt{b}")
                if sink is None:
                    for z in range(2):
                        act.dma_start(cacheb[:, :].rearrange("p (b i c) -> p b i c", b=NB, i=2)[:, 4 * z:4 * z + 4],
                                      cache_mem_v[p].rearrange("b (i p) h d -> p b i (h d)", p=P)[:, 4 * z:4 * z + 4]
                                      ).then_inc(side_in, 16)
                wait(act, sV, p, "neg")
                w = 256 if sink is None else 160
                A(sprob[:, 0:w], ps[:, 0, 0:w] if sink is None else sprob[:, 0:w], ACT.Exp, sA, p, "exp",
                  bias=ast[:, 33:34], accum_out=ast[:, 34:35])
                if sink is not None:
                    A(ast[:, 35:36], ast[:, 33:34], ACT.Exp, sA, p, "sink", bias=sink)
                else:
                    A(ast[:, 35:36], ast[:, 33:34], ACT.Copy, sA, p, "sink")

            def pair(p, pump, n_next, n_out, g, u_next):
                pump.upto(n_next)
                for s in range(8 + 2):
                    if s >= 2:
                        prompt_turn(8 * p + s - 2)
                    if s < 8:
                        half, q, h2 = s // 4, s // 2 % 2, s % 2
                        prompt_exp(8 * p + s, None if g is None else col(S_SINK + 3 * (2 * half + h2) + g))
                sample_attn(p, None if g is None else col(S_SROW + g))
                pump.upto(n_out + 1)
                wait(act, sV, p, "o1")
                A(mm[0][:, :, :], qh, ACT.Copy, oA, p, "hi")
                pump.upto(n_out + 2)
                if u_next is not None:
                    head_squares(u_next)
                    if u_next != U_KEYS:
                        query_stds(u_next)

            def ffn(L):
                def split(jb, it, s):
                    hi_split(act, jb % 3, jb // 3 + it, s, 0)

                def chunk(r, par_, c):
                    wait(act, fT, r, "g")
                    if not (isinstance(r, int) and r == 0):
                        wait(act, fV, r - 1, "mul")
                    A(three(sg[:, :]), fm(0), ACT.Silu, fA, r, "silu")
                    wait(act, fV, r, "mul")
                    A(mm[0][:, par_, :], gated[:, :], ACT.Copy, fA, r, "hi")

                if L == 0:
                    wait(act, hV, HEADS - 1, "lo")
                    act.wait_ge(stored, 16 * NS0)
                else:
                    wait(act, oV, NPAIR - 1, "lo")
                    act.wait_ge(stored, 16 * NSTORE)
                for d, s in ((0, EVEN[0]), (1, EVEN[2])):
                    j = FFN0[L] + d
                    hi_split(act, j % 3, j // 3, s, 0)
                norms(NORM_FFN[L], first=FOUT0[L] - 1)
                act.wait_ge(w_used, USED0[L] + MIX_JOBS[L])
                ffn_splits(L, split, 1, 1)
                chunk(NCH * L, 0, 0)
                with act.Fori(0, (NCH - 2) // 2) as it:
                    for z in range(2):
                        c = 2 * it + 1 + z
                        ffn_splits(L, split, c + 1, z)
                        chunk(c + NCH * L, 1 - z, c)
                split(FFN0[L] - 1, NCH, LAST_SLOT)
                chunk(NCH * L + NCH - 1, 1, NCH - 1)

            def hgrn_head(h, pump, n0):
                if h == 0:
                    act.wait_ge(stored, 16 * 2)
                else:
                    wait(act, hV, h - 1, "lo")
                wait(act, hQ, h, "q")
                A(three(tA[:, :]), fm(0), ACT.Sigmoid, hA, h, "sq")
                pump.upto(n0 + 1)
                wait(act, hZ, h, "z")
                A(three(E[:, 0:T]), fm(3), ACT.Sigmoid, hA, h, "f")
                A(three(K[:, :]), fm(3), ACT.Sigmoid, hA, h, "k", scale=-1.0)
                wait(act, hA, h, "k")
                A(E[:, 0:T], E[:, 0:T], ACT.Identity, hA, h, "e", scale=col(S_ML + h), bias=col(S_L + h))
                A(K[:, :], K[:, :], ACT.Copy, hA, h, "ks", scale=col(S_ML + h))
                pump.upto(n0 + 2)
                last = h == HEADS - 1
                wait(act, hT_, h, "g")
                wait(act, hV, h, "q")
                A(three(tA[:, :]), fm(0), ACT.Sigmoid, hA, h, "sg")
                if not last:
                    pump.upto(n0 + 4)
                else:
                    pump.upto(n0 + 3)
                wait(act, hT_, h, "v")
                A(three(VF[:, :]), fm(3), ACT.Copy, hA, h, "vf")
                wait(act, hT_, h, "kr")
                nc.scalar.activation(KR[:, 0:4, :], ps[:, 6, :].rearrange("p (i c) -> p i c", i=4), ACT.Copy)
                nc.scalar.activation(KR[:, 4:8, :], ps[:, 7, :].rearrange("p (i c) -> p i c", i=4), ACT.Copy)
                nc.scalar.activation(V[0:TS, 8, :], ps[0:TS, 5, 0:P], ACT.Copy)
                A(KR[0:TS, 8, :], ps[0:TS, 5, P:2 * P], ACT.Copy, hA, h, "kr")
                wait(act, hV, h, "m")
                A(mm[0][:, 0, :], tA[:, :], ACT.Copy, hA, h, "hi")
                nc.scalar.activation(O2[:, 0:SEQ].rearrange("p (g n) -> p g n", g=2), ps[:, 3:5, :], ACT.Square)
                A(O2[:, SEQ:T], ps[:, 5, 0:TS], ACT.Square, hA, h, "o2")
                wait(act, hT_, h, "ssq")
                nc.scalar.activation(HR[:, 0:NPT], ps[:, 6, 0:NPT], ACT.Sqrt, scale=1.0 / P, bias=col(S_EPS))
                A(HR[0:TS, NPT:NT], ps[0:TS, 6, NPT:NT], ACT.Sqrt, hA, h, "std",
                  scale=1.0 / P, bias=col(S_EPS)[0:TS])
                pump.upto(n0 + (3 if last else 5))

            act.wait_ge(small_in, 32)
            act.wait_ge(init, 1)
            nc.scalar.activation(col(S_L, HEADS), col(S_L, HEADS), ACT.Exp).then_inc(lb_exp, 1)
            for L in range(2):
                pump = Pump(L, act_emit(act))
                if L:
                    pump.upto(2)
                norms(NORM_MIX[L], first=None if L == 0 else FOUT0[0] + NCH - 1,
                      mem=lambda i: mem_keys(L, pump, i))
                pump.upto(J_MQ + 2)
                head_squares([0, 1][L])
                query_stds([0, 1][L])
                pair(L, pump, J_FILL + 2, J_MO, None, [None, 2][L])
                n0 = J_TOK
                if L == 0:
                    for h in range(HEADS):
                        hgrn_head(h, pump, n0 + HGRN_JOBS * h)
                else:
                    pump.upto(n0 + 2)
                    key_std(U_KEYS, 0)
                    pump.upto(n0 + 4)
                    key_std(U_KEYS, 1)
                    head_squares(3)
                    query_stds(3)
                    for g in range(QG):
                        no = n0 + 4 + PAIR_JOBS * g + (2 if g < QG - 1 else 0)
                        pair(2 + g, pump, no, no, g, 4 + g if g < QG - 1 else None)
                pump.upto(MIX_JOBS[L])
                ffn(L)

        @block.gpsimd
        def _(pool):
            def norms(r0, mem=None):
                for i in range(NT + (2 if mem else 0)):
                    if mem:
                        mem(i)
                    t = i - 2 if mem else i
                    dst, c0, m = (hT, t * P, rows(t)) if t >= 0 else (memT, i * P, P)
                    wait(pool, nH, r0 + i, "hi")
                    nc.gpsimd.tensor_tensor(dst[1][:, :, c0:c0 + m],
                                            gained[(r0 + i) % 2][:, 0:KT * m].rearrange("p (k t) -> p k t", k=KT),
                                            dst[0][:, :, c0:c0 + m].bitcast(F32), ALU.subtract).then_inc(nP.sem, 1)

            def ffn(L):
                def split(jb, it, s):
                    lo_split(pool, jb % 3, jb + 3 * it, s)

                for d, s in ((0, EVEN[0]), (1, EVEN[2])):
                    lo_split(pool, (FFN0[L] + d) % 3, FFN0[L] + d, s)
                norms(NORM_FFN[L])
                ffn_splits(L, split, 1, 1)
                with pool.Fori(0, (NCH - 2) // 2) as it:
                    for z in range(2):
                        ffn_splits(L, split, 2 * it + 2 + z, z)
                split(FFN0[L] - 1, NCH, LAST_SLOT)

            def hgrn_head(h, pump, n0):
                pump.upto(n0 + 2)
                last = h == HEADS - 1
                for l in range(LEVELS):
                    w = 1 << l
                    n = T if l < 2 else SEQ
                    Eo = E[:, EOFF[l]:EOFF[l] + n // w].rearrange("p (b z) -> p b z", z=2)
                    wait(pool, hT_, h, f"l{l}")
                    if l:
                        wait(pool, hP, h, f"e{l - 1}")
                    Kv = K[:, 0:n].rearrange("p (b z w) -> p b z w", z=2, w=w)[:, :, 0, :]
                    nc.gpsimd.tensor_tensor(Kv, Kv, Eo[:, :, 1].unsqueeze(2).to_broadcast([P, n // (2 * w), w]),
                                            ALU.mult).then_inc(hP.sem, 1)
                    nc.gpsimd.tensor_tensor(E[:, EOFF[l + 1]:EOFF[l + 1] + n // (2 * w)], Eo[:, :, 0], Eo[:, :, 1],
                                            ALU.mult).then_inc(hP.sem, 1)
                    if l == 4 and not last:
                        pump.upto(n0 + 3)
                pump.upto(n0 + (3 if last else 5))

            for L in range(2):
                pump = Pump(L, pool_emit(pool))
                if L:
                    pump.upto(2)
                norms(NORM_MIX[L], mem=lambda i: pump.upto({2: 2, 4: MEM_JOBS, 8: J_MQ + 1}.get(i, 0)))
                if L == 0:
                    pump.upto(J_TOK)
                    for h in range(HEADS):
                        hgrn_head(h, pump, J_TOK + HGRN_JOBS * h)
                pump.upto(MIX_JOBS[L])
                ffn(L)

        @block.vector
        def _(dve):
            V_ = nc.vector

            def tt(out, a, b, op=ALU.mult):
                return V_.tensor_tensor(out, a, b, op)

            def stt(out, a, s, b, op0=ALU.mult, op1=ALU.mult):
                return V_.scalar_tensor_tensor(out=out, in0=a, scalar=s, in1=b, op0=op0, op1=op1)

            def add_group(G, i, n, scaled=False):
                dve.wait_ge(out_ready, G + 1)
                if not isinstance(G, int) or G >= OUTG:
                    dve.wait_ge(x_added, G - OUTG + 1)
                xs = x[0:rows(i), i, 512 * n:512 * n + 512]
                if scaled:
                    stt(xs, ps[0:rows(i), 6 + n, :], HR[0:rows(i), NT + i:NT + i + 1], xs,
                        ALU.mult, ALU.add).then_inc(x_added, 1)
                else:
                    tt(xs, xs, ps[0:rows(i), 6 + n, :], ALU.add).then_inc(x_added, 1)

            def adds(o, tiles=range(NT), scaled=False):
                for i in tiles:
                    for n in range(2):
                        add_group(o * OUTG + 2 * i + n, i, n, scaled)

            def norms(r0, gain, mem_gain=None, o=None, scaled=False, mem=None):
                srcs = [(x[:, i, :], rows(i), gain) for i in range(NT)]
                if mem:
                    srcs = [(xmem[:, i, :], P, mem_gain) for i in range(2)] + srcs
                for i in range(len(srcs) + 3):
                    t = i - 2 if mem else i
                    if o is not None and 0 <= t < NT:
                        for n in range(2):
                            add_group(o * OUTG + 2 * t + n, t, n, scaled)
                    if 1 <= i <= len(srcs):
                        r, (src, m, _) = r0 + i - 1, srcs[i - 1]
                        wait(dve, nA, r, "std")
                        V_.reciprocal(nrstd[0:m, r:r + 1], nstat[0:m, r:r + 1]).then_inc(nV.sem, 1)
                        wait(dve, nV, r, "rstd")
                        V_.tensor_scalar(xn[0:m, r % 2, :], src[0:m], nrstd[0:m, r:r + 1], None,
                                         ALU.mult).then_inc(nV.sem, 1)
                    if i >= 3:
                        r, (_, m, g) = r0 + i - 3, srcs[i - 3]
                        wait(dve, nT, r, "tr")
                        if r >= 2:
                            wait(dve, nP, r - 2, "lo")
                        for z in range(2):
                            b = 2 * (r % 2) + z
                            tt(gained[r % 2][:, 4 * m * z:4 * m * (z + 1)].rearrange("p (k t) -> p k t", k=4),
                               ps[:, b, 0:4 * m].rearrange("p (k t) -> p k t", k=4),
                               col(g + 4 * z, 4).unsqueeze(2).to_broadcast([P, 4, m])).then_inc(nG.sem, 1)
                    if mem:
                        mem(i)

            def mem_keys(L, i):
                if i == 9:
                    wait(dve, mA, L, "sq")
                    V_.tensor_scalar(kmem.rearrange("p a m -> p (a m)"), ps[:, 4, :], col(S_MK + L), None,
                                     ALU.mult).then_inc(mV.sem, 1)
                if i == 10:
                    wait(dve, mT, L, "v")
                    V_.tensor_copy(vmem.rearrange("p i c -> p (i c)"), ps[:, 5, :]).then_inc(mV.sem, 1)

            def head_gains(u, dsts, gain):
                for z, dst in enumerate(dsts):
                    wait(dve, qA, u, f"sq{z}")
                    V_.tensor_scalar(three(dst), fm(3 - 3 * z), gain, None, ALU.mult).then_inc(qV.sem, 1)

            def key_norm(u, z, dst):
                wait(dve, qA, u, f"std{z}")
                V_.reciprocal(probT[:, :], probT[:, :]).then_inc(qV.sem, 1)
                wait(dve, qV, u, f"rstd{z}")
                tt(dst, dst, probT[:, :]).then_inc(qV.sem, 1)

            def query_norm(u):
                n = 4 * NPT
                wait(dve, qA, u, "std0")
                V_.reciprocal(HS[:, n:2 * n], HS[:, 0:n]).then_inc(qV.sem, 1)
                wait(dve, qA, u, "std1")
                for t in (prob, prob2):
                    ins = V_.reciprocal(t[:, SEQ:T], t[:, SEQ:T])
                ins.then_inc(qV.sem, 1)
                wait(dve, qV, u, "n0")
                for z, t in enumerate((prob, prob2)):
                    tt(qh[:, z, SEQ:T], qh[:, z, SEQ:T], t[:, SEQ:T]).then_inc(qV.sem, 1)

            def prompt_max(r, first, head):
                buf, s = (prob, prob2)[r % 2], 20 * (r % 4)
                wait(dve, aSC, r, "sc")
                b0 = 2 * (r % 2)
                if head is None:
                    V_.tensor_reduce(st[:, s:s + 4], ps[:, b0:b0 + 2, :].rearrange("p b (i m) -> p (b i) m", i=2),
                                     AX.X, ALU.max).then_inc(vM.sem, 1)
                else:
                    if r % 8 >= 2:
                        wait(dve, aPT, r - 2, "pt")
                    for i in range(4):
                        c = C_BAND + (0 if first and i == 0 else 256)
                        m = V_.tensor_tensor_reduce(buf[:, 256 * i:256 * i + 256],
                                                    ps[:, b0 + i // 2, 256 * (i % 2):256 * (i % 2) + 256],
                                                    cst[:, c:c + 256], 1.0, cst[:, C_BAND:C_BAND + 1],
                                                    ALU.add, ALU.max, st[:, s + i:s + i + 1])
                    m.then_inc(vM.sem, 1)
                wait(dve, vM, r, "max")
                neg, c0 = st[:, s + 4:s + 8], row_scale(r, 0)
                scaled = stt(neg, st[:, s:s + 4], -1.0, HS[:, c0:c0 + 7:2])
                if head is None:
                    scaled.then_inc(vM.sem, 1)
                else:
                    scaled.then_inc(vS.sem, 1)
                    wait(dve, vS, r - 16, "max")
                    tt(neg, neg, col(S_NS + head).to_broadcast([P, 4]), ALU.min).then_inc(vM.sem, 1)

            def prompt_rinv(r, window):
                s = 20 * (r % 4)
                wait(dve, aE, r, "exp")
                den = st[:, s + 8:s + 12]
                if window:
                    wait(dve, aSK, r - 16, "sink")
                    tt(den, den, st[:, s + 12:s + 16], ALU.add).then_inc(vD.sem, 1)
                    wait(dve, vD, r - 16, "den")
                V_.reciprocal(st[:, s + 16:s + 20], den).then_inc(vR.sem, 1)

            def prompt_turn(r):
                wait(dve, aPT, r, "pt")
                if r >= 1:
                    wait(dve, aPV, r - 1, "pv")
                V_.tensor_copy(probT[:, 512:1024], ps[:, 5, :]).then_inc(vC.sem, 1)

            def prompt_rows(r, h2):
                s = 20 * (r % 4)
                wait(dve, aPV, r, "pv")
                if r >= 2:
                    wait(dve, aOT, r // 2 - 1, "ot")
                wait(dve, vR, r, "rinv")
                tt(orow[:, :, 64 * h2:64 * h2 + 64], ps[:, 6, 256 * h2:256 * h2 + 256].rearrange("p (i d) -> p i d", i=4),
                   st[:, s + 16:s + 20].unsqueeze(2).to_broadcast([P, 4, HD])).then_inc(vO.sem, 1)

            def prompt_out(r, half, q):
                wait(dve, aOT, r // 2, "ot")
                V_.tensor_copy(qh[:, half, 512 * q:512 * q + 512], ps[:, 7, :]).then_inc(vOT.sem, 1)

            def sample_attn(p, g):
                for half in range(2):
                    m = tt(qblk[:, half, :, :].rearrange("p b (s q) -> p b s q", q=TQ),
                           qh[:, half, SEQ:T].rearrange("p (b q) -> p b q", q=TQ).unsqueeze(2)
                           .to_broadcast([P, NB, 8, TQ]),
                           cst[:, C_QB + 64 * half:C_QB + 64 * half + 64].rearrange("p (b s) -> p b s", b=NB)
                           .unsqueeze(3).to_broadcast([P, NB, 8, TQ]))
                m.then_inc(sV.sem, 1)
                wait(dve, sT, p, "sc")
                if g is None:
                    V_.tensor_reduce(ast[:, 32:33], ps[:, 0, 0:256], AX.X, ALU.max).then_inc(sV.sem, 1)
                else:
                    V_.tensor_tensor_reduce(sprob[:, 0:160], ps[:, 0, 0:160], cst[:, C_SROW:C_SROW + 160], 1.0,
                                            col(S_SROW + g), ALU.add, ALU.max, ast[:, 32:33]).then_inc(sV.sem, 1)
                wait(dve, sV, p, "max")
                V_.tensor_scalar(ast[:, 33:34], ast[:, 32:33], -1.0, None, ALU.mult).then_inc(sV.sem, 1)
                wait(dve, sA, p, "sink")
                if g is None:
                    V_.tensor_copy(ast[:, 36:37], ast[:, 34:35]).then_inc(sV.sem, 1)
                else:
                    tt(ast[:, 36:37], ast[:, 34:35], ast[:, 35:36], ALU.add).then_inc(sV.sem, 1)
                wait(dve, sV, p, "den")
                V_.reciprocal(ast[:, 37:38], ast[:, 36:37]).then_inc(sV.sem, 1)
                wait(dve, sV, p, "rinv")
                w = 256 if g is None else 160
                V_.tensor_scalar(sprob[:, 0:w], sprob[:, 0:w], ast[:, 37:38], None, ALU.mult).then_inc(sV.sem, 1)
                wait(dve, sT, p, "pt")
                if g is None:
                    V_.tensor_copy(sprobT, ps[:, 1, 0:256].rearrange("p (c r) -> p c r", c=2)).then_inc(sV.sem, 1)
                else:
                    V_.tensor_copy(sprobT[:, 0, :], ps[:, 1, 0:P])
                    V_.tensor_copy(sprobT[0:TS, 1, :], ps[0:TS, 1, P:2 * P]).then_inc(sV.sem, 1)
                wait(dve, sT, p, "pv")
                for h2 in range(2):
                    r = slice(64 * h2, 64 * h2 + 64)
                    V_.tensor_copy(qh[r, :, SEQ:T].rearrange("p a (b q) -> p a b q", q=TQ),
                                   ps[r, 2, 0:P].rearrange("p (a b z q) -> p a b z q", a=2, b=NB, z=2)[:, :, :, h2, :]
                                   ).then_inc(sV.sem, 1)

            def pair(p, g):
                for s in range(8 + 4):
                    if s >= 4 and s % 2:
                        prompt_out(8 * p + s - 4, (s - 4) // 4, (s - 4) // 2 % 2)
                    if 3 <= s < 11:
                        prompt_rows(8 * p + s - 3, (s - 3) % 2)
                    if 2 <= s < 10:
                        prompt_turn(8 * p + s - 2)
                        prompt_rinv(8 * p + s - 2, g is not None)
                    if s < 8:
                        half, q, h2 = s // 4, s // 2 % 2, s % 2
                        prompt_max(8 * p + s, q == 0, None if g is None else 3 * (2 * half + h2) + g)
                sample_attn(p, g)
                wait(dve, oA, p, "hi")
                tt(mm[1], qh, mm[0].bitcast(F32), ALU.subtract).then_inc(oV.sem, 1)

            def hgrn_head(h):
                if h == 0:
                    wait(dve, oV, 0, "lo")
                    dve.wait_ge(stored, 16 * 2)
                    V_.memset(ones[:, :], 1.0)
                    V_.memset(att[:, :], 0.0).then_inc(init, 1)
                    dve.wait_ge(init, INIT + 1)
                inc = hV.sem
                wait(dve, hA, h, "sq")
                stt(three(Q[:, :]), fm(0), float(P) ** -0.5, three(tA[:, :])).then_inc(inc, 1)
                if h:
                    adds(OUT0[0] + h, range(4, NT), scaled=True)
                wait(dve, hT_, h, "diag")
                idm = ident.bitcast(I32)
                V_.copy_predicated(att[:, 0:SEQ].rearrange("p (i t) -> p i t", i=NPT),
                                   idm.unsqueeze(1).to_broadcast([P, NPT, P]),
                                   ps[:, 6:8, :].rearrange("p b (i t) -> p (b i) t", i=4))
                V_.copy_predicated(att[0:TS, SEQ:T], idm[0:TS, 0:TS], ps[0:TS, 5, C_SD:C_SD + TS]).then_inc(inc, 1)
                wait(dve, hV, h, "q")
                tt(Q[:, :], Q[:, :], E[:, 0:T]).then_inc(inc, 1)
                for l in range(LEVELS):
                    w = 1 << l
                    n = T if l < 2 else SEQ
                    wait(dve, hT_, h, f"l{l}")
                    mask = cst[:, C_LVL + 64 * l:C_LVL + 64 * l + 64].bitcast(I32)
                    av = att[:, 0:SEQ].rearrange("p (i b z w) -> p i b z w", i=NPT, z=2, w=w)[:, :, :, 1, :]
                    ins = V_.copy_predicated(
                        av, mask.rearrange("p (b w) -> p b w", w=w).unsqueeze(1).to_broadcast([P, NPT, 64 // w, w]),
                        ps[:, 6 + l % 2, :].rearrange("p (i b w) -> p i b w", i=NPT, w=w))
                    if l < 2:
                        ins = V_.copy_predicated(
                            att[0:TS, SEQ:T].rearrange("p (b z w) -> p b z w", z=2, w=w)[:, :, 1, :],
                            mask[0:TS, 0:16].rearrange("p (b w) -> p b w", w=w),
                            ps[0:TS, 5, C_SL + 16 * l:C_SL + 16 * l + 16].rearrange("p (b w) -> p b w", w=w))
                    ins.then_inc(inc, 1)
                    if l:
                        wait(dve, hP, h, f"e{l - 1}")
                    wait(dve, hV, h, "qf" if l == 0 else f"q{l - 1}")
                    Qv = Q[:, 0:n].rearrange("p (b z w) -> p b z w", z=2, w=w)[:, :, 1, :]
                    Ee = E[:, EOFF[l]:EOFF[l] + n // w].rearrange("p (b z) -> p b z", z=2)[:, :, 0]
                    tt(Qv, Qv, Ee.unsqueeze(2).to_broadcast([P, n // (2 * w), w])).then_inc(inc, 1)
                wait(dve, hA, h, "sg")
                tt(three(G[:, :]), fm(0), three(tA[:, :])).then_inc(inc, 1)
                wait(dve, hT_, h, "vr")
                V_.tensor_copy(V[:, 0:8, :], ps[:, 3:5, :].rearrange("p b (i c) -> p (b i) c", i=4)).then_inc(inc, 1)
                wait(dve, hA, h, "kr")
                tt(VM[0:TS, :].rearrange("p (b v) -> p b v", b=NB), V[0:TS, 8, :].unsqueeze(1).to_broadcast([TS, NB, P]),
                   cst[0:TS, C_VM:C_VM + NB].unsqueeze(2).to_broadcast([TS, NB, P])).then_inc(inc, 1)
                wait(dve, hT_, h, "ds")
                wait(dve, hP, h, f"e{LEVELS - 1}")
                if h:
                    dve.wait_ge(stored, 16 * (2 + 2 * h))
                for i in range(NPT):
                    ds = ps[:, 6 + i // 4, P * (i % 4):P * (i % 4) + P]
                    if i == 0:
                        V_.tensor_copy(S[:, 0, :], ds).then_inc(inc, 1)
                    else:
                        wait(dve, hV, h, f"s{i - 1}")
                        stt(S[:, i, :], S[:, i - 1, :], E[:, EOFF[LEVELS] + i:EOFF[LEVELS] + i + 1], ds,
                            ALU.mult, ALU.add).then_inc(inc, 1)
                dve.wait_ge(side_in, 16 * (4 + h + 1))
                sv = SN[:, :].rearrange("p (b v) -> p b v", b=NB)
                tt(sv, S0[:, :].rearrange("p (b v) -> p b v", b=NB),
                   E[:, EOFF[2] + SEQ // 4:EOFF[2] + T // 4].unsqueeze(2).to_broadcast([P, NB, P])).then_inc(inc, 1)
                wait(dve, hV, h, "sn")
                wait(dve, hT_, h, "ds8")
                tt(SN[:, :].rearrange("p (b v) -> p b v", b=2), SN[:, :].rearrange("p (b v) -> p b v", b=2),
                   ps[:, 6:8, :], ALU.add).then_inc(inc, 1)
                wait(dve, hT_, h, "o")
                stt(tA[:, 0:SEQ].rearrange("p (b n) -> p b n", b=2), ps[:, 3:5, :], col(S_GN + h),
                    G[:, 0:SEQ].rearrange("p (b n) -> p b n", b=2))
                stt(tA[:, SEQ:T], ps[:, 5, 0:TS], col(S_GN + h), G[:, SEQ:T]).then_inc(inc, 1)
                wait(dve, hA, h, "hi")
                tt(mm[1][:, 0, :], tA[:, :], mm[0][:, 0, :].bitcast(F32), ALU.subtract).then_inc(inc, 1)
                wait(dve, hA, h, "std")
                V_.reciprocal(HR[:, NT:NT + NPT], HR[:, 0:NPT])
                V_.reciprocal(HR[0:TS, NT + NPT:2 * NT], HR[0:TS, NPT:NT]).then_inc(inc, 1)
                wait(dve, hV, h, "rstd")
                if h < HEADS - 1:
                    adds(OUT0[0] + 1 + h, range(4), scaled=True)

            def ffn(L):
                def chunk(r, par_, G0):
                    if G0 is not None:
                        for i in range(NT):
                            for n in range(2):
                                add_group(G0 + 2 * i + n, i, n)
                    wait(dve, fT, r, "u")
                    wait(dve, fA, r, "silu")
                    tt(three(gated[:, :]), fm(3), three(sg[:, :])).then_inc(fV.sem, 1)
                    wait(dve, fA, r, "hi")
                    tt(mm[1][:, par_, :], gated[:, :], mm[0][:, par_, :].bitcast(F32),
                       ALU.subtract).then_inc(fV.sem, 1)

                norms(NORM_FFN[L], S_FFN + KT * L, o=FOUT0[L] - 1, scaled=L == 0)
                chunk(NCH * L, 0, None)
                with dve.Fori(0, (NCH - 2) // 2) as it:
                    for z in range(2):
                        chunk(2 * it + 1 + z + NCH * L, 1 - z, OUTG * 2 * it + OUTG * (z + FOUT0[L]))
                chunk(NCH * L + NCH - 1, 1, OUTG * (FOUT0[L] + NCH - 2))

            def setup():
                n = [0]

                def done(ins):
                    n[0] += 1
                    ins.then_inc(init, 1)
                    return n[0]

                V_.memset(col(S_EPS), EPS)
                dve.wait_ge(small_in, 32)
                lb, ml, rawl = col(S_L, HEADS), col(S_ML, HEADS), col(S_LB, HEADS)
                V_.tensor_scalar(col(S_GQ, 1), col(S_SQ, 1), HD ** -0.5, None, ALU.mult)
                V_.tensor_scalar(col(S_GQ + 1, 2), col(S_MQ, 2), HD ** -0.5, None, ALU.mult)
                V_.tensor_scalar(col(S_NS, 12), col(S_SINK, 12), -1.0, None, ALU.mult)
                k = done(tt(lb, rawl, rawl, ALU.subtract))
                dve.wait_ge(lb_exp, 1)
                k = done(V_.reciprocal(ml, lb))
                dve.wait_ge(init, k)
                k = done(tt(lb, lb, ml))
                dve.wait_ge(init, k)
                k = done(tt(ml, lb, lb, ALU.subtract))
                dve.wait_ge(init, k)
                k = done(V_.tensor_scalar(lb, ml, 0.0, 0.999, ALU.max, ALU.min))
                dve.wait_ge(init, k)
                k = done(V_.tensor_scalar(ml, lb, -1.0, 1.0, ALU.mult, ALU.add))
                dve.wait_ge(init, k)
                assert k == INIT

            setup()
            for L in range(2):
                norms(NORM_MIX[L], S_MIX + KT * L, S_MEM + KT * L, o=None if L == 0 else FOUT0[0] + NCH - 1,
                      mem=lambda i: mem_keys(L, i))
                wait(dve, mA, L, "std")
                V_.reciprocal(kmem_rstd[:, :], kmem_rstd[:, :]).then_inc(mV.sem, 1)
                wait(dve, mV, L, "rstd")
                km = kmem.rearrange("p a m -> p (a m)")
                tt(km, km, kmem_rstd[:, :]).then_inc(mV.sem, 1)
                wait(dve, mT, L, "rows")
                V_.tensor_copy(ktok_mem.rearrange("p i c -> p (i c)"), ps[:, 6, :]).then_inc(mV.sem, 1)
                dve.wait_ge(masks_in, 16)
                heads_of_qh = [qh[:, half, :] for half in range(2)]
                head_gains([0, 1][L], heads_of_qh, col(S_GQ + 1 + L))
                query_norm([0, 1][L])
                wait(dve, qV, [0, 1][L], "n1")
                pair(L, None)
                if L == 0:
                    adds(OUT0[L])
                    for h in range(HEADS):
                        hgrn_head(h)
                else:
                    dve.wait_ge(stored, 16 * (NS0 + 2))
                    V_.memset(kpad[:, :, 0:WIN], 0.0).then_inc(kV.sem, 1)
                    keys = [kpad[:, half, WIN:WIN + T] for half in range(2)]
                    head_gains(U_KEYS, keys, col(S_SK))
                    adds(OUT0[L])
                    key_norm(U_KEYS, 0, keys[0])
                    wait(dve, kT, 0, "v")
                    V_.tensor_copy(vwin[:, 0:8, :], ps[:, 0:4, :].rearrange("p b (i c) -> p (b i) c", i=2))
                    V_.tensor_copy(vwin[0:TS, 8, :], ps[0:TS, 4, 0:256]).then_inc(kV.sem, 1)
                    key_norm(U_KEYS, 1, keys[1])
                    head_gains(3, heads_of_qh, col(S_GQ))
                    wait(dve, kT, 0, "rows")
                    V_.tensor_copy(ktok[:, 0, :], ps[:, 6, 0:256])
                    V_.tensor_copy(ktok[0:TS, 1, :], ps[0:TS, 6, 256:512]).then_inc(kV.sem, 1)
                    query_norm(3)
                    for g in range(QG):
                        wait(dve, qV, 3 + g, "n1")
                        pair(2 + g, g)
                        if g < QG - 1:
                            wait(dve, oV, 2 + g, "lo")
                            head_gains(4 + g, heads_of_qh, col(S_GQ))
                            adds(OUT0[1] + 1 + g, range(6))
                            query_norm(4 + g)
                            adds(OUT0[1] + 1 + g, range(6, NT))
                ffn(L)
            adds(FOUT0[1] + NCH - 1)

        @block.tensor
        def _(pe):
            mmul = nc.tensor.matmul
            PASS = ((0, 0), (0, 1), (1, 0))

            def feat_mm(s, b0, m):
                k, (a, b), g = m // 9, PASS[m % 9 // 3], m % 3
                return mmul(ps[:, b0 + g, 0:TW], slot(a, s)[:, P * k:P * k + P], hT[b][:, k, TW * g:TW * g + TW],
                            start=m < 3, stop=m >= 69)

            def feat(j, s, b0, steps, part=(0, 1)):
                a, b = part
                if a == 0:
                    pe.wait_ge(w_lo, j + 1)
                for m in range(72 * a // b, 72 * (a + 1) // b):
                    ins = feat_mm(s, b0, m)
                if a == b - 1:
                    ins.then_inc(steps.sem, 1)
                    used(j)

            def used(j):
                pe.drain().then_inc(w_used, 1)

            def both_cols(j, act, tiles, place):
                pe.wait_ge(w_lo, j + 2)
                for i, m in tiles:
                    for k in range(KT):
                        for q, (a, b) in enumerate(PASS):
                            cols = w01[a][:, :].rearrange("p (s n) -> p s n", s=2)[:, :, P * k:P * k + P]
                            mmul(place(i, m), act[b][:, k, P * i:P * i + m], cols,
                                 start=k == 0 and q == 0, stop=k == KT - 1 and q == 2)
                pe.drain().then_inc(w_used, 2)

            def out_group(G, i, n, srcs):
                if not isinstance(G, int) or G >= 2:
                    pe.wait_ge(x_added, G - 1)
                steps = [(p, s, a, b) for p, s in srcs for a, b in PASS]
                for q, (p, s, a, b) in enumerate(steps):
                    ins = mmul(ps[0:rows(i), 6 + n, :], mm[b][:, p, P * i:P * i + rows(i)],
                               slot(a, s)[:, 512 * n:512 * n + 512], start=q == 0, stop=q == len(steps) - 1)
                return ins.then_inc(out_ready, 1)

            def outs(o, j, srcs, after=None):
                pe.wait_ge(w_lo, j + 1)
                if len(srcs) == 2:
                    if o:
                        pe.wait_ge(x_added, o * OUTG)
                    for last, (p, s) in enumerate(srcs):
                        if last:
                            pe.wait_ge(w_lo, j + 2)
                        for n in range(2):
                            for q, (a, b) in enumerate(PASS):
                                ins = mmul(ps[:, 6 + n, :], mm[b][:, p, 0:P], slot(a, s)[:, 512 * n:512 * n + 512],
                                           start=last == 0 and q == 0, stop=last == 1 and q == 2)
                            if last:
                                ins.then_inc(out_ready, 1)
                    if after:
                        after(0)
                for i in range(1 if len(srcs) == 2 else 0, NT):
                    for n in range(2):
                        out_group(o * OUTG + 2 * i + n, i, n, srcs)
                    if after:
                        after(i)
                if srcs[0][1] != LAST_SLOT:
                    pe.drain().then_inc(w_used, len(srcs))

            def transposes(r, m):
                wait(pe, nV, r, "xn")
                if r >= 2:
                    wait(pe, nG, r - 2, "g1")
                for k in range(KT):
                    ins = nc.tensor.transpose(ps[:, 2 * (r % 2) + k // 4, m * (k % 4):m * (k % 4) + m],
                                              xn[0:m, r % 2, P * k:P * k + P], ident[0:m, 0:m])
                ins.then_inc(nT.sem, 1)

            def norms(r0, mem=None, out=None):
                n = NT + (2 if mem else 0)
                lag = 0 if mem else 2

                def after(i):
                    if i >= lag:
                        transposes(r0 + i - lag, P if mem and i < 2 else rows(i - 2))
                    if mem:
                        mem(i)

                if out:
                    outs(*out, after=after)
                for i in range(NT if out else lag, n + lag):
                    after(i)

            def mem_keys(L, i):
                J = MIX0[L]
                if i == 4:
                    wait(pe, nP, NORM_MIX[L] + 1, "lo")
                    pe.wait_ge(w_lo, J + 2)
                    for h in range(2):
                        for k in range(KT):
                            for q, (a, b) in enumerate(PASS):
                                ins = mmul(ps[:, 4, N_MEM * h:N_MEM * (h + 1)], slot(a, h)[:, P * k:P * k + P],
                                           memT[b][:, k, :], start=k == 0 and q == 0, stop=k == KT - 1 and q == 2)
                        ins.then_inc(w_used, 1)
                    pe.drain().then_inc(mT.sem, 1)
                if i == 7:
                    both_cols(J + 2, memT, [(0, P), (1, P)], lambda i, m: ps[:, 5, 256 * i:256 * i + 256])
                    pe.drain().then_inc(mT.sem, 1)
                if i == 9:
                    wait(pe, mV, L, "v")
                    mmul(ps[:, 5, :], cst[:, C_BLK:C_BLK + P], kmem_sq[:, :], start=True, stop=True).then_inc(mT.sem, 1)

            def first_queries(L, j):
                r0 = NORM_MIX[L] + 2
                pe.wait_ge(w_lo, j + 1)
                for g in (1, 0, 2):
                    wait(pe, nP, r0 + min((TW * (g + 1) - 1) // P, NPT), "lo")
                    if g == 1:
                        wait(pe, mV, L, "g")
                    if g == 0:
                        assert (r0 + NPT - 1) % 2 == 1
                        wait(pe, nG, r0 + NPT - 1, "g1")
                    if g == 2:
                        wait(pe, mA, L, "std")
                    for m in range(g, 72, 3):
                        ins = feat_mm(0, 3, m)
                ins.then_inc(qT.sem, 1)
                used(j)

            def key_sums(u, z):
                t = (prob, prob2)[z]
                for b in range(2):
                    mmul(ps[:, 6 + b, :], cst[:, C_BLK:C_BLK + P], t[:, 512 * b:512 * b + 512], start=True, stop=True)
                mmul(ps[:, 5 - 3 * z, TW:TW + TS], cst[:, C_BLK:C_BLK + P], t[:, SEQ:T],
                     start=True, stop=True).then_inc(qT.sem, 1)

            def query_sums(u):
                wait(pe, qA, u, "sq1")
                wait(pe, qV, u, "g0")
                heads = cst[:, C_BLK:C_BLK + P].rearrange("p (h c) -> p h c", h=2)[:, :, 0]
                for z, t in enumerate((prob, prob2)):
                    for i in range(NPT):
                        c0 = C_HR + 2 * NPT * z + 2 * i
                        mmul(ps[:, 5, c0:c0 + 2], t[:, P * i:P * i + P], heads, start=True, stop=True)
                    mmul(ps[:, 5, C_HS + TS * z:C_HS + TS * (z + 1)], cst[:, C_BLK:C_BLK + P], t[:, SEQ:T],
                         start=True, stop=True).then_inc(qT.sem, 1)

            def prompt_scores(r, half, h2, q, window):
                hs = slice(64 * h2, 64 * h2 + 64)
                if r % 8 >= 2:
                    wait(pe, vM, r - 2, "max") if window else wait(pe, aE, r - 2, "exp")
                for i in range(4):
                    t = 4 * q + i
                    rhs = kpad[hs, half, P * t:P * t + 256] if window else kmem[hs, half, :]
                    b = 2 * (r % 2) + i // 2
                    ins = mmul(ps[:, b, 256 * (i % 2):256 * (i % 2) + 256], qh[hs, half, P * t:P * t + P], rhs,
                               start=True, stop=True)
                ins.then_inc(aSC.sem, 1)

            def prompt_turn(r):
                buf = (prob, prob2)[r % 2]
                wait(pe, aE, r, "exp")
                if r >= 1:
                    wait(pe, vC, r - 1, "pt")
                    wait(pe, aC, r - 1, "pt")
                for i in range(4):
                    for c in range(2):
                        ins = nc.tensor.transpose(ps[:, 4 + c, P * i:P * i + P],
                                                  buf[:, 256 * i + P * c:256 * i + P * c + P], ident)
                ins.then_inc(aPT.sem, 1)

            def prompt_rows(r, half, h2, q, window):
                wait(pe, vC, r, "pt")
                wait(pe, aC, r, "pt")
                if r >= 1:
                    wait(pe, vO, r - 1, "o")
                for i in range(4):
                    t = 4 * q + i
                    cs = [c for c in range(2) if not window or t + c > 0]
                    for c in cs:
                        hc = slice(P * half + 64 * h2, P * half + 64 * h2 + 64)
                        rhs = vwin[:, t - 1 + c, hc] if window else vmem[:, c, hc]
                        ins = mmul(ps[:, 6, 256 * h2 + 64 * i:256 * h2 + 64 * i + 64],
                                   probT[:, 512 * c + P * i:512 * c + P * i + P], rhs,
                                   start=c == cs[0], stop=c == 1)
                ins.then_inc(aPV.sem, 1)

            def prompt_out(r):
                wait(pe, vO, r, "o")
                if r >= 2:
                    wait(pe, vOT, r // 2 - 1, "ot")
                for i in range(4):
                    ins = nc.tensor.transpose(ps[:, 7, P * i:P * i + P], orow[:, i, :], ident)
                ins.then_inc(aOT.sem, 1)

            def sample_attn(p, window, fill):
                n = 1 if window else 2
                pe.wait_ge(side_in, 16 * [2, 12, 16, 16, 16][p])
                wait(pe, vOT, 4 * p + 3, "ot")
                wait(pe, sV, p, "qb")

                def scores(b):
                    wait(pe, sA, p, f"kt{b}")
                    grp, e = b // 2, b % 2
                    out = slice(32 * grp, 32 * grp + 32)
                    for half in range(2):
                        mmul(ps[out, 0, 0:P * n], qblk[:, half, b, :], kcT[:, b % 2, P * n * half:P * n * (half + 1)],
                             start=e == 0 and half == 0, stop=e == 1 and half == 1)
                    if window and e:
                        for z, bb in enumerate((b - 1, b)):
                            for half in range(2):
                                mmul(ps[out, 0, P:P + TS], qblk[:, half, bb, :], kpad[:, half, WIN + SEQ:WIN + T],
                                     start=z == 0 and half == 0, stop=z == 1 and half == 1)

                for b in range(NB):
                    if b >= 2:
                        wait(pe, sA, p, f"kt{b - 2}")
                    for half in range(2):
                        for i in range(n):
                            c0 = (b * n + i) * 256 + P * half
                            o0 = P * n * half + P * i
                            ins = nc.tensor.transpose(ps[:, 6 + b % 2, o0:o0 + P], cacheb[:, c0:c0 + P], ident)
                    ins.then_inc(sT.sem, 1)
                    if b:
                        fill(b - 1, 10)
                        scores(b - 1)
                fill(7, 10)
                scores(NB - 1)
                pe.drain().then_inc(sT.sem, 1)
                fill(8, 10)
                fill(9, 10)
                wait(pe, sV, p, "p")
                nc.tensor.transpose(ps[:, 1, 0:P], sprob[:, 0:P], ident)
                w = TS if window else P
                nc.tensor.transpose(ps[0:w, 1, P:2 * P], sprob[:, P:P + w], ident).then_inc(sT.sem, 1)
                wait(pe, sV, p, "pt")
                if not window:
                    pe.wait_ge(side_in, 16 * [4, 14][p])
                for half in range(2):
                    hc = slice(P * half, P * half + P)
                    if window:
                        new = sprobT[0:TS, 1, :].rearrange("p (b a r) -> p b a r", b=NB, a=2)[:, :, half, :]
                        mmul(ps[:, 2, 64 * half:64 * half + 64], vwin[0:TS, NPT, hc], new, start=True, stop=False,
                             skip_group_check=True)
                    for b in range(NB):
                        r0 = 16 * b + 8 * half
                        out = ps[:, 2, 64 * half + 8 * b:64 * half + 8 * b + 8]
                        for c in range(1 if window else 2):
                            c0 = 2048 + 256 * b if window else (2 * b + c) * 256
                            ins = mmul(out, cacheb[:, c0 + P * half:c0 + P * half + P], sprobT[:, c, r0:r0 + 8],
                                       start=not window and c == 0, stop=not window and c == 1 or window and b == NB - 1,
                                       skip_group_check=window)
                ins.then_inc(sT.sem, 1)

            def pair(p, window, fills):
                wait(pe, qV, [0, 1, 3, 4, 5][p], "g1")
                wait(pe, qA, [0, 1, 3, 4, 5][p], "std1")
                for s in range(8 + 4):
                    at_ = lambda s: (8 * p + s, s // 4, s % 2, s // 2 % 2)
                    if s >= 4 and s % 2:
                        prompt_out(8 * p + s - 4)
                    if 3 <= s < 11:
                        prompt_rows(*at_(s - 3), window)
                    if 2 <= s < 10:
                        prompt_turn(8 * p + s - 2)
                    if s < 8:
                        prompt_scores(*at_(s), window)

                def fill(a, b):
                    if fills:
                        feat(fills[0][0], fills[0][1], 3, fills[0][2], (a, b))

                sample_attn(p, window, fill)
                if fills:
                    wait(pe, sV, p, "o1")
                    feat(fills[1][0], fills[1][1], 0, fills[1][2])
                wait(pe, oV, p, "lo")

            def hgrn_head(h, j):
                inc = hT_.sem
                n0 = j - MIX0[0]
                last = h == HEADS - 1
                wait(pe, hV, h, "q")
                wait(pe, hA, h, "ks")
                for i in range(NPT):
                    mmul(ps[:, 6 + i // 4, P * (i % 4):P * (i % 4) + P], K[:, P * i:P * i + P], Q[:, P * i:P * i + P],
                         start=True, stop=True)
                mmul(ps[0:TS, 5, C_SD:C_SD + TS], K[:, SEQ:T], Q[:, SEQ:T], start=True, stop=True).then_inc(inc, 1)
                feat(j, n0 % 2, 0, hT_, (0, 4))
                for l in range(LEVELS):
                    w = 1 << l
                    wait(pe, hV, h, "qf" if l == 0 else f"q{l - 1}")
                    if l:
                        wait(pe, hP, h, f"k{l - 1}")
                    for i in range(NPT):
                        qv = Q[:, P * i:P * i + P].rearrange("p (b z w) -> p b z w", z=2, w=w)[:, :, 1, :]
                        ins = mmul(ps[:, 6 + l % 2, 64 * i:64 * i + 64].rearrange("p (b w) -> p b w", w=w),
                                   K[:, P * i:P * i + P], qv, start=True, stop=True)
                    if l < 2:
                        qv = Q[:, SEQ:T].rearrange("p (b z w) -> p b z w", z=2, w=w)[:, :, 1, :]
                        ins = mmul(ps[0:TS, 5, C_SL + 16 * l:C_SL + 16 * l + 16].rearrange("p (b w) -> p b w", w=w),
                                   K[:, SEQ:T], qv, start=True, stop=True)
                    ins.then_inc(inc, 1)
                    if l < 3:
                        feat(j, n0 % 2, 0, hT_, (l + 1, 4))
                    else:
                        feat(j + 1, (n0 + 1) % 2, 3, hT_, (l - 3, 4))

                def fill(a):
                    if not last:
                        if a == 0:
                            wait(pe, hV, h, "g")
                        feat(j + 2, n0 % 2, 0, hQ, (a, 4))

                wait(pe, hV, h, f"q{LEVELS - 1}")
                wait(pe, hP, h, f"k{LEVELS - 1}")
                for i in range(NPT):
                    nc.tensor.transpose(ps[:, 6 + i // 4, P * (i % 4):P * (i % 4) + P], K[:, P * i:P * i + P], ident)
                wait(pe, hA, h, "vf")
                nc.tensor.transpose(ps[0:TS, 5, 0:P], VF[:, SEQ:T], ident)
                nc.tensor.transpose(ps[0:TS, 5, P:2 * P], K[:, SEQ:T], ident).then_inc(inc, 1)
                for i in range(NPT):
                    ins = nc.tensor.transpose(ps[:, 3 + i // 4, P * (i % 4):P * (i % 4) + P],
                                              VF[:, P * i:P * i + P], ident)
                ins.then_inc(inc, 1)
                fill(0)
                wait(pe, hA, h, "kr")
                wait(pe, hV, h, "v")
                for i in range(NPT):
                    ins = mmul(ps[:, 6 + i // 4, P * (i % 4):P * (i % 4) + P], KR[:, i, :], V[:, i, :],
                               start=True, stop=True)
                ins.then_inc(inc, 1)
                fill(1)
                wait(pe, hV, h, f"s{NPT - 1}")
                for z in range(2):
                    ins = mmul(ps[:, 6 + z, :], KR[0:TS, 8, :], VM[0:TS, 512 * z:512 * z + 512], start=True, stop=True)
                ins.then_inc(inc, 1)
                for i in range(NPT):
                    out = ps[:, 3 + i // 4, P * (i % 4):P * (i % 4) + P]
                    mmul(out, V[:, i, :], att[:, P * i:P * i + P], start=True, stop=i == 0)
                    if i:
                        mmul(out, S[:, i - 1, :], Q[:, P * i:P * i + P], start=False, stop=True)
                mmul(ps[:, 5, 0:TS], V[0:TS, 8, :], att[0:TS, SEQ:T], start=True, stop=False, skip_group_check=True)
                for b in range(NB):
                    ins = mmul(ps[:, 5, TQ * b:TQ * b + TQ], S0[:, P * b:P * b + P], Q[:, SEQ + TQ * b:SEQ + TQ * b + TQ],
                               start=False, stop=b == NB - 1, skip_group_check=True)
                ins.then_inc(inc, 1)
                fill(2)
                fill(3)
                wait(pe, hA, h, "o2")
                wait(pe, hV, h, "sd")
                for i in range(NT):
                    m = rows(i)
                    ins = mmul(ps[0:m, 6, i:i + 1], O2[:, P * i:P * i + m], ones[:, 0:1],
                               start=True, stop=True)
                ins.then_inc(inc, 1)
                if last:
                    wait(pe, hV, h, "lo")
                    wait(pe, hA, h, "std")
                    return
                wait(pe, hV, h, "m")
                G0, g = (OUT0[0] + 1 + h) * OUTG, 0
                pe.wait_ge(w_lo, j + 4)
                for m in range(72):
                    if m >= 32 and m % 4 == 0:
                        if g == 0:
                            wait(pe, hV, h, "lo")
                            wait(pe, hA, h, "std")
                            pe.wait_ge(w_lo, j + 5)
                        out_group(G0 + g, g // 2, g % 2, [(0, n0 % 2)])
                        g += 1
                    ins = feat_mm((n0 + 1) % 2, 3, m)
                ins.then_inc(hZ.sem, 1)
                used(j + 3)
                for g in range(g, OUTG):
                    out_group(G0 + g, g // 2, g % 2, [(0, n0 % 2)])
                used(j + 4)
                pe.wait_ge(x_added, G0 + OUTG)

            def ffn(L, first_out):
                def chunk(r, c_par, jg, ju, slots, prev):
                    pe.wait_ge(w_lo, jg + 1)
                    if prev is not None or L:
                        wait(pe, fA, r - 1, "silu")
                    G0, so = prev if prev is not None else (None, None)
                    g = 0
                    for m in range(144):
                        if m == 72:
                            pe.wait_ge(w_lo, ju + 1)
                            if prev is not None or L:
                                wait(pe, fV, r - 1, "mul")
                        ins = feat_mm(slots[0], 0, m) if m < 72 else feat_mm(slots[2], 3, m - 72)
                        if m == 71:
                            ins.then_inc(fT.sem, 1)
                        if prev is not None and m >= 34 and (m - 34) % 6 == 0 and g < OUTG:
                            if g == 0:
                                pe.wait_ge(w_lo, jg + 2)
                                wait(pe, fV, r - 1, "lo")
                            out_group(G0 + g, g // 2, g % 2, [(1 - c_par, so)])
                            g += 1
                    assert prev is None or g == OUTG
                    ins.then_inc(fT.sem, 1)

                def first_chunk(r, j):
                    r0 = NORM_FFN[L]
                    pe.wait_ge(w_lo, j + 2)
                    for half, g in ((1, 1), (0, 0), (0, 1), (1, 0), (0, 2), (1, 2)):
                        wait(pe, nP, r0 + min((TW * (g + 1) - 1) // P, NPT), "lo")
                        if (half, g) == (0, 0):
                            assert (r0 + NPT) % 2 == 1
                            wait(pe, nG, r0 + NPT - 1, "g1")
                        if (half, g) == (1, 0):
                            wait(pe, nG, r0 + NPT, "g1")
                        for m in range(g, 72, 3):
                            ins = feat_mm(EVEN[2 * half], 3 * half, m)
                        if g == 2:
                            ins.then_inc(fT.sem, 1)

                F0 = FFN0[L]
                norms(NORM_FFN[L], out=first_out)
                first_chunk(NCH * L, F0)
                with pe.Fori(0, (NCH - 2) // 2) as it:
                    for z in range(2):
                        jg = 6 * it + (F0 + 2 + 3 * z)
                        slots = EVEN if z else ODD
                        chunk(2 * it + (1 + z + NCH * L), 1 - z, jg, jg + 2, slots,
                              (2 * OUTG * it + OUTG * (z + FOUT0[L]), slots[1]))
                jg = F0 + 3 * (NCH - 1) - 1
                chunk(NCH * L + NCH - 1, 1, jg, jg + 2, ODD, (OUTG * (FOUT0[L] + NCH - 2), ODD[1]))
                wait(pe, fV, NCH * L + NCH - 1, "lo")

            pe.wait_ge(small_in, 32)
            pe.wait_ge(init, 1)
            last_out = None
            for L in range(2):
                norms(NORM_MIX[L], mem=lambda i: mem_keys(L, i), out=last_out)
                J = MIX0[L]
                first_queries(L, J + J_MQ)
                wait(pe, mV, L, "k")
                for i in range(2):
                    for h in range(2):
                        ins = nc.tensor.transpose(ps[:, 6, 256 * i + P * h:256 * i + P * h + P],
                                                  kmem[:, h, P * i:P * i + P], ident)
                ins.then_inc(mT.sem, 1)
                wait(pe, nG, NORM_MIX[L] + NT + 1, "g1")
                J += J_MQ
                feat(J + 1, 1, 0, qT)
                wait(pe, mV, L, "rows")
                query_sums([0, 1][L])
                pair(L, False, [(J + 2, 0, hZ), (J + 3, 1, hQ)] if L == 0 else [(J + 2, 0, qT), (J + 3, 1, qT)])
                outs(OUT0[L], J + 4, [(0, 0), (1, 1)])
                pe.wait_ge(x_added, (OUT0[L] + 1) * OUTG)
                J += 6
                if L == 0:
                    for h in range(HEADS):
                        hgrn_head(h, J)
                        J += HGRN_JOBS
                    ffn(L, (OUT0[0] + HEADS, J - HGRN_JOBS + 2, [(0, (J - HGRN_JOBS + 2) % 2)]))
                else:
                    wait(pe, qA, U_KEYS, "sq1")
                    wait(pe, qV, U_KEYS, "g1")
                    key_sums(U_KEYS, 0)
                    both_cols(J, hT, [(i, rows(i)) for i in range(NT)],
                              lambda i, m: ps[0:m, i // 2, 256 * (i % 2):256 * (i % 2) + 256])
                    pe.drain().then_inc(kT.sem, 1)
                    wait(pe, kV, 0, "v")
                    wait(pe, qV, U_KEYS, "n0")
                    key_sums(U_KEYS, 1)
                    J += 2
                    feat(J, 0, 3, qT)
                    wait(pe, qA, U_KEYS, "std1")
                    feat(J + 1, 1, 0, qT)
                    wait(pe, qV, U_KEYS, "n1")
                    for h in range(2):
                        nc.tensor.transpose(ps[:, 6, P * h:P * h + P], kpad[:, h, SEQ:SEQ + P], ident)
                        ins = nc.tensor.transpose(ps[0:TS, 6, 256 + P * h:256 + P * h + P],
                                                  kpad[:, h, WIN + SEQ:WIN + T], ident)
                    ins.then_inc(kT.sem, 1)
                    query_sums(3)
                    wait(pe, kV, 0, "rows")
                    J += 2
                    for g in range(QG):
                        more = g < QG - 1
                        pair(2 + g, True, [(J, 0, qT), (J + 1, 1, qT)] if more else None)
                        J += 2 if more else 0
                        o = (OUT0[1] + 1 + g, J, [(0, 0), (1, 1)])
                        if more:
                            outs(*o, after=lambda i: query_sums(4 + g) if i == 2 else None)
                            pe.wait_ge(x_added, (OUT0[L] + 2 + g) * OUTG)
                        J += 2
                    ffn(L, o)
                last_out = (FOUT0[L] + NCH - 1, FFN0[L] + FFN_JOBS - 1, [(1, LAST_SLOT)])
            outs(*last_out)


_SHAPES = dict(
    y_prompt=(1, SEQ, D), y_sample=(NB, TQ, D), new_mem_k=(2, 1, N_MEM, 4, HD), new_mem_v=(2, 1, N_MEM, 4, HD),
    new_hg_p=(1, 1, HEADS, P, P), new_hg_s=(1, NB, HEADS, P, P), new_swk_p=(1, 1, WIN, 4, HD),
    new_swv_p=(1, 1, WIN, 4, HD), new_swk_s=(1, NB, WIN, 4, HD), new_swv_s=(1, NB, WIN, 4, HD))
_INS = ['x_prompt', 'x_sample', 'cache_mem_k', 'cache_mem_v', 'state_hgrn', 'cache_swa_k', 'cache_swa_v',
        'mem_prompt', 'w_in_hgrn', 'w_in_swa', 'w_mem_kv', 'w_out', 'w_ffn_in', 'w_ffn_out']


def _params(a):
    cols = [np.asarray(a[n]).reshape(2 * KT, P).T for n in ('norm_mix', 'norm_ffn', 'norm_mem')]
    cols += [np.asarray(a[n]).reshape(HEADS, P).T for n in ('hgrn_out_norm', 'hgrn_lb_raw')]
    cols += [np.tile(np.asarray(a[n]), (1, 2)).T for n in ('swa_q_norm', 'swa_k_norm', 'mem_q_norm', 'mem_k_norm')]
    sinks = np.asarray(a['swa_sinks']).reshape(1, 12)
    cols += [np.broadcast_to(sinks, (P, 12))]
    cols += [np.tile(np.repeat(sinks.reshape(4, QG), TQ, axis=0), (NB, 1))]
    return np.ascontiguousarray(np.concatenate(cols, axis=1))


def kernel(**inputs):
    import concourse.bacc as _bacc
    from concourse.bass_utils import run_bass_kernel_spmd as _run

    nc = _bacc.Bacc("TRN2", target_bir_lowering=False, num_devices=1,
                     dynamic_dma_scratch_size=1024)
    arrays, args = {}, []
    data = [(n, np.ascontiguousarray(inputs[n])) for n in _INS]
    data += [("constants", constants()), ("params", _params(inputs))]
    for name, a in data:
        arrays[f"in_{name}_dram"] = a
        args.append(nc.dram_tensor(f"in_{name}_dram", a.shape, mybir.dt.from_np(a.dtype), kind="ExternalInput").ap())
    for name, shape in _SHAPES.items():
        args.append(nc.dram_tensor(f"out_{name}_dram", shape, F32, kind="ExternalOutput").ap())
    hybrid_step(nc, *args)
    r = _run(nc, [arrays], core_ids=[0])
    return tuple(r.results[0][f"out_{name}_dram"] for name in _SHAPES)
```
